# Optimizing a Trainium2 kernel written in Bass

```python
import jax, jax.numpy as jnp
from jax import lax
import numpy as np

D_MODEL = 2048
BATCH = 1
SEQ = 256
DEPTH = 2
DEC_BATCH = 8
DEC_SEQ = 1
PAST_LEN = 2048
PAGE_SIZE = 128

N_AB = (DEPTH + 1) // 2
N_ML = DEPTH // 2
D_RNN = D_MODEL // 2
D_CONV = D_MODEL // 2
RNN_HEADS = 16
RNN_HEAD_DIM = D_RNN // RNN_HEADS
RNN_CONV_W = 4
LRU_C = 8.0
CONF_CONV_W = 31
ML_HEADS = 8
ML_QK = D_MODEL // 2
ML_V = D_MODEL
ML_DK = ML_QK // ML_HEADS
ML_DV = ML_V // ML_HEADS
ML_CHUNK = 128
D_FF = 4 * D_MODEL
EPS = 1e-6

kernel_name = "hawk_conformer_mlstm_hybrid_step"

def rmsnorm(x, g):
    xf = x.astype(jnp.float32)
    y = xf * lax.rsqrt(jnp.mean(xf * xf, axis=-1, keepdims=True) + EPS)
    return (y * g.astype(jnp.float32)).astype(x.dtype)

def layernorm(x, g, b):
    xf = x.astype(jnp.float32)
    mu = jnp.mean(xf, axis=-1, keepdims=True)
    var = jnp.mean(jnp.square(xf - mu), axis=-1, keepdims=True)
    y = (xf - mu) * lax.rsqrt(var + EPS)
    return (y * g.astype(jnp.float32) + b.astype(jnp.float32)).astype(x.dtype)

def causal_dwconv(x, buf, w, b):
    W, C = w.shape
    xp = jnp.concatenate([buf.astype(x.dtype), x], axis=1)
    y = lax.conv_general_dilated(xp, w.astype(x.dtype)[:, None, :], window_strides=(1,), padding='VALID',
                                 dimension_numbers=('NWC', 'WIO', 'NWC'), feature_group_count=C)
    return y + b.astype(x.dtype), xp[:, xp.shape[1] - (W - 1):]

def linear_scan(a, u, h0):
    def comb(l, r):
        return l[0] * r[0], r[0] * l[1] + r[1]
    A, Bc = lax.associative_scan(comb, (a, u), axis=1)
    h = A * h0[:, None, :] + Bc
    return h, h[:, -1]

def rglru_conformer_mixer(xn, w_in, conv_w, conv_b, wa, ba, wx, bx, lam, dw_w, dw_b, ln_g, ln_b, w_out,
                          rconv_buf, h0, cconv_buf):
    B, T, _ = xn.shape
    f32 = jnp.float32
    proj = jnp.einsum('btd,de->bte', xn, w_in)
    x_r, g_r, a_c, b_c = jnp.split(proj, [D_RNN, 2 * D_RNN, 2 * D_RNN + D_CONV], axis=-1)
    xc, new_rconv = causal_dwconv(x_r, rconv_buf, conv_w, conv_b)
    xh = xc.reshape(B, T, RNN_HEADS, RNN_HEAD_DIM)
    r = jax.nn.sigmoid(jnp.einsum('bthi,hij->bthj', xh, wa).reshape(B, T, D_RNN) + ba)
    ig = jax.nn.sigmoid(jnp.einsum('bthi,hij->bthj', xh, wx).reshape(B, T, D_RNN) + bx)
    log_a = (-LRU_C * jax.nn.softplus(-lam.astype(f32))) * r.astype(f32)
    a = jnp.exp(log_a)
    u = jnp.sqrt(-jnp.expm1(2.0 * log_a)) * (ig * xc).astype(f32)
    h, h_last = linear_scan(a, u, h0.astype(f32))
    y_r = h.astype(xn.dtype) * jax.nn.gelu(g_r)
    glu = a_c * jax.nn.sigmoid(b_c)
    yc, new_cconv = causal_dwconv(glu, cconv_buf, dw_w, dw_b)
    y_c = jax.nn.silu(layernorm(yc, ln_g, ln_b))
    y = jnp.einsum('bte,ed->btd', jnp.concatenate([y_r, y_c], axis=-1), w_out)
    return y, new_rconv, h_last, new_cconv

def mlstm_chunk_step(carry, xs):
    C, n, m = carry
    q, k, v, ig, lf = xs
    L = q.shape[2]
    b = lax.cumsum(lf, axis=2)
    causal = jnp.tril(jnp.ones((L, L), dtype=bool))
    dmat = jnp.where(causal, b[..., :, None] - b[..., None, :] + ig[..., None, :], -jnp.inf)
    inter = b + m[..., None]
    m_t = jnp.maximum(inter, jnp.max(dmat, axis=-1))
    s = jnp.einsum('bhtd,bhsd->bhts', q, k) * jnp.exp(dmat - m_t[..., None])
    scale_in = jnp.exp(inter - m_t)
    num = jnp.einsum('bhts,bhsv->bhtv', s, v) + scale_in[..., None] * jnp.einsum('bhtd,bhdv->bhtv', q, C)
    den = jnp.sum(s, axis=-1) + scale_in * jnp.einsum('bhtd,bhd->bht', q, n)
    h = num / jnp.maximum(jnp.abs(den), jnp.exp(-m_t))[..., None]
    b_last = b[..., -1]
    g = b_last[..., None] - b + ig
    m_new = jnp.maximum(b_last + m, jnp.max(g, axis=-1))
    decay = jnp.exp(b_last + m - m_new)
    wk = jnp.exp(g - m_new[..., None])
    C_new = decay[..., None, None] * C + jnp.einsum('bhs,bhsd,bhsv->bhdv', wk, k, v)
    n_new = decay[..., None] * n + jnp.einsum('bhs,bhsd->bhd', wk, k)
    return (C_new, n_new, m_new), h

def mlstm_mixer(xn, w_in, b_if, hn_g, w_out, C0, n0, m0):
    B, T, _ = xn.shape
    f32 = jnp.float32
    proj = jnp.einsum('btd,de->bte', xn, w_in)
    q, k, v, o, gif = jnp.split(proj, [ML_QK, 2 * ML_QK, 2 * ML_QK + ML_V, 2 * ML_QK + 2 * ML_V], axis=-1)

    def heads(z, dh):
        return z.reshape(B, T, ML_HEADS, dh).transpose(0, 2, 1, 3).astype(f32)

    q = heads(q, ML_DK) * (ML_DK ** -0.5)
    k = heads(k, ML_DK)
    v = heads(v, ML_DV)
    gif = (gif + b_if).astype(f32).transpose(0, 2, 1)
    ig = gif[:, :ML_HEADS]
    lf = jax.nn.log_sigmoid(gif[:, ML_HEADS:])
    L = ML_CHUNK if T % ML_CHUNK == 0 else T
    nc = T // L

    def chunks(z):
        return jnp.moveaxis(z.reshape(z.shape[:2] + (nc, L) + z.shape[3:]), 2, 0)

    (C, n, m), h = lax.scan(mlstm_chunk_step, (C0.astype(f32), n0.astype(f32), m0.astype(f32)),
                            (chunks(q), chunks(k), chunks(v), chunks(ig), chunks(lf)))
    h = jnp.moveaxis(h, 0, 2).reshape(B, ML_HEADS, T, ML_DV)
    h = h * lax.rsqrt(jnp.mean(h * h, axis=-1, keepdims=True) + EPS)
    h = h.transpose(0, 2, 1, 3).reshape(B, T, ML_V).astype(xn.dtype)
    y = (h * hn_g) * jax.nn.sigmoid(o)
    return jnp.einsum('bte,ed->btd', y, w_out), C, n, m

def sq_relu_mlp(xn, w_up, w_down):
    hdn = jnp.square(jax.nn.relu(jnp.einsum('btd,df->btf', xn, w_up)))
    return jnp.einsum('btf,fd->btd', hdn, w_down)

def run_trunk(x, rconv, rh, cconv, mC, mn, mm, P):
    o_rconv, o_rh, o_cconv, o_C, o_n, o_m = [], [], [], [], [], []
    for l in range(DEPTH):
        i = l // 2
        if l % 2 == 0:
            y, s1, s2, s3 = rglru_conformer_mixer(
                rmsnorm(x, P['ab_norm'][i]), P['ab_w_in'][i], P['rglru_conv_w'][i], P['rglru_conv_b'][i],
                P['rglru_wa'][i], P['rglru_ba'][i], P['rglru_wx'][i], P['rglru_bx'][i], P['rglru_lambda'][i],
                P['conf_dw_w'][i], P['conf_dw_b'][i], P['conf_ln_g'][i], P['conf_ln_b'][i], P['ab_w_out'][i],
                rconv[i], rh[i], cconv[i])
            o_rconv.append(s1); o_rh.append(s2); o_cconv.append(s3)
        else:
            y, C, n, m = mlstm_mixer(rmsnorm(x, P['ml_norm'][i]), P['ml_w_in'][i], P['ml_b_if'][i],
                                     P['ml_hnorm_g'][i], P['ml_w_out'][i], mC[i], mn[i], mm[i])
            o_C.append(C); o_n.append(n); o_m.append(m)
        x = x + y
        x = x + sq_relu_mlp(rmsnorm(x, P['mlp_norm'][l]), P['mlp_w_up'][l], P['mlp_w_down'][l])
    y_out = rmsnorm(x, P['final_norm'])
    return (y_out, jnp.stack(o_rconv), jnp.stack(o_rh), jnp.stack(o_cconv),
            jnp.stack(o_C), jnp.stack(o_n), jnp.stack(o_m))

def setup_inputs(seed: int = 0) -> dict:
    key = jax.random.key(seed)
    ks = jax.random.split(key, 40)
    f32 = jnp.float32
    nrm = lambda k, s, sc: jax.random.normal(k, s, f32) * sc
    u = jax.random.uniform(ks[0], (N_AB, D_RNN), f32, 0.9, 0.999)
    a0 = u ** (1.0 / LRU_C)
    lam = jnp.log(a0) - jnp.log1p(-a0)
    b_if = jnp.concatenate([nrm(ks[1], (N_ML, ML_HEADS), 0.1),
                            3.0 + nrm(ks[2], (N_ML, ML_HEADS), 0.5)], axis=-1)
    ml_in = 2 * ML_QK + 2 * ML_V + 2 * ML_HEADS
    return {
        'x_prompt': nrm(ks[3], (BATCH, SEQ, D_MODEL), 1.0),
        'x_sample': nrm(ks[4], (DEC_BATCH, DEC_SEQ, D_MODEL), 1.0),
        'state_rglru_conv': nrm(ks[5], (N_AB, DEC_BATCH, RNN_CONV_W - 1, D_RNN), 1.0),
        'state_rglru_h': nrm(ks[6], (N_AB, DEC_BATCH, D_RNN), 0.5),
        'state_conf_conv': nrm(ks[7], (N_AB, DEC_BATCH, CONF_CONV_W - 1, D_CONV), 0.5),
        'state_mlstm_C': nrm(ks[8], (N_ML, DEC_BATCH, ML_HEADS, ML_DK, ML_DV), 0.3),
        'state_mlstm_n': nrm(ks[9], (N_ML, DEC_BATCH, ML_HEADS, ML_DK), 0.3),
        'state_mlstm_m': nrm(ks[10], (N_ML, DEC_BATCH, ML_HEADS), 1.0),
        'ab_norm': 1.0 + nrm(ks[11], (N_AB, D_MODEL), 0.05),
        'ab_w_in': nrm(ks[12], (N_AB, D_MODEL, 2 * D_RNN + 2 * D_CONV), D_MODEL ** -0.5),
        'rglru_conv_w': nrm(ks[13], (N_AB, RNN_CONV_W, D_RNN), RNN_CONV_W ** -0.5),
        'rglru_conv_b': nrm(ks[14], (N_AB, D_RNN), 0.01),
        'rglru_wa': nrm(ks[15], (N_AB, RNN_HEADS, RNN_HEAD_DIM, RNN_HEAD_DIM), RNN_HEAD_DIM ** -0.5),
        'rglru_ba': nrm(ks[16], (N_AB, D_RNN), 0.01),
        'rglru_wx': nrm(ks[17], (N_AB, RNN_HEADS, RNN_HEAD_DIM, RNN_HEAD_DIM), RNN_HEAD_DIM ** -0.5),
        'rglru_bx': nrm(ks[18], (N_AB, D_RNN), 0.01),
        'rglru_lambda': lam,
        'conf_dw_w': nrm(ks[19], (N_AB, CONF_CONV_W, D_CONV), CONF_CONV_W ** -0.5),
        'conf_dw_b': nrm(ks[20], (N_AB, D_CONV), 0.01),
        'conf_ln_g': 1.0 + nrm(ks[21], (N_AB, D_CONV), 0.05),
        'conf_ln_b': nrm(ks[22], (N_AB, D_CONV), 0.01),
        'ab_w_out': nrm(ks[23], (N_AB, D_RNN + D_CONV, D_MODEL), (D_RNN + D_CONV) ** -0.5),
        'ml_norm': 1.0 + nrm(ks[24], (N_ML, D_MODEL), 0.05),
        'ml_w_in': nrm(ks[25], (N_ML, D_MODEL, ml_in), D_MODEL ** -0.5),
        'ml_b_if': b_if,
        'ml_hnorm_g': 1.0 + nrm(ks[26], (N_ML, ML_V), 0.05),
        'ml_w_out': nrm(ks[27], (N_ML, ML_V, D_MODEL), ML_V ** -0.5),
        'mlp_norm': 1.0 + nrm(ks[28], (DEPTH, D_MODEL), 0.05),
        'mlp_w_up': nrm(ks[29], (DEPTH, D_MODEL, D_FF), D_MODEL ** -0.5),
        'mlp_w_down': nrm(ks[30], (DEPTH, D_FF, D_MODEL), D_FF ** -0.5),
        'final_norm': 1.0 + nrm(ks[31], (D_MODEL,), 0.05),
    }

def reference(x_prompt, x_sample, state_rglru_conv, state_rglru_h, state_conf_conv, state_mlstm_C,
              state_mlstm_n, state_mlstm_m, ab_norm, ab_w_in, rglru_conv_w, rglru_conv_b, rglru_wa,
              rglru_ba, rglru_wx, rglru_bx, rglru_lambda, conf_dw_w, conf_dw_b, conf_ln_g, conf_ln_b,
              ab_w_out, ml_norm, ml_w_in, ml_b_if, ml_hnorm_g, ml_w_out, mlp_norm, mlp_w_up, mlp_w_down,
              final_norm):
    P = {'ab_norm': ab_norm, 'ab_w_in': ab_w_in, 'rglru_conv_w': rglru_conv_w, 'rglru_conv_b': rglru_conv_b,
         'rglru_wa': rglru_wa, 'rglru_ba': rglru_ba, 'rglru_wx': rglru_wx, 'rglru_bx': rglru_bx,
         'rglru_lambda': rglru_lambda, 'conf_dw_w': conf_dw_w, 'conf_dw_b': conf_dw_b,
         'conf_ln_g': conf_ln_g, 'conf_ln_b': conf_ln_b, 'ab_w_out': ab_w_out, 'ml_norm': ml_norm,
         'ml_w_in': ml_w_in, 'ml_b_if': ml_b_if, 'ml_hnorm_g': ml_hnorm_g, 'ml_w_out': ml_w_out,
         'mlp_norm': mlp_norm, 'mlp_w_up': mlp_w_up, 'mlp_w_down': mlp_w_down, 'final_norm': final_norm}
    f32 = jnp.float32
    Bp = x_prompt.shape[0]
    z_rconv = jnp.zeros((N_AB, Bp, RNN_CONV_W - 1, D_RNN), x_prompt.dtype)
    z_rh = jnp.zeros((N_AB, Bp, D_RNN), f32)
    z_cconv = jnp.zeros((N_AB, Bp, CONF_CONV_W - 1, D_CONV), x_prompt.dtype)
    z_C = jnp.zeros((N_ML, Bp, ML_HEADS, ML_DK, ML_DV), f32)
    z_n = jnp.zeros((N_ML, Bp, ML_HEADS, ML_DK), f32)
    z_m = jnp.zeros((N_ML, Bp, ML_HEADS), f32)
    y_prompt, p_rconv, p_rh, p_cconv, p_C, p_n, p_m = run_trunk(x_prompt, z_rconv, z_rh, z_cconv, z_C, z_n, z_m, P)
    y_sample, s_rconv, s_rh, s_cconv, s_C, s_n, s_m = run_trunk(
        x_sample, state_rglru_conv, state_rglru_h, state_conf_conv, state_mlstm_C, state_mlstm_n,
        state_mlstm_m, P)
    return (y_prompt, y_sample, p_rconv, p_rh, p_cconv, p_C, p_n, p_m,
            s_rconv, s_rh, s_cconv, s_C, s_n, s_m)


_drawn_inputs = setup_inputs


def setup_inputs(seed=0):
    import zlib

    import numpy as np

    out = dict(_drawn_inputs(seed))
    spreads = {}
    factors = {'rglru_ba': 28.159,
     'rglru_bx': 8.0,
     'conf_dw_b': 4.044,
     'conf_ln_b': 6.171,
     'ml_hnorm_g': 3.565}
    for name, (base, spread) in spreads.items():
        noise = np.random.default_rng([zlib.crc32(name.encode()), seed]).standard_normal(out[name].shape)
        drawn = base * np.exp(spread * noise) if base else spread * noise
        out[name] = __import__('jax').numpy.asarray(drawn.astype(out[name].dtype))
    for name, factor in factors.items():
        out[name] = (out[name] * factor).astype(out[name].dtype)
    return out
```

```python
from contextlib import ExitStack

import concourse.bass as bass
from concourse import mybir

F32 = mybir.dt.float32
F32R = mybir.dt.float32r
ACT = mybir.ActivationFunctionType
ALU = mybir.AluOpType
AX = mybir.AxisListType

P = 128
D = 2048
KT = D // P
TP, NS = 256, 8
T = TP + NS
DR = D // 2
FF = 4 * D
NH, DK, DV = 8, 128, 256
W4, W31 = 4, 31
C = 128
ESW = T + C + 2 * NS
EPS = 1e-6
BLK = 1024
RAW, SPLIT = 8, 4
HI_AHEAD, LO_AHEAD = 3, 2

ABN, MLN, MPN, FIN, HNG, CB, BA, BX, LAM = 0, 16, 32, 64, 80, 96, 104, 112, 120
DWB, LNG, LNB, H0, CW = 128, 136, 144, 152, 216
NPAR = 248


class Phase:

    def __init__(self, before, iters, steps, groups, lo="D"):
        self.iters, self.steps, self.groups = iters, steps, groups
        self.lo = (lo * steps)[:steps]
        self.n0 = before.n0 + before.iters * before.steps if before else 0
        self.g0 = before.g0 + before.iters * before.groups if before else 0
        self.d0 = before.d0 + before.iters * before.lo.count("D") if before else 0
        self.p0 = before.p0 + before.iters * before.lo.count("P") if before else 0
        assert self.lo[:LO_AHEAD] == "D" * LO_AHEAD or lo == "D"
        assert iters == 1 or (steps % RAW == 0 and groups % 2 == 0)

    def n(self, it, c):
        return self.n0 + c + it * self.steps

    def g(self, it, j):
        return self.g0 + j + it * self.groups


DEPTH = 2


def phases():
    ph = {}
    def add(name, *a, **k):
        ph[name] = Phase(list(ph.values())[-1] if ph else None, *a, **k)
    add("in0", 4, 16, 4, lo="DDPPDPPPDPPPDPPP")
    add("out0a", 2, 8, 4, lo="DDPPDPPP")
    add("out0b", 2, 8, 4)
    for l in range(DEPTH):
        for h in (0, 1):
            add(f"up{l}{h}", 8, 8, 2)
            add(f"down{l}{h}", 4, 16, 2)
        if l == 0:
            add("gif", 1, 2, 1)
            add("in1", 4, 24, 6, lo="DDPDDDPDDDPDDDPDDDPDDDPD")
            add("out1a", 1, 24, 8)
            add("out1b", 1, 8, 8)
    return ph


PH = phases()
LAST = PH[f"down{DEPTH - 1}1"]
NB = LAST.n(LAST.iters, 0)


def program(nc, I, O):
    ctx = ExitStack()
    with ctx:
        def sem(name):
            return ctx.enter_context(nc.semaphore(name))

        def sb(stack, name, shape, dt=F32):
            return stack.enter_context(nc.sbuf_tensor(name, shape, dt))

        X = sb(ctx, "X", [P, KT, T])
        A_hi = sb(ctx, "A_hi", [P, KT, T], F32R)
        A_lo = sb(ctx, "A_lo", [P, KT, T], F32R)
        raw = sb(ctx, "raw", [P, RAW, BLK])
        w_hi = sb(ctx, "w_hi", [P, SPLIT, BLK], F32R)
        w_lo = sb(ctx, "w_lo", [P, SPLIT, BLK], F32R)
        ident = sb(ctx, "ident", [P, P])
        ones = sb(ctx, "ones", [P, P])
        par = sb(ctx, "par", [P, NPAR])
        SQ = sb(ctx, "SQ", [P, 2, T])
        ssq = sb(ctx, "ssq", [P, 2, T])
        RMS = sb(ctx, "RMS", [P, T])
        RS = sb(ctx, "RS", [P, T])
        eps = sb(ctx, "eps", [P, 1])
        tiny = sb(ctx, "tiny", [P, 1])
        PS = ctx.enter_context(nc.psum_tensor("PS", [P, 8, 512], F32))

        mixers = ExitStack()
        B_hi = sb(mixers, "B_hi0", [P, KT, T], F32R)
        B_lo = sb(mixers, "B_lo0", [P, KT, T], F32R)
        m0 = ExitStack()
        GLs = sb(m0, "GLs", [P, 8, NS, W31])
        XRs = sb(m0, "XRs", [P, 8, NS, W4])
        w31 = sb(m0, "w31", [P, 8, W31])
        YC = sb(m0, "YC", [P, 8, T])
        HS = sb(m0, "HS", [P, 72])
        GLp = sb(m0, "GLp", [P, 2, W31 - 1 + TP])
        XRp = sb(m0, "XRp", [P, 2, W4 - 1 + TP])
        hBA = sb(m0, "hBA", [P, 8])
        hBX = sb(m0, "hBX", [P, 8])
        hla = sb(m0, "hla", [P, 8])
        nhla = sb(m0, "nhla", [P, 8])
        hLNG = sb(m0, "hLNG", [P, 8])
        hLNB = sb(m0, "hLNB", [P, 8])
        spt = sb(m0, "spt", [P, 6, 8])
        GW = sb(m0, "GW", [P, 4, P])
        TS = sb(m0, "TS", [P, 2, 49])
        tmp0 = ExitStack()
        XC = sb(tmp0, "XC", [P, 2, T])
        XP = sb(tmp0, "XP", [P, 2, NS, W4])
        G = sb(tmp0, "G", [P, 2, T])
        G2 = sb(tmp0, "G2", [P, 2, T])
        G3 = sb(tmp0, "G3", [P, 2, T])
        RG = sb(tmp0, "RG", [P, 2, T])
        IG = sb(tmp0, "IG", [P, 2, T])
        AA = sb(tmp0, "AA", [P, 2, T])
        TL = sb(tmp0, "TL", [P, 2, T])
        TB = sb(tmp0, "TB", [P, 2, T])
        GP = sb(tmp0, "GP", [P, 2, NS, W31])
        OH = sb(tmp0, "OH", [72, P])
        OT = sb(tmp0, "OT", [49, 2, P])
        tmp0.close()
        turn = ExitStack()
        crow = sb(turn, "crow", [120, 2, DR])
        drow = sb(turn, "drow", [W31, DR])
        rrow = sb(turn, "rrow", [24, DR])
        turn.close()
        m0.close()
        m1 = ExitStack()
        E = sb(m1, "E", [P, NH, 2, C])
        ES = sb(m1, "ES", [P, NH, ESW])
        AT = sb(m1, "AT", [P, 32])
        WKsT = sb(m1, "WKsT", [NS, NH])
        NSt = sb(m1, "NSt", [P, 64])
        NO = sb(m1, "NO", [P, 72])
        HG = sb(m1, "HG", [P, KT])
        MO = sb(m1, "MO", [NH, 9])
        mprev = sb(m1, "mprev", [NH, NS])
        bIF = sb(m1, "bIF", [2 * NH, 1])
        mw = sb(m1, "mw", [NS, NS])
        nsa = sb(m1, "nsa", [P, NS])
        nq = sb(m1, "nq", [P, NS])
        QA = sb(m1, "QA", [P, 2, T])
        KA = sb(m1, "KA", [P, 2, T])
        Qb = sb(m1, "Qb", [P, T])
        Kb = sb(m1, "Kb", [P, T])
        heads = ExitStack()
        VV = sb(heads, "VV", [P, 2, T])
        OG = [sb(heads, f"OG{i}", [P, 2, T]) for i in range(2)]
        KTt = sb(heads, "KTt", [P, 2, C])
        VT = sb(heads, "VT", [P, 2, DV])
        SP = sb(heads, "SP", [P, 2, C])
        C1 = sb(heads, "C1", [P, DV + 1])
        n1r = sb(heads, "n1r", [P, P])
        Qsc = sb(heads, "Qsc", [P, C])
        kM = sb(heads, "kM", [NS, 2, DK])
        kS = sb(heads, "kS", [NS, DK])
        vS = sb(heads, "vS", [NS, DV])
        Hh = sb(heads, "Hh", [P, 2, T])
        Cs = sb(heads, "Cs", [P, NS, DV])
        heads.close()
        gate = ExitStack()
        rows = sb(gate, "rows", [NH, 13, T])
        IF = sb(gate, "IF", [2 * NH, T])
        SEL = sb(gate, "SEL", [NH, NH, P])
        MASK = sb(gate, "MASK", [P, 2, C])
        m1s = sb(gate, "m1s", [NH, 4])
        nrow = sb(gate, "nrow", [64, P])
        gate.close()
        tail1 = ExitStack()
        OH1 = sb(tail1, "OH1", [72, P])
        tail1.close()
        m1.close()
        mixers.close()
        start = ExitStack()
        xt = sb(start, "xt", [P, 2, D])
        xs = sb(start, "xs", [NS, D])
        prow = sb(start, "prow", [P, 2, P])
        start.close()
        mlp = ExitStack()
        H_hi = sb(mlp, "H_hi", [P, 32, T], F32R)
        H_lo = sb(mlp, "H_lo", [P, 32, T], F32R)
        UT = sb(mlp, "UT", [P, 2, T])
        U = sb(mlp, "U", [P, 2, T])
        mlp.close()
        final = ExitStack()
        YO = sb(final, "YO", [P, 2, D])
        YS = sb(final, "YS", [NS, D])
        final.close()

        raw_ready = [sem(f"raw_ready{i}") for i in range(RAW)]
        hi_done, lo_dve, lo_pool = sem("hi_done"), sem("lo_dve"), sem("lo_pool")
        pe_block, evac_done = sem("pe_block"), sem("evac_done")
        params_in, x_in, states_in = sem("params_in"), sem("x_in"), sem("states_in")
        consts, zeroed = sem("consts"), sem("zeroed")
        CONSTS = 7
        OUTS = 20
        par_turned, par_ready = sem("par_turned"), sem("par_ready")
        x_turned, x_loaded = sem("x_turned"), sem("x_loaded")
        sq_ready, ssq_added, ssq_ready = sem("sq_ready"), sem("ssq_added"), sem("ssq_ready")
        ssq_zeroed = sem("ssq_zeroed")
        rms_ready, rs_ready = sem("rms_ready"), sem("rs_ready")
        ah_ready, a_ready = sem("ah_ready"), sem("a_ready")
        small = sem("small")
        absl, expl = sem("absl"), sem("expl")
        states_turned, states_ready = sem("states_turned"), sem("states_ready")
        u_ready, hh_ready, h_ready = sem("u_ready"), sem("hh_ready"), sem("h_ready")
        out_done = sem("out_done")

        def two(bank):
            return PS[:, bank:bank + 2, 0:T]

        def over2(ap, n=2):
            return ap[:, None, :].broadcast_to([P, n, ap.shape[1]])

        def load(sp, ph, it, c, w, row, col):
            n, slot = ph.n(it, c), (ph.n0 + c) % RAW
            if not isinstance(n, int) or n >= RAW:
                sp.wait_ge(pe_block, n - RAW + 1)
            src = w[row:row + 4 * P, :].rearrange("(k p) e -> p k e", p=P)[:, :, bass.ds(col, 256)]
            sp.dma_start(raw[:, slot, :].rearrange("p (k e) -> p k e", k=4), src)\
              .then_inc(raw_ready[slot], 16)

        def split_hi(act, ph, it, c):
            n, m = ph.n(it, c) + HI_AHEAD, ph.n0 + c + HI_AHEAD
            if isinstance(n, int) and n >= NB:
                return
            act.wait_ge(raw_ready[m % RAW], 16 * (m // RAW + 1) + it * (16 * (ph.steps // RAW)))
            if not isinstance(n, int) or n >= SPLIT:
                act.wait_ge(pe_block, n - SPLIT + 1)
            nc.scalar.activation(w_hi[:, m % SPLIT, :], raw[:, m % RAW, :], ACT.Copy)\
              .then_inc(hi_done, 1)

        def split_lo(eng, who, ph, it, c):
            t = c + LO_AHEAD
            if (ph.lo[t] if t < ph.steps else "D") != who:
                return
            n, m = ph.n(it, c) + LO_AHEAD, ph.n0 + t
            if isinstance(n, int) and n >= NB:
                return
            eng.wait_ge(hi_done, n + 1)
            if not isinstance(n, int) or n >= SPLIT:
                eng.wait_ge(pe_block, n - SPLIT + 1)
            eng.tensor_tensor(w_lo[:, m % SPLIT, :], raw[:, m % RAW, :],
                              w_hi[:, m % SPLIT, :].bitcast(F32), ALU.subtract)\
               .then_inc(lo_dve if who == "D" else lo_pool, 1)

        def wait_split(pe, ph, it, c):
            who = ph.lo[c]
            done = ph.lo[:c + 1].count(who) + (ph.d0 if who == "D" else ph.p0)
            pe.wait_ge(lo_dve if who == "D" else lo_pool, done + it * ph.lo.count(who))

        def multiply(pe, ph, it, c, group, hi, lo, k0, first, last):
            wait_split(pe, ph, it, c)
            slot, bank = (ph.n0 + c) % SPLIT, 2 * ((ph.g0 + group) % 2)
            if first and not (isinstance(ph.g(it, group), int) and ph.g(it, group) < 2):
                pe.wait_ge(evac_done, ph.g(it, group) - 1)
            for k in range(4):
                for m in range(2):
                    w = slice(256 * k + P * m, 256 * k + P * m + P)
                    out = PS[:, bank + m, 0:T]
                    nc.tensor.matmul(out, w_hi[:, slot, w], hi[:, k0 + k, :], start=first and k == 0, stop=False)
                    nc.tensor.matmul(out, w_hi[:, slot, w], lo[:, k0 + k, :], start=False, stop=False)
                    mm = nc.tensor.matmul(out, w_lo[:, slot, w], hi[:, k0 + k, :], start=False,
                                          stop=last and k == 3)
            mm.then_inc(pe_block, 1)

        def group_bank(ph, j):
            return 2 * ((ph.g0 + j) % 2)

        def square_and_gain(act, e, p, gain):
            idx = p + 8 * e
            if not (isinstance(idx, int) and idx == 0):
                act.wait_ge(ssq_added, idx)
            nc.scalar.activation(SQ[:, :, :], X[:, bass.ds(2 * p, 2), :], ACT.Square).then_inc(sq_ready, 1)
            if gain is not None:
                for m in range(2):
                    q = nc.scalar.activation(A_hi[:, bass.ds(2 * p + m, 1), :], X[:, bass.ds(2 * p + m, 1), :],
                                             ACT.Copy, scale=par[:, bass.ds(2 * p + (gain + m), 1)])
                q.then_inc(ah_ready, 1)

        def gain_lo(dve, e, p, gain):
            dve.wait_ge(ah_ready, p + (8 * e + 1))
            for m in range(2):
                k = bass.ds(2 * p + m, 1)
                q = nc.vector.scalar_tensor_tensor(A_lo[:, k, :], X[:, k, :], par[:, bass.ds(2 * p + (gain + m), 1)],
                                                   A_hi[:, k, :].bitcast(F32), ALU.mult, ALU.subtract)
            q.then_inc(a_ready, 1)

        def add_squares(pool, e, p):
            pool.wait_ge(sq_ready, p + (8 * e + 1))
            pool.wait_ge(ssq_zeroed, e + 1)
            if not isinstance(p, int) or 8 * e + p > 0:
                pool.wait_ge(ssq_added, p + 8 * e)
            nc.gpsimd.tensor_tensor(ssq[:, :, :], ssq[:, :, :], SQ[:, :, :], ALU.add).then_inc(ssq_added, 1)

        def zero_squares(pool, e):
            if e:
                pool.wait_ge(ssq_ready, e)
            nc.gpsimd.memset(ssq[:, :, :], 0.0).then_inc(ssq_zeroed, 1)

        def sum_squares(pe, e):
            pe.wait_ge(ssq_added, 8 * (e + 1))
            nc.tensor.matmul(PS[:, 7, 0:T], ones[:, :], ssq[:, 0, :], start=True, stop=False)
            nc.tensor.matmul(PS[:, 7, 0:T], ones[:, :], ssq[:, 1, :], start=False, stop=True).then_inc(ssq_ready, 1)

        def root(act, e):
            act.wait_ge(ssq_ready, e + 1)
            if e:
                act.wait_ge(rs_ready, e)
            nc.scalar.activation(RMS[:, :], PS[:, 7, 0:T], ACT.Sqrt, scale=1.0 / D, bias=eps[:, :])\
              .then_inc(rms_ready, 1)

        def invert(dve, e):
            dve.wait_ge(rms_ready, e + 1)
            nc.vector.reciprocal(RS[:, :], RMS[:, :]).then_inc(rs_ready, 1)
            dve.wait_ge(rs_ready, e + 1)

        def turns(eng, ph, body, peel=0, tail=0):
            for it in range(peel):
                body(it)
            if ph.iters > peel + tail:
                with eng.Fori(peel, ph.iters - tail) as it:
                    body(it)
            for it in range(ph.iters - tail, ph.iters):
                body(it)

        xc_tap, xs_step, xc_ready = sem("xc_tap"), sem("xs_step"), sem("xc_ready")
        gw_in, gates_ready, gates_read, al_ready = sem("gw_in"), sem("gates_ready"), sem("gates_read"), sem("al_ready")
        w_step, w_ready, t_ready, root_ready = sem("w_step"), sem("w_ready"), sem("t_ready"), sem("root_ready")
        u0_ready, h0_step, h0_ready = sem("u0_ready"), sem("h0_step"), sem("h0_ready")
        g2_ready, g3_step, g3_ready, gth_ready = sem("g2_ready"), sem("g3_step"), sem("g3_ready"), sem("gth_ready")
        gl_step, y_ready, bh_ready, b_ready = sem("gl_step"), sem("y_ready"), sem("bh_ready"), sem("b_ready")
        tb_ready, gl_ready, tap_done = sem("tb_ready"), sem("gl_ready"), sem("tap_done")
        cs_step, yc_ready = sem("cs_step"), sem("yc_ready")
        tsx_ready, tsg_ready, hs_ready = sem("tsx_ready"), sem("tsg_ready"), sem("hs_ready")
        ts_turned, ot_ready, ot_out = sem("ts_turned"), sem("ot_ready"), sem("ot_out")
        hs_turned, oh_ready = sem("hs_turned"), sem("oh_ready")
        ln_zeroed, ln_added, mu_ready, mu_copied = sem("ln_zeroed"), sem("ln_added"), sem("mu_ready"), sem("mu_copied")
        yd_ready, lsq_ready, var_ready, dev_ready = sem("yd_ready"), sem("lsq_ready"), sem("var_ready"), sem("dev_ready")
        rv_ready, yn_ready, lth_ready = sem("rv_ready"), sem("yn_ready"), sem("lth_ready")
        z_step, z_ready = sem("z_step"), sem("z_ready")
        fin_ready, fin_turned, fin_copied = sem("fin_ready"), sem("fin_turned"), sem("fin_copied")
        fin_samples, lam_ready = sem("fin_samples"), sem("lam_ready")

        in0, out0a, out0b = PH["in0"], PH["out0a"], PH["out0b"]
        w31f = w31[:, :, :].rearrange("p j w -> p (j w)")
        H0v = par[:, H0:H0 + 64].rearrange("p (b j) -> p j b", j=8)
        CWv = par[:, CW:CW + 32].rearrange("p (w j) -> p j w", j=8)
        HSv = HS[:, 0:64].rearrange("p (b j) -> p j b", j=8)
        IN0_COLS = [0, DR, 3 * DR, 2 * DR]
        Zb, Tb = [XC, AA, TL, RG], [G2, G3, TB, IG]


        gate_in, gate_i, gate_s = sem("gate_in"), sem("gate_i"), sem("gate_s")
        gate_f, gate_e, gate_m, gate_x, gate_y = sem("gate_f"), sem("gate_e"), sem("gate_m"), sem("gate_x"), sem("gate_y")
        masks, at_turned, at_ready = sem("masks"), sem("at_turned"), sem("at_ready")
        bc_made, bc_copied, e_ready = sem("bc_made"), sem("bc_copied"), sem("e_ready")
        qb_copied, og_ready, hp_turned, kt_ready = sem("qb_copied"), sem("og_ready"), sem("hp_turned"), sem("kt_ready")
        sp_ready, c1_made, c1_copied, qsc_ready = sem("sp_ready"), sem("c1_made"), sem("c1_copied"), sem("qsc_ready")
        c2_made, c2_ready, nn_ready, pc_out = sem("c2_made"), sem("c2_ready"), sem("nn_ready"), sem("pc_out")
        ns_step, nq_ready = sem("ns_step"), sem("nq_ready")
        km_ready, outer_made, cs_upd = sem("km_ready"), sem("outer_made"), sem("cs_upd")
        cs_in, cs_out = [sem(f"cs_in{i}") for i in range(2)], [sem(f"cs_out{i}") for i in range(2)]
        nums_made, rd_step, hn_ready, sqh_ready = sem("nums_made"), sem("rd_step"), sem("hn_ready"), sem("sqh_ready")
        hss_made, rm_ready, rn_ready, ogs_ready = sem("hss_made"), sem("rm_ready"), sem("rn_ready"), sem("ogs_ready")
        yy_ready, bh1_ready, b1_ready = sem("yy_ready"), sem("bh1_ready"), sem("b1_ready")
        no_turned, oh1_ready = sem("no_turned"), sem("oh1_ready")

        gif, in1, out1a, out1b = (PH.get(n) for n in ("gif", "in1", "out1a", "out1b"))
        VQ, VK, VV0, VO, VG = 0, NH * DK, 2 * NH * DK, 2 * NH * DK + NH * DV, 2 * NH * DK + 2 * NH * DV
        IN1_COLS = [(VQ, 2 * DK), (VK, 2 * DK), (VV0, 2 * DV), (VV0 + DV, 2 * DV), (VO, 2 * DV), (VO + DV, 2 * DV)]
        GF, GE, GZ, GY, GL, GB, GA, GM, GW1, GEM, GSC, GNM, GT = range(13)
        ESf = ES[:, :, :].rearrange("p h f -> p (h f)")
        Ef = E[:, :, :, :].rearrange("p h c t -> p (h c t)")
        SPf = SP[:, :, :].rearrange("p c t -> p (c t)")
        NOv = NO[:, 0:64].rearrange("p (b h) -> p b h", b=NS)
        NStv = NSt[:, :].rearrange("p (b h) -> p b h", b=NS)
        id8 = ident[0:NS, 0:NS]

        def after(eng, s, value):
            if not (isinstance(value, int) and value <= 0):
                eng.wait_ge(s, value)

        def decays(k, first, n):
            return ESf[:, bass.ds(k * ESW + (T + first), n)]

        def head_steps(body, it, c):
            if c >= 12:
                body(c - 12, 2 * it, QA[:, 0, :], KA[:, 0, :], OG[0])
            elif not (isinstance(it, int) and it == 0):
                body(c, 2 * it - 1, Qb, Kb, OG[1])

        def load_mixer1(sp):
            w_in, w_out = I["ml_w_in"][0], I["ml_w_out"][0]
            for c in range(2):
                n, slot = gif.n(0, c), (gif.n0 + c) % RAW
                sp.wait_ge(pe_block, n - RAW + 1)
                src = w_in[1024 * c:1024 * c + 1024, VG:VG + 2 * NH].rearrange("(k p) e -> p k e", p=P)
                sp.dma_start(raw[:, slot, :].rearrange("p (k e) -> p k e", k=8)[:, :, 0:2 * NH], src)\
                  .then_inc(raw_ready[slot], 16)
            def load_in1(it):
                for c in range(24):
                    base, step = IN1_COLS[c // 4]
                    load(sp, in1, it, c, w_in, 512 * (c % 4), step * it + base)
            turns(sp, in1, load_in1)
            for c in range(24):
                load(sp, out1a, 0, c, w_out, 512 * (c % 3), 256 * (c // 3))
            for c in range(8):
                load(sp, out1b, 0, c, w_out, 1536, 256 * c)

        def pe_mixer1(pe):
            for c in range(2):
                pe.wait_ge(a_ready, 16 + 4 * (c + 1))
                wait_split(pe, gif, 0, c)
                slot, bank = (gif.n0 + c) % SPLIT, group_bank(gif, 0)
                if c == 0:
                    pe.wait_ge(evac_done, gif.g(0, 0) - 1)
                out = PS[0:2 * NH, bank, 0:T]
                for k in range(8):
                    w = slice(P * k, P * k + 2 * NH)
                    x = 8 * c + k
                    nc.tensor.matmul(out, w_hi[:, slot, w], A_hi[:, x, :], start=x == 0, stop=False)
                    nc.tensor.matmul(out, w_hi[:, slot, w], A_lo[:, x, :], start=False, stop=False)
                    mm = nc.tensor.matmul(out, w_lo[:, slot, w], A_hi[:, x, :], start=False, stop=x == 15)
                mm.then_inc(pe_block, 1)
            sum_squares(pe, 2)

            def gates(c):
                if c == 0:
                    pe.wait_ge(gate_i, 1)
                    nc.tensor.matmul(PS[0:NH, 5, 0:T], ident[0:2 * NH, NH:2 * NH], IF[:, :], start=True, stop=True).then_inc(gate_s, 1)
                if c == 6:
                    pe.wait_ge(gate_x, 3)
                    for i in range(2):
                        nc.tensor.transpose(PS[:, 4, 8 * i:8 * i + 8], rows[:, GA, C * i:C * i + C], id8)
                        nc.tensor.transpose(PS[:, 4, 16 + 8 * i:24 + 8 * i], rows[:, GW1, C * i:C * i + C], id8)
                    nc.tensor.transpose(PS[0:NS, 4, 32:40], rows[:, GSC, 136:144], id8)
                    nc.tensor.transpose(PS[:, 4, 64:128], nrow[:, :], ident[0:64, 0:64]).then_inc(at_turned, 1)
                if 7 <= c <= 10:
                    pe.wait_ge(masks, 3)
                    if c == 7:
                        pe.wait_ge(rms_ready, 3)
                        pe.wait_ge(at_ready, 1)
                    else:
                        pe.wait_ge(bc_copied, c - 7)
                        pe.wait_ge(e_ready, c - 7)
                    for x in range(2):
                        h = 2 * (c - 7) + x
                        nc.tensor.matmul(PS[:, 4 + x, 0:ESW], SEL[:, h, :],
                                         rows[:, GEM:GSC + 1, :].rearrange("p r t -> p (r t)")[:, 0:ESW], start=True, stop=True)
                        nc.tensor.matmul(PS[:, 6 + x, 0:2 * C], SEL[:, h, :], rows[:, GNM, 0:2 * C], start=True, stop=False)
                        mm = nc.tensor.matmul(PS[:, 6 + x, 0:2 * C], ident[:, :], MASK[:, :, :].rearrange("p c t -> p (c t)"),
                                              start=False, stop=True)
                    mm.then_inc(bc_made, 1)

            def head(t, k, Q, K, og):
                if t == 0:
                    if isinstance(k, int) and k == 0:
                        pe.wait_ge(bc_copied, 4)
                        pe.wait_ge(e_ready, 4)
                        pe.wait_ge(evac_done, in1.g(0, 2) + 1)
                    else:
                        pe.wait_ge(cs_upd, k * 4)
                        pe.wait_ge(rm_ready, k)
                        pe.wait_ge(hn_ready, k)
                        pe.wait_ge(evac_done, in1.g0 + 3 + 3 * k)
                    for i in range(2):
                        s = slice(C * i, C * i + C)
                        nc.tensor.transpose(PS[:, 4, s], K[:, s], ident[:, :])
                        for m in range(2):
                            nc.tensor.transpose(PS[:, 7, DV * i + P * m:DV * i + P * m + P], VV[:, m, s], ident[:, :])
                        nc.tensor.matmul(PS[:, 6, s], K[:, s], Q[:, s], start=True, stop=True)
                    nc.tensor.transpose(PS[0:NS, 5, 0:DK], K[:, TP:T], ident[:, :])
                    for m in range(2):
                        tr = nc.tensor.transpose(PS[0:NS, 5, P + P * m:2 * P + P * m], VV[:, m, TP:T], ident[:, :])
                    tr.then_inc(hp_turned, 1)
                if t == 1:
                    pe.wait_ge(kt_ready, k + 1)
                    nc.tensor.matmul(PS[:, 4, 0:DV], KTt[:, 0, :], VT[:, 0, :], start=True, stop=True)
                    nc.tensor.matmul(PS[:, 4, DV:DV + 1], KTt[:, 0, :], ones[:, 0:1], start=True, stop=True).then_inc(c1_made, 1)
                    pe.wait_ge(sp_ready, k + 1)
                    for m in range(2):
                        nc.tensor.matmul(PS[:, 6 + m, 0:C], VT[:, 0, P * m:P * m + P], SP[:, 0, :], start=True, stop=True)
                    nc.tensor.matmul(PS[:, 5, 0:C], ones[:, :], SP[:, 0, :], start=True, stop=True)
                if t == 2:
                    pe.wait_ge(qsc_ready, k + 1)
                    for m in range(2):
                        v = slice(P * m, P * m + P)
                        nc.tensor.matmul(PS[:, 6 + m, C:2 * C], VT[:, 1, v], SP[:, 1, :], start=True, stop=False)
                        nc.tensor.matmul(PS[:, 6 + m, C:2 * C], C1[:, v], Qsc[:, :], start=False, stop=True)
                    nc.tensor.matmul(PS[:, 5, C:2 * C], ones[:, :], SP[:, 1, :], start=True, stop=False)
                    nc.tensor.matmul(PS[:, 5, C:2 * C], n1r[:, :], Qsc[:, :], start=False, stop=True)
                    nc.tensor.matmul(PS[:, 4, 0:DV], KTt[:, 1, :], VT[:, 1, :], start=True, stop=True)
                    nc.tensor.matmul(PS[:, 4, DV:DV + 1], KTt[:, 1, :], ones[:, 0:1], start=True, stop=True).then_inc(c2_made, 1)
                if 4 <= t <= 7:
                    r = t - 4
                    pe.wait_ge(cs_upd, k * 4 + (r + 1))
                    for b in (2 * r, 2 * r + 1):
                        for m in range(2):
                            mm = nc.tensor.matmul(PS[:, 6 + m, TP + b:TP + b + 1], Cs[:, b, P * m:P * m + P], Q[:, TP + b:TP + b + 1],
                                                  start=True, stop=True)
                    if t == 7:
                        pe.wait_ge(nq_ready, k + 1)
                        nc.tensor.matmul(PS[:, 5, TP:T], ones[:, :], nq[:, :], start=True, stop=True).then_inc(nums_made, 1)
                if 3 <= t <= 6:
                    r = t - 3
                    pe.wait_ge(km_ready, k * 4 + (r + 1))
                    if r == 0:
                        pe.wait_ge(c2_ready, k + 1)
                    for x in range(2):
                        mm = nc.tensor.matmul(PS[:, 4, DV * x:DV * x + DV], kM[:, x, :], vS[:, :], start=True, stop=True)
                    mm.then_inc(outer_made, 1)
                if t == 9:
                    pe.wait_ge(sqh_ready, k + 1)
                    nc.tensor.matmul(PS[:, 5, 0:T], ones[:, :], SQ[:, 0, :], start=True, stop=False)
                    nc.tensor.matmul(PS[:, 5, 0:T], ones[:, :], SQ[:, 1, :], start=False, stop=True).then_inc(hss_made, 1)

            def mul_in1(it):
                for c in range(24):
                    multiply(pe, in1, it, c, c // 4, A_hi, A_lo, 4 * (c % 4), c % 4 == 0, c % 4 == 3)
                    if isinstance(it, int) and it == 0:
                        gates(c)
                    head_steps(head, it, c)
            turns(pe, in1, mul_in1, peel=1)
            for c in range(24):
                pe.wait_ge(b1_ready, 2 * (c % 3) + 2)
                multiply(pe, out1a, 0, c, c // 3, B_hi, B_lo, 4 * (c % 3), c % 3 == 0, c % 3 == 2)
                if c < 12:
                    head(c, NH - 1, Qb, Kb, OG[1])
                if c == 14:
                    pe.wait_ge(cs_upd, 4 * NH)
                    pe.wait_ge(nn_ready, NH)
                    pe.wait_ge(nq_ready, NH)
                    nc.tensor.transpose(PS[0:72, 4, 0:P], NO[:, :], ident[:, :]).then_inc(no_turned, 1)
            pe.wait_ge(b1_ready, NH)
            for c in range(8):
                multiply(pe, out1b, 0, c, c, B_hi, B_lo, 12, True, True)

        def act_mixer1(act):
            for c in range(2):
                split_hi(act, gif, 0, c)
                if c == 0:
                    act.wait_ge(pe_block, gif.n(0, 0))
                    act.wait_ge(ot_out, 64 * 4)
                    act.wait_ge(out_done, 16 * 4)
                    act.dma_start(bIF[:, :], I["ml_b_if"][0].rearrange("(h o) -> h o", o=1)).then_inc(gate_in, 16)
                    act.dma_start(mprev[:, :], I["state_mlstm_m"][0].rearrange("b h -> h b"), allow_slow_non_contiguous=True).then_inc(gate_in, 16)
                    act.dma_start(nrow[:, :], I["state_mlstm_n"][0].rearrange("b h d -> (b h) d")).then_inc(gate_in, 16)
            root(act, 2)

            def gates(c):
                if c == 0:
                    act.wait_ge(gate_f, 1)
                    nc.scalar.activation(rows[:, GY, :], rows[:, GF, :], ACT.Abs).then_inc(gate_y, 1)
                    act.wait_ge(gate_y, 1)
                    nc.scalar.activation(rows[:, GE, :], rows[:, GY, :], ACT.Exp, scale=-1.0).then_inc(gate_e, 1)
                if c == 5:
                    act.wait_ge(gate_m, 1)
                    for i in range(2):
                        last = rows[:, GNM, C * i + C - 1:C * i + C]
                        nc.scalar.activation(rows[:, GW1, C * i:C * i + C], rows[:, GA, C * i:C * i + C], ACT.Exp, bias=last)\
                          .then_inc(gate_x if i else gate_e, 1)
                    nc.scalar.activation(rows[:, GSC, 0:C], rows[:, GNM, C:2 * C], ACT.Exp, bias=m1s[:, 0:1])
                    nc.scalar.activation(rows[:, GSC, C:C + 2 * NS], rows[:, GSC, C:C + 2 * NS], ACT.Exp).then_inc(gate_x, 1)
                    nc.scalar.activation(rows[:, GEM, :], rows[:, GT, :], ACT.Exp, scale=-1.0).then_inc(gate_x, 1)
                    act.dma_start(O["p_m"][0, 0, :].rearrange("(h o) -> h o", o=1), MO[:, 0:1]).then_inc(out_done, 16)
                    act.dma_start(O["s_m"][0].rearrange("b h -> h b"), MO[:, 1:1 + NS], allow_slow_non_contiguous=True).then_inc(out_done, 16)
                if c == 7:
                    act.wait_ge(at_turned, 1)
                    nc.scalar.copy(AT[:, :], PS[:, 4, 0:32])
                    nc.scalar.copy(WKsT[:, :], PS[0:NS, 4, 32:40])
                    nc.scalar.copy(NSt[:, :], PS[:, 4, 64:128]).then_inc(at_ready, 1)
                    act.wait_ge(at_ready, 1)
                if 8 <= c <= 11:
                    act.wait_ge(bc_made, c - 7)
                    for x in range(2):
                        h = 2 * (c - 8) + x
                        for i in range(2):
                            ex = nc.scalar.activation(E[:, h, i, :], PS[:, 6 + x, C * i:C * i + C], ACT.Exp,
                                                      bias=AT[:, NH * i + h:NH * i + h + 1])
                    ex.then_inc(e_ready, 1)
                if c == 11:
                    for half in range(2):
                        load_memory(0, half)

            def memory(ap, k, half):
                return ap.rearrange("b h d v -> h d b v")[bass.ds(k, 1), :, 4 * half:4 * half + 4, :].rearrange("h d b v -> (h d) b v")

            def load_memory(k, half):
                act.dma_start(Cs[:, 4 * half:4 * half + 4, :], memory(I["state_mlstm_C"][0], k, half)).then_inc(cs_in[half], 16)

            def head(t, k, Q, K, og):
                last = isinstance(k, int) and k == NH - 1
                if t == 0:
                    act.wait_ge(hp_turned, k + 1)
                    after(act, c2_made, k)
                    for i in range(2):
                        nc.scalar.activation(KTt[:, i, :], PS[:, 4, C * i:C * i + C], ACT.Copy,
                                             scale=AT[:, bass.ds(k + (16 + NH * i), 1)])
                    nc.scalar.copy(VT[:, :, :].rearrange("p c v -> p (c v)"), PS[:, 7, :]).then_inc(kt_ready, 1)
                if t == 1:
                    act.wait_ge(c1_made, k + 1)
                    after(act, pc_out, k * 16)
                    after(act, nn_ready, k)
                    nc.scalar.copy(C1[:, :], PS[:, 4, 0:DV + 1]).then_inc(c1_copied, 1)
                if t == 2:
                    act.wait_ge(c2_ready, k + 1)
                    act.dma_start(O["p_C"][0, 0, bass.ds(k, 1), :, :].rearrange("h d v -> (h d) v"), C1[:, 0:DV]).then_inc(pc_out, 16)
                if t in (5, 7):
                    half = (t - 5) // 2
                    act.wait_ge(cs_upd, k * 4 + (2 * half + 2))
                    act.dma_start(memory(O["s_C"][0], k, half), Cs[:, 4 * half:4 * half + 4, :]).then_inc(cs_out[half], 16)
                if t == 8:
                    act.wait_ge(hn_ready, k + 1)
                    if isinstance(k, int) and k == 0:
                        act.wait_ge(ssq_added, 24)
                    nc.scalar.activation(SQ[:, :, :], Hh[:, :, :], ACT.Square).then_inc(sqh_ready, 1)
                if t in (8, 10) and not last:
                    half = (t - 8) // 2
                    act.wait_ge(nums_made, k + 1)
                    act.wait_ge(cs_out[half], k * 16 + 16)
                    load_memory(k + 1, half)
                if t == 9:
                    act.wait_ge(hss_made, k + 1)
                    nc.scalar.activation(RMS[:, :], PS[:, 5, 0:T], ACT.Sqrt, scale=1.0 / DV, bias=eps[:, :]).then_inc(rm_ready, 1)
                if t == 10:
                    act.wait_ge(yy_ready, k + 1)
                    for m in range(2):
                        cp = nc.scalar.activation(B_hi[:, bass.ds(2 * k + m, 1), :], Hh[:, m:m + 1, :], ACT.Copy,
                                                  scale=HG[:, bass.ds(2 * k + m, 1)])
                    cp.then_inc(bh1_ready, 1)

            def act_in1(it):
                for c in range(24):
                    split_hi(act, in1, it, c)
                    if isinstance(it, int) and it == 0:
                        gates(c)
                    head_steps(head, it, c)
                    if c in (19, 23):
                        g = (c - 3) // 4
                        act.wait_ge(evac_done, in1.g(it, g) + 1)
                        o = OG[g - 4]
                        nc.scalar.activation(o[:, :, :], o[:, :, :], ACT.Tanh, scale=0.5).then_inc(og_ready, 1)
            turns(act, in1, act_in1, peel=1)
            for c in range(24):
                split_hi(act, out1a, 0, c)
                if c < 12:
                    head(c, NH - 1, Qb, Kb, OG[1])
                if c == 15:
                    act.wait_ge(no_turned, 1)
                    nc.scalar.copy(OH1[:, :], PS[0:72, 4, 0:P]).then_inc(oh1_ready, 1)
                    act.wait_ge(oh1_ready, 1)
                    act.dma_start(O["s_n"][0].rearrange("b h d -> (b h) d"), OH1[0:64, :]).then_inc(out_done, 16)
                    act.dma_start(O["p_n"][0, 0], OH1[64:72, :]).then_inc(out_done, 16)
            for c in range(8):
                split_hi(act, out1b, 0, c)
                act.wait_ge(evac_done, out1b.g(0, c) + 1)
                square_and_gain(act, 3, c, MPN + KT)
            wait_outputs1(act)

        def wait_outputs1(eng):
            eng.wait_ge(pc_out, 16 * NH)
            for half in range(2):
                eng.wait_ge(cs_out[half], 16 * NH)
            eng.wait_ge(out_done, 16 * 8)

        def pool_mixer1(pool):
            pool.wait_ge(pe_block, gif.n(0, 0))
            pool.wait_ge(ot_out, 64 * 4)
            pool.wait_ge(out_done, 16 * 4)
            nc.gpsimd.memset(MASK[:, :, :], 0.0).then_inc(masks, 1)
            nc.gpsimd.tensor_copy(SEL[:, :, :], ident[0:NH, 0:NH][:, :, None].broadcast_to([NH, NH, P])).then_inc(masks, 1)
            pool.wait_ge(masks, 2)
            nc.gpsimd.affine_select(out=MASK[:, :, :], in_=MASK[:, :, :], compare_op=ALU.is_ge, fill=-1e30, base=0,
                                    pattern=[[0, 2], [1, C]], channel_multiplier=-1).then_inc(masks, 1)

            def pool_in1(it):
                for c in range(24):
                    if c == 12:
                        pool.wait_ge(evac_done, in1.g(it, 1) + 1)
                        if not (isinstance(it, int) and it == 0):
                            pool.wait_ge(nums_made, 2 * it)
                    split_lo(pool, "P", in1, it, c)
                    if c == 12:
                        nc.gpsimd.tensor_copy(Qb[:, :], QA[:, 1, :])
                        nc.gpsimd.tensor_copy(Kb[:, :], KA[:, 1, :]).then_inc(qb_copied, 1)
            turns(pool, in1, pool_in1, peel=1)
            pool.wait_ge(b1_ready, NH)
            zero_squares(pool, 3)
            for p in range(8):
                add_squares(pool, 3, p)

        def dve_mixer1(dve, link, log1p_terms):
            V = nc.vector
            row = lambda r, a=0, b=T: rows[:, r, a:b]
            for c in range(2):
                split_lo(dve, "D", gif, 0, c)
            V.tensor_scalar(HG[:, :], par[:, HNG:HNG + KT], 0.5, None, ALU.mult)
            invert(dve, 2)
            dve.wait_ge(pe_block, gif.n(0, 2))
            dve.wait_ge(gate_in, 48)
            bank = group_bank(gif, 0)
            V.tensor_tensor(IF[:, :], PS[0:2 * NH, bank, 0:T], RS[0:2 * NH, :], ALU.mult).then_inc(evac_done, 1)
            dve.wait_ge(evac_done, gif.g(0, 1))
            V.tensor_scalar(IF[:, :], IF[:, :], bIF[:, :], None, ALU.add).then_inc(gate_i, 1)

            def gates(c):
                if c in (0, 1, 2):
                    if c == 0:
                        dve.wait_ge(gate_s, 1)
                        V.tensor_copy(row(GF), PS[0:NH, 5, 0:T]).then_inc(gate_f, 1)
                        dve.wait_ge(gate_e, 1)
                    log1p_terms(c, row(GE), row(GZ), row(GY), row(GL))
                if c == 2:
                    link(V.tensor_scalar(row(GY), row(GF), 0.0, None, ALU.min))
                    link(V.scalar_tensor_tensor(row(GL), row(GL), -2.0, row(GY), ALU.mult, ALU.add))
                if c == 3:
                    for i in range(2):
                        s = (C * i, C * i + C)
                        V.tensor_tensor_scan(row(GB, *s), ones[0:NH, :], row(GL, *s), 0.0, ALU.mult, ALU.add)
                    link(V.tensor_copy(row(GB, TP, T), row(GL, TP, T)))
                    link(V.tensor_tensor(row(GA), IF[0:NH, :], row(GB), ALU.subtract))
                if c == 4:
                    link(V.tensor_tensor_scan(row(GM, 0, C), ones[0:NH, :], row(GA, 0, C), 0.0, ALU.mult, ALU.max))
                    link(V.tensor_tensor(m1s[:, 0:1], row(GB, C - 1, C), row(GM, C - 1, C), ALU.add))
                    link(V.tensor_tensor_scan(row(GM, C, TP), ones[0:NH, :], row(GA, C, TP), m1s[:, 0:1], ALU.mult, ALU.max))
                    link(V.tensor_tensor(row(GM, TP, T), row(GA, TP, T), mprev[:, :], ALU.max))
                    V.tensor_tensor(row(GT), row(GB), row(GM), ALU.add)
                    V.tensor_scalar(row(GNM), row(GM), -1.0, None, ALU.mult)
                    V.tensor_tensor(row(GSC, C, C + NS), mprev[:, :], row(GM, TP, T), ALU.subtract)
                    link(V.tensor_tensor(row(GSC, C + NS, C + 2 * NS), row(GA, TP, T), row(GM, TP, T), ALU.subtract))
                    V.tensor_copy(MO[:, 0:1], row(GT, TP - 1, TP))
                    V.tensor_copy(MO[:, 1:1 + NS], row(GT, TP, T)).then_inc(gate_m, 1)
                if 8 <= c <= 11:
                    dve.wait_ge(bc_made, c - 7)
                    g = 2 * (c - 8)
                    V.tensor_copy(ES[:, g:g + 2, :], PS[:, 4:6, 0:ESW]).then_inc(bc_copied, 1)

            def pair_keys(k, r):
                V.tensor_tensor(kM[:, :, :], kS[:, :][:, None, :].broadcast_to([NS, 2, DK]),
                                mw[:, 2 * r:2 * r + 2][:, :, None].broadcast_to([NS, 2, DK]), ALU.mult).then_inc(km_ready, 1)

            def head(t, k, Q, K, og):
                if t == 0:
                    dve.wait_ge(hp_turned, k + 1)
                    after(dve, c2_made, k)
                    after(dve, outer_made, k * 4)
                    V.tensor_tensor(SPf, PS[:, 6, 0:2 * C], Ef[:, bass.ds(k * (2 * C), 2 * C)], ALU.mult)
                    V.tensor_copy(kS[:, :], PS[0:NS, 5, 0:DK])
                    V.tensor_scalar(mw[:, :], id8, WKsT[:, bass.ds(k, 1)], None, ALU.mult)
                    V.tensor_copy(vS[:, :], PS[0:NS, 5, P:P + DV]).then_inc(sp_ready, 1)
                    dve.wait_ge(sp_ready, k + 1)
                    pair_keys(k, 0)
                if t == 1:
                    V.tensor_tensor(Qsc[:, :], Q[:, C:2 * C], decays(k, 0, C), ALU.mult)
                    dve.wait_ge(c1_copied, k + 1)
                    V.tensor_scalar(n1r[:, :], ones[:, :], C1[:, DV:DV + 1], None, ALU.mult).then_inc(qsc_ready, 1)
                if t == 2:
                    dve.wait_ge(c2_made, k + 1)
                    V.scalar_tensor_tensor(C1[:, :], C1[:, :], decays(k, C - 1, 1), PS[:, 4, 0:DV + 1], ALU.mult, ALU.add).then_inc(c2_ready, 1)
                    dve.wait_ge(c2_ready, k + 1)
                    V.tensor_copy(NO[:, bass.ds(k + 64, 1)], C1[:, DV:DV + 1]).then_inc(nn_ready, 1)
                if t == 3:
                    after(dve, nums_made, k)
                    V.tensor_tensor(nsa[:, :], K[:, TP:T], decays(k, C + NS, NS), ALU.mult)
                    new = NOv[:, :, bass.ds(k, 1)]
                    V.tensor_tensor(new, NStv[:, :, bass.ds(k, 1)], decays(k, C, NS)[:, :, None], ALU.mult).then_inc(ns_step, 1)
                    dve.wait_ge(ns_step, k * 2 + 1)
                    V.tensor_tensor(new, new, nsa[:, :][:, :, None], ALU.add).then_inc(ns_step, 1)
                    dve.wait_ge(ns_step, k * 2 + 2)
                    V.tensor_tensor(nq[:, :][:, :, None], new, Q[:, TP:T][:, :, None], ALU.mult).then_inc(nq_ready, 1)
                if 3 <= t <= 6:
                    r = t - 3
                    dve.wait_ge(outer_made, k * 4 + (r + 1))
                    if r % 2 == 0:
                        dve.wait_ge(cs_in[r // 2], k * 16 + 16)
                    for x in range(2):
                        b = 2 * r + x
                        u = V.scalar_tensor_tensor(Cs[:, b, :], Cs[:, b, :], decays(k, C + b, 1), PS[:, 4, DV * x:DV * x + DV],
                                                   ALU.mult, ALU.add)
                    u.then_inc(cs_upd, 1)
                    if r < 3:
                        pair_keys(k, r + 1)
                if t == 7:
                    dve.wait_ge(nums_made, k + 1)
                    RD = ssq[:, 0, :]
                    V.scalar_tensor_tensor(RD, PS[:, 5, 0:T], -1.0, ESf[:, bass.ds(k * ESW, T)], ALU.mult, ALU.max).then_inc(rd_step, 1)
                    dve.wait_ge(rd_step, k * 3 + 1)
                    V.tensor_tensor(RD, PS[:, 5, 0:T], RD, ALU.max).then_inc(rd_step, 1)
                    dve.wait_ge(rd_step, k * 3 + 2)
                    V.reciprocal(RD, RD).then_inc(rd_step, 1)
                    dve.wait_ge(rd_step, k * 3 + 3)
                    after(dve, b1_ready, k)
                    V.tensor_tensor(Hh[:, :, :], two(6), over2(RD), ALU.mult).then_inc(hn_ready, 1)
                if t == 9:
                    dve.wait_ge(rm_ready, k + 1)
                    RN = ssq[:, 1, :]
                    V.reciprocal(RN, RMS[:, :]).then_inc(rn_ready, 1)
                    dve.wait_ge(rn_ready, k + 1)
                    dve.wait_ge(og_ready, k + 1)
                    V.scalar_tensor_tensor(og[:, :, :], og[:, :, :], 1.0, over2(RN), ALU.add, ALU.mult).then_inc(ogs_ready, 1)
                if t == 10:
                    dve.wait_ge(ogs_ready, k + 1)
                    dve.wait_ge(sqh_ready, k + 1)
                    V.tensor_tensor(Hh[:, :, :], og[:, :, :], Hh[:, :, :], ALU.mult).then_inc(yy_ready, 1)
                if t == 11:
                    dve.wait_ge(bh1_ready, k + 1)
                    for m in range(2):
                        j = bass.ds(2 * k + m, 1)
                        lo = V.scalar_tensor_tensor(B_lo[:, j, :], Hh[:, m:m + 1, :], HG[:, j], B_hi[:, j, :].bitcast(F32), ALU.mult, ALU.subtract)
                    lo.then_inc(b1_ready, 1)

            def dve_in1(it):
                zero = isinstance(it, int) and it == 0
                rs2 = over2(RS[:, :])
                for c in range(24):
                    split_lo(dve, "D", in1, it, c)
                    if zero:
                        gates(c)
                    head_steps(head, it, c)
                    if c % 4 == 3:
                        g = c // 4
                        dve.wait_ge(pe_block, in1.n(it, c + 1))
                        if c == 3 and not zero:
                            dve.wait_ge(qb_copied, it)
                            dve.wait_ge(nums_made, 2 * it - 1)
                        if c == 11 and zero:
                            dve.wait_ge(bc_made, 4)
                        if c == 11 and not zero:
                            dve.wait_ge(hp_turned, 2 * it)
                        if c == 15:
                            dve.wait_ge(hp_turned, 2 * it + 1)
                        ps = two(group_bank(in1, g))
                        if g == 0:
                            V.scalar_tensor_tensor(QA[:, :, :], ps, DK ** -0.5, rs2, ALU.mult, ALU.mult).then_inc(evac_done, 1)
                        else:
                            out = (KA, VV, VV, OG[0], OG[1])[g - 1]
                            V.tensor_tensor(out[:, :, :], ps, rs2, ALU.mult).then_inc(evac_done, 1)
            turns(dve, in1, dve_in1, peel=1)
            for c in range(24):
                split_lo(dve, "D", out1a, 0, c)
                if c < 12:
                    head(c, NH - 1, Qb, Kb, OG[1])
                if c % 3 == 2:
                    dve.wait_ge(pe_block, out1a.n(0, c + 1))
                    add1(out1a, c // 3)
            for c in range(8):
                split_lo(dve, "D", out1b, 0, c)
                dve.wait_ge(pe_block, out1b.n(0, c + 1))
                add1(out1b, c)
                gain_lo(dve, 3, c, MPN + KT)
            wait_outputs1(dve)

        def add1(ph, p):
            x = X[:, 2 * p:2 * p + 2, :]
            nc.vector.tensor_tensor(x, two(group_bank(ph, p)), x, ALU.add).then_inc(evac_done, 1)

        block = ctx.enter_context(nc.Block())

        @block.sync
        def _(sp):
            param_rows = [("ab_norm", 0, ABN, 16), ("ml_norm", 0, MLN, 16), ("mlp_norm", 0, MPN, 32),
                          ("final_norm", 0, FIN, 16), ("ml_hnorm_g", 0, HNG, 16), ("rglru_conv_b", 0, CB, 8),
                          ("rglru_ba", 0, BA, 8), ("rglru_bx", 0, BX, 8), ("rglru_lambda", 0, LAM, 8),
                          ("conf_dw_b", 1, DWB, 8), ("conf_ln_g", 1, LNG, 8), ("conf_ln_b", 1, LNB, 8),
                          ("state_rglru_h", 1, H0, 64), ("rglru_conv_w", 1, CW, 32)]
            for name, half, col, rows in param_rows:
                sp.dma_start(prow[col - P * half:col - P * half + rows, half, :], flat(I[name], rows))\
                  .then_inc(params_in, 16)
            for c in range(2):
                sp.dma_start(xt[:, c, :], I["x_prompt"][0, P * c:P * c + P, :]).then_inc(x_in, 16)
            sp.dma_start(xs[:, :], I["x_sample"][:, 0, :]).then_inc(x_in, 16)
            w_in = I["ab_w_in"][0]
            def load_in0(it):
                for c in range(16):
                    load(sp, in0, it, c, w_in, 512 * (c % 4), 256 * it + IN0_COLS[c // 4])
                    if isinstance(it, int) and it == 0 and c == 3:
                        sp.dma_start(drow[:, :], I["conf_dw_w"][0]).then_inc(states_in, 16)
                        sp.dma_start(rrow[:, :], I["state_rglru_conv"][0].rearrange("b t c -> (b t) c")).then_inc(states_in, 16)
                        for c2 in range(2):
                            sp.dma_start(crow[:, c2, :], I["state_conf_conv"][0].rearrange("b t c -> (b t) c")[120 * c2:120 * c2 + 120, :])\
                              .then_inc(states_in, 16)
            turns(sp, in0, load_in0, peel=1)
            sp.dma_start(O["s_cconv"][0, :, 0:W31 - 2, :], I["state_conf_conv"][0, :, 1:W31 - 1, :]).then_inc(out_done, 16)
            sp.dma_start(O["s_rconv"][0, :, 0:W4 - 2, :], I["state_rglru_conv"][0, :, 1:W4 - 1, :]).then_inc(out_done, 16)
            w_out = I["ab_w_out"][0]
            for ph, row in ((out0a, 0), (out0b, DR)):
                def load_out0(it):
                    for c in range(8):
                        load(sp, ph, it, c, w_out, row + 512 * (c % 2), 1024 * it + 256 * (c // 2))
                turns(sp, ph, load_out0)
            def load_mlp(l):
                for h in (0, 1):
                    def load_up(it):
                        for c in range(8):
                            load(sp, PH[f"up{l}{h}"], it, c, I["mlp_w_up"][l], 512 * (c % 4),
                                 512 * it + (FF // 2 * h + 256 * (c // 4)))
                    def load_down(it):
                        for c in range(16):
                            load(sp, PH[f"down{l}{h}"], it, c, I["mlp_w_down"][l], FF // 2 * h + 512 * (c % 8),
                                 512 * it + 256 * (c // 8))
                    turns(sp, PH[f"up{l}{h}"], load_up)
                    turns(sp, PH[f"down{l}{h}"], load_down)
            load_mlp(0)
            load_mixer1(sp)
            load_mlp(1)
            for q in range(4):
                sp.wait_ge(fin_copied, 2 * (q + 1))
                sp.wait_ge(fin_samples, 2 * (q + 1))
                cols = slice(512 * q, 512 * q + 512)
                for c in range(2):
                    sp.dma_start(O["y_prompt"][0, P * c:P * c + P, cols], YO[:, c, cols]).then_inc(out_done, 16)
                sp.dma_start(O["y_sample"][:, 0, cols], YS[:, cols]).then_inc(out_done, 16)
            sp.wait_ge(out_done, 16 * OUTS)
            sp.wait_ge(ot_out, 64 * 4)
            wait_outputs1(sp)

        @block.tensor
        def _(pe):
            pe.wait_ge(consts, CONSTS)
            pe.wait_ge(params_in, 16 * 14)
            nc.tensor.transpose(PS[:, 4, 0:P], prow[:, 0, :], ident[:, :])
            nc.tensor.transpose(PS[:, 4, P:P + 120], prow[0:120, 1, :], ident[0:120, 0:120]).then_inc(par_turned, 1)
            pe.wait_ge(x_in, 48)
            for p in range(8):
                if p >= 2:
                    pe.wait_ge(x_loaded, p - 1)
                for m in range(2):
                    bank, f = 2 * (p % 2) + m, slice(256 * p + P * m, 256 * p + P * m + P)
                    for c in range(2):
                        nc.tensor.transpose(PS[:, bank, P * c:P * c + P], xt[:, c, f], ident[:, :])
                    tr = nc.tensor.transpose(PS[:, bank, TP:T], xs[:, f], ident[0:NS, 0:NS])
                tr.then_inc(x_turned, 1)
            pe.wait_ge(x_loaded, 8)
            def states_in_turn(part):
                pe.wait_ge(states_in, 64)
                if part == 0:
                    for j in range(8):
                        nc.tensor.transpose(PS[:, 4, 31 * j:31 * j + 31], drow[:, P * j:P * j + P], ident[0:W31, 0:W31])
                        tr = nc.tensor.transpose(PS[:, 5, 24 * j:24 * j + 24], rrow[:, P * j:P * j + P], ident[0:24, 0:24])
                else:
                    pe.wait_ge(states_ready, 2 * part)
                    for j in range(8):
                        tr = nc.tensor.transpose(PS[:, 4 + j // 4, 120 * (j % 4):120 * (j % 4) + 120],
                                                 crow[:, part - 1, P * j:P * j + P], ident[0:120, 0:120])
                tr.then_inc(states_turned, 1)

            def turn_states(q):
                for m in range(2):
                    tr = nc.tensor.transpose(PS[0:49, 4, P * m:P * m + P], TS[:, m, :], ident[:, :])
                tr.then_inc(ts_turned, 1)

            def wait_states(q):
                pe.wait_ge(tsg_ready, q + 1)
                pe.wait_ge(gates_read, q + 1)

            def mul_in0(it):
                zero = isinstance(it, int) and it == 0
                for c in range(16):
                    if c == 3 and not zero:
                        wait_states(it - 1)
                    if zero and c < 4:
                        pe.wait_ge(a_ready, 2 * (c + 1))
                    multiply(pe, in0, it, c, c // 4, A_hi, A_lo, 4 * (c % 4), c % 4 == 0, c % 4 == 3)
                    if c == 1 and zero:
                        sum_squares(pe, 0)
                    if zero and 2 <= c <= 4:
                        states_in_turn(c - 2)
                    if c == 3 and not zero:
                        turn_states(it - 1)
                    if c == 5:
                        pe.wait_ge(xc_ready, it + 1)
                        pe.wait_ge(gw_in, it * 64 + 64)
                        if zero:
                            pe.wait_ge(rms_ready, 1)
                            pe.wait_ge(states_ready, 6)
                        else:
                            pe.wait_ge(ot_ready, it)
                        for gate in range(2):
                            for m in range(2):
                                mm = nc.tensor.matmul(PS[:, 4 + 2 * gate + m, 0:T], GW[:, 2 * gate + m, :],
                                                      XC[:, m, :], start=True, stop=True)
                        mm.then_inc(gates_ready, 1)
            turns(pe, in0, mul_in0, peel=1)

            def column_sums(bank):
                nc.tensor.matmul(PS[:, bank, 0:T], ones[:, :], ssq[:, 0, :], start=True, stop=False)
                return nc.tensor.matmul(PS[:, bank, 0:T], ones[:, :], ssq[:, 1, :], start=False, stop=True)

            def mul_out0a(it):
                for c in range(8):
                    pe.wait_ge(b_ready, 2 * (c % 2 + 1))
                    multiply(pe, out0a, it, c, c // 2, B_hi, B_lo, 4 * (c % 2), c % 2 == 0, c % 2 == 1)
                    s = 8 * it + c
                    if s == 2:
                        wait_states(3)
                        turn_states(3)
                        pe.wait_ge(hs_ready, 4)
                        nc.tensor.transpose(PS[0:72, 5, 0:P], HS[:, :], ident[:, :]).then_inc(hs_turned, 1)
                    if s == 10:
                        pe.wait_ge(ln_added, 4)
                        column_sums(6).then_inc(mu_ready, 1)
                    if s == 12:
                        pe.wait_ge(ln_added, 8)
                        column_sums(7).then_inc(var_ready, 1)
            turns(pe, out0a, mul_out0a, peel=2)

            def mul_out0b(it):
                for c in range(8):
                    pe.wait_ge(b_ready, 4 + 2 * (c % 2 + 1))
                    multiply(pe, out0b, it, c, c // 2, B_hi, B_lo, 8 + 4 * (c % 2), c % 2 == 0, c % 2 == 1)
            turns(pe, out0b, mul_out0b)

            def mul_mlp(l):
                e = 1 + 2 * l
                for h in (0, 1):
                    up, down = PH[f"up{l}{h}"], PH[f"down{l}{h}"]
                    def mul_up(it):
                        for c in range(8):
                            if isinstance(it, int) and it == 0 and c < 4:
                                pe.wait_ge(a_ready, 8 * e + 2 * (c + 1))
                            multiply(pe, up, it, c, c // 4, A_hi, A_lo, 4 * (c % 4), c % 4 == 0, c % 4 == 3)
                            if isinstance(it, int) and it == 0 and c == 1 and h == 0:
                                sum_squares(pe, e)
                    def mul_down(it):
                        for c in range(16):
                            pe.wait_ge(h_ready, 16 * (2 * l + h) + 2 * (c % 8 + 1))
                            multiply(pe, down, it, c, c // 8, H_hi, H_lo, 4 * (c % 8), c % 8 == 0, c % 8 == 7)
                    turns(pe, up, mul_up, peel=1 - h)
                    turns(pe, down, mul_down)
            mul_mlp(0)
            pe_mixer1(pe)
            mul_mlp(1)
            sum_squares(pe, 2 * DEPTH)
            for p in range(8):
                pe.wait_ge(fin_ready, p + 1)
                if p == 0:
                    pe.wait_ge(evac_done, LAST.g(LAST.iters, 0))
                if p == 3:
                    pe.wait_ge(rms_ready, 2 * DEPTH + 1)
                if p >= 4:
                    pe.wait_ge(fin_copied, p - 3)
                    pe.wait_ge(fin_samples, p - 3)
                bank = 2 * (p % 4)
                for m in range(2):
                    f = X[:, 2 * p + m, :]
                    for c in range(2):
                        nc.tensor.transpose(PS[:, bank, 256 * c + P * m:256 * c + P * m + P], f[:, P * c:P * c + P], ident[:, :])
                    tr = nc.tensor.transpose(PS[0:NS, bank + 1, P * m:P * m + P], f[:, TP:T], ident[:, :])
                tr.then_inc(fin_turned, 1)

        @block.scalar
        def _(act):
            act.wait_ge(par_turned, 1)
            nc.scalar.copy(par[:, :], PS[:, 4, 0:NPAR]).then_inc(par_ready, 1)
            act.wait_ge(consts, CONSTS)
            act.wait_ge(par_ready, 1)
            for p in range(8):
                act.wait_ge(x_loaded, p + 1)
                square_and_gain(act, 0, p, ABN)
                if p % 2 == 1 and p < 7:
                    split_hi(act, in0, 0, p // 2 - HI_AHEAD)
            nc.scalar.mul(hBA[:, :], par[:, BA:BA + 8], 0.5).then_inc(absl, 1)
            nc.scalar.mul(hBX[:, :], par[:, BX:BX + 8], 0.5).then_inc(absl, 1)
            nc.scalar.mul(hLNG[:, :], par[:, LNG:LNG + 8], 0.5).then_inc(absl, 1)
            nc.scalar.mul(hLNB[:, :], par[:, LNB:LNB + 8], 0.5).then_inc(absl, 1)
            nc.scalar.activation(spt[:, 0, :], par[:, LAM:LAM + 8], ACT.Abs).then_inc(absl, 1)
            act.wait_ge(absl, 5)
            nc.scalar.activation(spt[:, 1, :], spt[:, 0, :], ACT.Exp, scale=-1.0).then_inc(expl, 1)

            def write_states(q):
                act.wait_ge(ts_turned, q + 1)
                if not isinstance(q, int) or q:
                    act.wait_ge(ot_out, q * 64)
                nc.scalar.copy(OT[:, :, :].rearrange("p m f -> p (m f)"), PS[0:49, 4, 0:256]).then_inc(ot_ready, 1)
                act.wait_ge(ot_ready, q + 1)
                cols = bass.ds(256 * q, 256)
                rows = OT[:, :, :].rearrange("p m f -> p (m f)")
                for dst, r in ((O["p_cconv"][0, 0, :, cols], slice(0, 30)),
                               (O["s_cconv"][0, :, W31 - 2, cols], slice(30, 38)),
                               (O["p_rconv"][0, 0, :, cols], slice(38, 41)),
                               (O["s_rconv"][0, :, W4 - 2, cols], slice(41, 49))):
                    act.dma_start(dst, rows[r, :]).then_inc(ot_out, 16)

            def act_in0(it):
                zero = isinstance(it, int) and it == 0
                for c in range(16):
                    split_hi(act, in0, it, c)
                    if c == 0:
                        if not zero:
                            act.wait_ge(gates_ready, it)
                        else:
                            act.wait_ge(consts, CONSTS)
                        for gate, name in enumerate(("rglru_wa", "rglru_wx")):
                            for sub in range(2):
                                src = I[name][0].rearrange("(q m s) a c -> q s a m c", m=2, s=2)[bass.ds(it, 1), sub]
                                act.dma_start(GW[64 * sub:64 * sub + 64, 2 * gate:2 * gate + 2, 64 * sub:64 * sub + 64],
                                              src.rearrange("q a m c -> (q a) m c")).then_inc(gw_in, 16)
                    if zero and c == 1:
                        root(act, 0)
                    if zero and c == 2:
                        act.wait_ge(states_turned, 1)
                        nc.scalar.copy(w31f, PS[:, 4, 0:248]).then_inc(states_ready, 1)
                        nc.scalar.copy(XRs[:, :, :, 0:3], PS[:, 5, 0:192].rearrange("p (j b w) -> p j b w", j=8, b=8))\
                          .then_inc(states_ready, 1)
                    if zero and 3 <= c <= 4:
                        half = c - 3
                        act.wait_ge(states_turned, half + 2)
                        for jh in range(2):
                            for jj in range(4):
                                cp = nc.scalar.copy(GLs[:, 4 * jh + jj, 4 * half:4 * half + 4, 0:30],
                                                    PS[:, 4 + jh, 120 * jj:120 * jj + 120].rearrange("p (b w) -> p b w", b=4))
                            cp.then_inc(states_ready, 1)
                    if c == 4 and not zero:
                        write_states(it - 1)
                    if c == 5:
                        act.wait_ge(gates_ready, it + 1)
                        if not zero:
                            act.wait_ge(hs_ready, it)
                        for m in range(2):
                            nc.scalar.activation(RG[:, m:m + 1, :], PS[:, 4 + m:5 + m, 0:T], ACT.Tanh, scale=0.5,
                                                 bias=hBA[:, bass.ds(2 * it + m, 1)])
                            q = nc.scalar.activation(IG[:, m:m + 1, :], PS[:, 6 + m:7 + m, 0:T], ACT.Tanh, scale=0.5,
                                                     bias=hBX[:, bass.ds(2 * it + m, 1)])
                        q.then_inc(gates_read, 1)
                    if c == 6:
                        act.wait_ge(gates_read, it + 1)
                        if zero:
                            act.wait_ge(lam_ready, 1)
                        for m in range(2):
                            j = bass.ds(2 * it + m, 1)
                            nc.scalar.activation(AA[:, m:m + 1, :], RG[:, m:m + 1, :], ACT.Exp, scale=hla[:, j], bias=hla[:, j])
                            q = nc.scalar.activation(TL[:, m:m + 1, :], RG[:, m:m + 1, :], ACT.Tanh, scale=nhla[:, j], bias=nhla[:, j])
                        q.then_inc(al_ready, 1)
                    if c == 8:
                        act.wait_ge(evac_done, in0.g(it, 1) + 1)
                        nc.scalar.activation(G2[:, :, :], G[:, :, :], ACT.Square).then_inc(g2_ready, 1)
                        act.wait_ge(w_ready, it + 1)
                        nc.scalar.activation(TL[:, :, :], TL[:, :, :], ACT.Sqrt, bias=tiny[:, :]).then_inc(root_ready, 1)
                    if c == 9:
                        act.wait_ge(g3_ready, it + 1)
                        nc.scalar.activation(G3[:, :, :], G3[:, :, :], ACT.Tanh, scale=0.7978845608028654).then_inc(gth_ready, 1)
                    if c == 11:
                        act.wait_ge(y_ready, it + 1)
                        nc.scalar.activation(B_hi[:, bass.ds(2 * it, 2), :], G2[:, :, :], ACT.Copy).then_inc(bh_ready, 1)
                    if c == 12:
                        act.wait_ge(evac_done, in0.g(it, 2) + 1)
                        nc.scalar.activation(TB[:, :, :], TB[:, :, :], ACT.Tanh, scale=0.5).then_inc(tb_ready, 1)
            turns(act, in0, act_in0, peel=1)

            def act_out0a(it):
                for c in range(8):
                    split_hi(act, out0a, it, c)
                    s = 8 * it + c
                    if s == 3:
                        write_states(3)
                        act.wait_ge(hs_turned, 1)
                        nc.scalar.copy(OH[:, :], PS[0:72, 5, 0:P]).then_inc(oh_ready, 1)
                        act.wait_ge(oh_ready, 1)
                        act.dma_start(flat(O["s_rh"], 64), OH[0:64, :]).then_inc(out_done, 16)
                        act.dma_start(flat(O["p_rh"], 8), OH[64:72, :]).then_inc(out_done, 16)
                    if s == 11:
                        for q in range(4):
                            act.wait_ge(yd_ready, q + 1)
                            if q:
                                act.wait_ge(ln_added, 4 + q)
                            nc.scalar.activation(SQ[:, :, :], YC[:, 2 * q:2 * q + 2, :], ACT.Square).then_inc(lsq_ready, 1)
                    if s == 12:
                        act.wait_ge(var_ready, 1)
                        nc.scalar.activation(G[:, 1, :], PS[:, 7, 0:T], ACT.Sqrt, scale=1.0 / DR, bias=eps[:, :]).then_inc(dev_ready, 1)
                        for q in range(4):
                            act.wait_ge(yn_ready, q + 1)
                            for m in range(2):
                                j = slice(2 * q + m, 2 * q + m + 1)
                                th = nc.scalar.activation(Tb[q][:, m, :], YC[:, 2 * q + m, :], ACT.Tanh, scale=hLNG[:, j], bias=hLNB[:, j])
                            th.then_inc(lth_ready, 1)
                    if s == 13:
                        for q in range(4):
                            act.wait_ge(z_ready, q + 1)
                            nc.scalar.activation(B_hi[:, 8 + 2 * q:10 + 2 * q, :], Zb[q][:, :, :], ACT.Copy, scale=0.5).then_inc(bh_ready, 1)
            turns(act, out0a, act_out0a, peel=2)

            def act_out0b(it):
                for c in range(8):
                    split_hi(act, out0b, it, c)
                    if c % 2 == 1:
                        act.wait_ge(evac_done, out0b.g(it, c // 2) + 1)
                        square_and_gain(act, 1, 4 * it + c // 2, MPN)
            turns(act, out0b, act_out0b)

            def act_mlp(l):
                for h in (0, 1):
                    up, down = PH[f"up{l}{h}"], PH[f"down{l}{h}"]
                    k = 2 * l + h
                    def act_up(it):
                        for c in range(8):
                            split_hi(act, up, it, c)
                            if isinstance(it, int) and it == 0 and c == 2 and h == 0:
                                root(act, 1 + 2 * l)
                            if c % 4 == 3:
                                p = 2 * it + c // 4
                                act.wait_ge(u_ready, p + (16 * k + 1))
                                nc.scalar.activation(H_hi[:, bass.ds(2 * p, 2), :], U[:, :, :], ACT.Copy).then_inc(hh_ready, 1)
                    def act_down(it):
                        for c in range(16):
                            split_hi(act, down, it, c)
                            if c % 8 == 7 and h == 1:
                                act.wait_ge(evac_done, down.g(it, c // 8) + 1)
                                square_and_gain(act, 2 + 2 * l, 2 * it + c // 8, None if l == DEPTH - 1 else MLN)
                    turns(act, up, act_up, peel=1 - h)
                    turns(act, down, act_down, tail=1 if down is LAST else 0)
            act_mlp(0)
            act_mixer1(act)
            act_mlp(1)
            root(act, 2 * DEPTH)
            for p in range(8):
                act.wait_ge(fin_turned, p + 1)
                nc.scalar.copy(YO[:, :, 256 * p:256 * p + 256], PS[:, 2 * (p % 4), :].rearrange("p (c f) -> p c f", c=2)).then_inc(fin_copied, 1)

        @block.gpsimd
        def _(pool):
            nc.gpsimd.memset(ident[:, :], 0.0).then_inc(zeroed, 1)
            nc.gpsimd.memset(ones[:, :], 1.0).then_inc(consts, 1)
            pool.wait_ge(zeroed, 1)
            nc.gpsimd.affine_select(out=ident[:, :], in_=ident[:, :], compare_op=ALU.not_equal, fill=1.0, base=0,
                                    pattern=[[-1, P]], channel_multiplier=1).then_inc(consts, 1)
            nc.gpsimd.memset(eps[:, :], EPS).then_inc(consts, 1)
            nc.gpsimd.memset(tiny[:, :], 1e-30).then_inc(consts, 1)
            nc.gpsimd.memset(GW[:, :, :], 0.0).then_inc(consts, 1)
            nc.gpsimd.memset(GLp[:, :, 0:W31 - 1], 0.0).then_inc(consts, 1)
            nc.gpsimd.memset(XRp[:, :, 0:W4 - 1], 0.0).then_inc(consts, 1)
            zero_squares(pool, 0)
            for p in range(8):
                add_squares(pool, 0, p)

            def glu_columns(q):
                nc.gpsimd.tensor_copy(TS[:, :, 0:30], GLp[:, :, TP:TP + 30])
                nc.gpsimd.tensor_copy(TS[:, :, 30:38], GLs[:, bass.ds(2 * q, 2), :, W31 - 1]).then_inc(tsg_ready, 1)

            def pool_in0(it):
                zero = isinstance(it, int) and it == 0
                pair = bass.ds(2 * it, 2)
                for c in range(16):
                    if c == 0 and not zero:
                        pool.wait_ge(gl_ready, it)
                    if c == 4:
                        pool.wait_ge(evac_done, in0.g(it, 0) + 1)
                        if not zero:
                            pool.wait_ge(ts_turned, it)
                    if c == 11:
                        pool.wait_ge(h0_ready, it + 1)
                    split_lo(pool, "P", in0, it, c)
                    if c == 0 and not zero:
                        glu_columns(it - 1)
                    if c == 4:
                        nc.gpsimd.tensor_copy(TS[:, :, 38:41], XRp[:, :, TP:TP + 3])
                        nc.gpsimd.tensor_copy(TS[:, :, 41:49], XRs[:, pair, :, 3]).then_inc(tsx_ready, 1)
                    if c == 11:
                        nc.gpsimd.tensor_copy(HSv[:, pair, :], RG[:, :, TP:T])
                        nc.gpsimd.tensor_copy(HS[:, bass.ds(2 * it + 64, 2)], RG[:, :, TP - 1]).then_inc(hs_ready, 1)
            turns(pool, in0, pool_in0, peel=1)
            pool.wait_ge(gl_ready, 4)
            glu_columns(3)

            def pool_out0a(it):
                for c in range(8):
                    split_lo(pool, "P", out0a, it, c)
                    s = 8 * it + c
                    if s == 0:
                        pool.wait_ge(ssq_ready, 1)
                        nc.gpsimd.memset(ssq[:, :, :], 0.0).then_inc(ln_zeroed, 1)
                    if s in (1, 2, 3, 9):
                        q = min(s - 1, 3)
                        pool.wait_ge(ln_zeroed, 1)
                        pool.wait_ge(yc_ready, q + 1)
                        if q:
                            pool.wait_ge(ln_added, q)
                        nc.gpsimd.tensor_tensor(ssq[:, :, :], ssq[:, :, :], YC[:, 2 * q:2 * q + 2, :], ALU.add).then_inc(ln_added, 1)
                    if s == 10:
                        pool.wait_ge(mu_ready, 1)
                        nc.gpsimd.memset(ssq[:, :, :], 0.0).then_inc(ln_zeroed, 1)
                    if s == 11:
                        pool.wait_ge(ln_zeroed, 2)
                        for q in range(4):
                            pool.wait_ge(lsq_ready, q + 1)
                            if q:
                                pool.wait_ge(ln_added, 4 + q)
                            nc.gpsimd.tensor_tensor(ssq[:, :, :], ssq[:, :, :], SQ[:, :, :], ALU.add).then_inc(ln_added, 1)
            turns(pool, out0a, pool_out0a, peel=2)
            pool.wait_ge(var_ready, 1)
            zero_squares(pool, 1)

            def pool_out0b(it):
                for c in range(8):
                    split_lo(pool, "P", out0b, it, c)
                    if c % 2 == 1:
                        add_squares(pool, 1, 4 * it + c // 2)
            turns(pool, out0b, pool_out0b)

            def pool_mlp(l):
                zero_squares(pool, 2 + 2 * l)
                down = PH[f"down{l}1"]
                def pool_down(it):
                    for c in (7, 15):
                        add_squares(pool, 2 + 2 * l, 2 * it + c // 8)
                turns(pool, down, pool_down)
            pool_mlp(0)
            pool_mixer1(pool)
            pool_mlp(1)

        @block.vector
        def _(dve):
            V = nc.vector
            steps = [0]

            def link(ins):
                steps[0] += 1
                ins.then_inc(small, 1)
                dve.wait_ge(small, steps[0])

            def log1p_terms(part, e, z, z2, p):
                if part == 0:
                    link(V.tensor_scalar(z2, e, 2.0, None, ALU.add))
                    link(V.reciprocal(z, z2))
                    link(V.tensor_tensor(z, z, e, ALU.mult))
                    link(V.tensor_tensor(z2, z, z, ALU.mult))
                    link(V.tensor_scalar(p, z2, 1.0 / 17, None, ALU.mult))
                for k in ((), (7, 6, 5, 4), (3, 2, 1))[part]:
                    link(V.scalar_tensor_tensor(p, p, 1.0 / (2 * k + 1), z2, ALU.add, ALU.mult))
                if part == 2:
                    link(V.scalar_tensor_tensor(p, p, 1.0, z, ALU.add, ALU.mult))

            for p in range(8):
                dve.wait_ge(x_turned, p + 1)
                V.tensor_copy(X[:, 2 * p:2 * p + 2, :], two(2 * (p % 2))).then_inc(x_loaded, 1)
                if p:
                    gain_lo(dve, 0, p - 1, ABN)
                if p in (5, 7):
                    split_lo(dve, "D", in0, 0, (p - 5) // 2 - LO_AHEAD)
            gain_lo(dve, 0, 7, ABN)
            dve.wait_ge(expl, 1)
            for part in range(3):
                log1p_terms(part, spt[:, 1, :], spt[:, 2, :], spt[:, 3, :], spt[:, 4, :])
            link(V.tensor_scalar(spt[:, 5, :], par[:, LAM:LAM + 8], -1.0, 0.0, ALU.mult, ALU.max))
            link(V.scalar_tensor_tensor(spt[:, 5, :], spt[:, 4, :], 2.0, spt[:, 5, :], ALU.mult, ALU.add))
            link(V.tensor_scalar(hla[:, :], spt[:, 5, :], -4.0, None, ALU.mult))
            V.tensor_scalar(nhla[:, :], spt[:, 5, :], 4.0, None, ALU.mult).then_inc(lam_ready, 1)

            def taps(q, c, last):
                for w in range(2 * c, 2 * c + (3 if last else 2)):
                    for m in range(2):
                        j = 2 * q + m
                        y = YC[:, bass.ds(j, 1), 0:TP]
                        x = GLp[:, m:m + 1, w:w + TP]
                        ww = w31f[:, bass.ds(31 * j + w, 1)]
                        if w == 0:
                            dve.wait_ge(gl_ready, q + 1)
                            V.tensor_scalar(y, x, ww, par[:, bass.ds(j + DWB, 1)], ALU.mult, ALU.add).then_inc(tap_done, 1)
                        else:
                            dve.wait_ge(tap_done, q * 62 + (2 * w + m - 1))
                            V.scalar_tensor_tensor(y, x, ww, y, ALU.mult, ALU.add).then_inc(tap_done, 1)

            def sample_conv(q):
                pair = bass.ds(2 * q, 2)
                w = w31[:, pair, :][:, :, None, :].broadcast_to([P, 2, NS, W31])
                V.tensor_tensor(GP[:, :, :, :], GLs[:, pair, :, :], w, ALU.mult).then_inc(cs_step, 1)
                dve.wait_ge(cs_step, q * 2 + 1)
                V.tensor_reduce(YC[:, pair, TP:T], GP[:, :, :, :], AX.X, ALU.add).then_inc(cs_step, 1)
                dve.wait_ge(cs_step, q * 2 + 2)
                bias = par[:, bass.ds(2 * q + DWB, 2)][:, :, None].broadcast_to([P, 2, NS])
                V.tensor_tensor(YC[:, pair, TP:T], YC[:, pair, TP:T], bias, ALU.add).then_inc(yc_ready, 1)

            def dve_in0(it):
                zero = isinstance(it, int) and it == 0
                pair = bass.ds(2 * it, 2)
                rs2, rsp, rss = over2(RS[:, :]), over2(RS[:, 0:TP]), over2(RS[:, TP:T])
                for c in range(16):
                    split_lo(dve, "D", in0, it, c)
                    if not zero and c < 15:
                        taps(it - 1, c, c == 14)
                    if c == 3:
                        if zero:
                            invert(dve, 0)
                        else:
                            dve.wait_ge(tsx_ready, it)
                        dve.wait_ge(pe_block, in0.n(it, 4))
                        b = group_bank(in0, 0)
                        V.tensor_tensor(XRp[:, :, 3:3 + TP], PS[:, b:b + 2, 0:TP], rsp, ALU.mult)
                        V.tensor_tensor(XRs[:, pair, :, 3], PS[:, b:b + 2, TP:T], rss, ALU.mult).then_inc(evac_done, 1)
                        dve.wait_ge(evac_done, in0.g(it, 0) + 1)
                        if zero:
                            dve.wait_ge(states_turned, 3)
                        for w in range(W4):
                            for m in range(2):
                                y, x = XC[:, m:m + 1, 0:TP], XRp[:, m:m + 1, w:w + TP]
                                ww = par[:, bass.ds(2 * it + (CW + 8 * w + m), 1)]
                                if w == 0:
                                    V.tensor_scalar(y, x, ww, par[:, bass.ds(2 * it + (CB + m), 1)], ALU.mult, ALU.add).then_inc(xc_tap, 1)
                                else:
                                    dve.wait_ge(xc_tap, it * 8 + (2 * w + m - 1))
                                    V.scalar_tensor_tensor(y, x, ww, y, ALU.mult, ALU.add).then_inc(xc_tap, 1)
                    if c == 4:
                        if zero:
                            dve.wait_ge(states_ready, 2)
                        w = CWv[:, pair, :][:, :, None, :].broadcast_to([P, 2, NS, W4])
                        V.tensor_tensor(XP[:, :, :, :], XRs[:, pair, :, :], w, ALU.mult).then_inc(xs_step, 1)
                        dve.wait_ge(xs_step, it * 2 + 1)
                        V.tensor_reduce(XC[:, :, TP:T], XP[:, :, :, :], AX.X, ALU.add).then_inc(xs_step, 1)
                        dve.wait_ge(xs_step, it * 2 + 2)
                        bias = par[:, bass.ds(2 * it + CB, 2)][:, :, None].broadcast_to([P, 2, NS])
                        V.tensor_tensor(XC[:, :, TP:T], XC[:, :, TP:T], bias, ALU.add).then_inc(xc_ready, 1)
                    if c == 7:
                        dve.wait_ge(pe_block, in0.n(it, 8))
                        V.tensor_tensor(G[:, :, :], two(group_bank(in0, 1)), rs2, ALU.mult).then_inc(evac_done, 1)
                        dve.wait_ge(al_ready, it + 1)
                        V.tensor_tensor(RG[:, :, :], AA[:, :, :], AA[:, :, :], ALU.mult).then_inc(w_step, 1)
                        V.scalar_tensor_tensor(IG[:, :, :], IG[:, :, :], 1.0, XC[:, :, :], ALU.add, ALU.mult).then_inc(t_ready, 1)
                        dve.wait_ge(w_step, it + 1)
                        V.scalar_tensor_tensor(TL[:, :, :], RG[:, :, :], 1.0, TL[:, :, :], ALU.add, ALU.mult).then_inc(w_ready, 1)
                    if c == 8:
                        dve.wait_ge(g2_ready, it + 1)
                        V.tensor_scalar(G3[:, :, :], G2[:, :, :], 0.044715, 1.0, ALU.mult, ALU.add).then_inc(g3_step, 1)
                        dve.wait_ge(g3_step, it + 1)
                        V.tensor_tensor(G3[:, :, :], G3[:, :, :], G[:, :, :], ALU.mult).then_inc(g3_ready, 1)
                    if c == 9:
                        dve.wait_ge(root_ready, it + 1)
                        dve.wait_ge(t_ready, it + 1)
                        V.scalar_tensor_tensor(IG[:, :, :], IG[:, :, :], 0.5, TL[:, :, :], ALU.mult, ALU.mult).then_inc(u0_ready, 1)
                        V.tensor_tensor(RG[:, :, TP:T], AA[:, :, TP:T], H0v[:, pair, :], ALU.mult).then_inc(h0_step, 1)
                        dve.wait_ge(u0_ready, it + 1)
                        for m in range(2):
                            V.tensor_tensor_scan(RG[:, m, 0:TP], AA[:, m, 0:TP], IG[:, m, 0:TP], 0.0, ALU.mult, ALU.add)
                        dve.wait_ge(h0_step, it + 1)
                        V.tensor_tensor(RG[:, :, TP:T], RG[:, :, TP:T], IG[:, :, TP:T], ALU.add).then_inc(h0_ready, 1)
                    if c == 10:
                        dve.wait_ge(gth_ready, it + 1)
                        V.scalar_tensor_tensor(G[:, :, :], G3[:, :, :], 1.0, G[:, :, :], ALU.add, ALU.mult).then_inc(gl_step, 1)
                        dve.wait_ge(gl_step, it + 1)
                        dve.wait_ge(h0_ready, it + 1)
                        V.scalar_tensor_tensor(G2[:, :, :], G[:, :, :], 0.5, RG[:, :, :], ALU.mult, ALU.mult).then_inc(y_ready, 1)
                    if c == 11:
                        dve.wait_ge(pe_block, in0.n(it, 12))
                        V.tensor_tensor(TB[:, :, :], two(group_bank(in0, 2)), rs2, ALU.mult).then_inc(evac_done, 1)
                    if c == 12:
                        dve.wait_ge(bh_ready, it + 1)
                        V.tensor_tensor(B_lo[:, pair, :], G2[:, :, :], B_hi[:, pair, :].bitcast(F32), ALU.subtract).then_inc(b_ready, 1)
                    if c == 15:
                        if not zero:
                            if not isinstance(it, int) or it == 1:
                                dve.wait_ge(states_ready, 6)
                            sample_conv(it - 1)
                            dve.wait_ge(tsg_ready, it)
                            dve.wait_ge(tap_done, it * 62)
                        dve.wait_ge(pe_block, in0.n(it, 16))
                        V.scalar_tensor_tensor(XC[:, :, :], two(group_bank(in0, 3)), 0.5, rs2, ALU.mult, ALU.mult).then_inc(evac_done, 1)
                        dve.wait_ge(evac_done, in0.g(it, 3) + 1)
                        dve.wait_ge(tb_ready, it + 1)
                        V.scalar_tensor_tensor(GLp[:, :, 30:30 + TP], TB[:, :, 0:TP], 1.0, XC[:, :, 0:TP], ALU.add, ALU.mult)
                        V.scalar_tensor_tensor(GLs[:, pair, :, 30], TB[:, :, TP:T], 1.0, XC[:, :, TP:T], ALU.add, ALU.mult).then_inc(gl_ready, 1)
            turns(dve, in0, dve_in0, peel=1)

            def add_to_x(ph, it, j, p):
                x = X[:, bass.ds(2 * p, 2), :]
                V.tensor_tensor(x, two(group_bank(ph, j)), x, ALU.add).then_inc(evac_done, 1)

            def dve_out0a(it):
                for c in range(8):
                    split_lo(dve, "D", out0a, it, c)
                    s = 8 * it + c
                    if s < 8:
                        taps(3, 2 * s, False)
                        if s < 7:
                            taps(3, 2 * s + 1, False)
                        else:
                            for m in range(2):
                                dve.wait_ge(tap_done, 3 * 62 + 2 * 30 + m - 1)
                                y = YC[:, 6 + m:7 + m, 0:TP]
                                V.scalar_tensor_tensor(y, GLp[:, m:m + 1, 30:30 + TP], w31f[:, 31 * (6 + m) + 30:31 * (6 + m) + 31], y,
                                                       ALU.mult, ALU.add).then_inc(tap_done, 1)
                            sample_conv(3)
                    if s == 10:
                        dve.wait_ge(mu_ready, 1)
                        V.tensor_scalar(G[:, 0, :], PS[:, 6, 0:T], 1.0 / DR, None, ALU.mult).then_inc(mu_copied, 1)
                        dve.wait_ge(mu_copied, 1)
                        dve.wait_ge(tap_done, 4 * 62)
                        dve.wait_ge(yc_ready, 4)
                        dve.wait_ge(ln_added, 4)
                        for q in range(4):
                            y = YC[:, 2 * q:2 * q + 2, :]
                            V.tensor_tensor(y, y, over2(G[:, 0, :]), ALU.subtract).then_inc(yd_ready, 1)
                    if s == 12:
                        dve.wait_ge(dev_ready, 1)
                        V.reciprocal(G[:, 1, :], G[:, 1, :]).then_inc(rv_ready, 1)
                        dve.wait_ge(rv_ready, 1)
                        dve.wait_ge(yd_ready, 4)
                        dve.wait_ge(lsq_ready, 4)
                        for q in range(4):
                            y = YC[:, 2 * q:2 * q + 2, :]
                            V.tensor_tensor(y, y, over2(G[:, 1, :]), ALU.mult).then_inc(yn_ready, 1)
                        for q in range(4):
                            dve.wait_ge(yn_ready, q + 1)
                            for m in range(2):
                                j = 2 * q + m
                                zz = V.tensor_scalar(Zb[q][:, m, :], YC[:, j, :], par[:, LNG + j:LNG + j + 1],
                                                     par[:, LNB + j:LNB + j + 1], ALU.mult, ALU.add)
                            zz.then_inc(z_step, 1)
                    if s == 13:
                        for q in range(4):
                            dve.wait_ge(z_step, q + 1)
                            dve.wait_ge(lth_ready, q + 1)
                            V.scalar_tensor_tensor(Zb[q][:, :, :], Tb[q][:, :, :], 1.0, Zb[q][:, :, :], ALU.add, ALU.mult).then_inc(z_ready, 1)
                    if s == 14:
                        for q in range(4):
                            k = slice(8 + 2 * q, 10 + 2 * q)
                            dve.wait_ge(bh_ready, 5 + q)
                            V.scalar_tensor_tensor(B_lo[:, k, :], Zb[q][:, :, :], 0.5, B_hi[:, k, :].bitcast(F32),
                                                   ALU.mult, ALU.subtract).then_inc(b_ready, 1)
                    if c % 2 == 1:
                        dve.wait_ge(pe_block, out0a.n(it, c + 1))
                        add_to_x(out0a, it, c // 2, 4 * it + c // 2)
            turns(dve, out0a, dve_out0a, peel=2)

            def dve_out0b(it):
                for c in range(8):
                    split_lo(dve, "D", out0b, it, c)
                    if c % 2 == 1:
                        p = 4 * it + c // 2
                        dve.wait_ge(pe_block, out0b.n(it, c + 1))
                        add_to_x(out0b, it, c // 2, p)
                        gain_lo(dve, 1, p, MPN)
            turns(dve, out0b, dve_out0b)

            def dve_mlp(l):
                for h in (0, 1):
                    up, down = PH[f"up{l}{h}"], PH[f"down{l}{h}"]
                    k = 2 * l + h
                    def dve_up(it):
                        for c in range(8):
                            split_lo(dve, "D", up, it, c)
                            if c % 4 == 3:
                                p = 2 * it + c // 4
                                if isinstance(it, int) and it == 0 and c == 3 and h == 0:
                                    invert(dve, 1 + 2 * l)
                                dve.wait_ge(pe_block, up.n(it, c + 1))
                                V.tensor_tensor(UT[:, :, :], two(group_bank(up, c // 4)), over2(RS[:, :]), ALU.mult).then_inc(evac_done, 1)
                                dve.wait_ge(evac_done, up.g(it, c // 4) + 1)
                                V.scalar_tensor_tensor(U[:, :, :], UT[:, :, :], 0.0, UT[:, :, :], ALU.max, ALU.mult).then_inc(u_ready, 1)
                                dve.wait_ge(hh_ready, p + (16 * k + 1))
                                q = bass.ds(2 * p, 2)
                                V.tensor_tensor(H_lo[:, q, :], U[:, :, :], H_hi[:, q, :].bitcast(F32), ALU.subtract).then_inc(h_ready, 1)
                    def dve_down(it):
                        for c in range(16):
                            split_lo(dve, "D", down, it, c)
                            if c % 8 == 7:
                                p = 2 * it + c // 8
                                dve.wait_ge(pe_block, down.n(it, c + 1))
                                add_to_x(down, it, c // 8, p)
                                if h == 1 and l < DEPTH - 1:
                                    gain_lo(dve, 2 + 2 * l, p, MLN)
                    turns(dve, up, dve_up, peel=1 - h)
                    turns(dve, down, dve_down, tail=1 if down is LAST else 0)
            dve_mlp(0)
            dve_mixer1(dve, link, log1p_terms)
            dve_mlp(1)
            invert(dve, 2 * DEPTH)
            dve.wait_ge(evac_done, LAST.g(LAST.iters, 0))
            dve.wait_ge(sq_ready, 8 * (2 * DEPTH + 1))
            for p in range(8):
                for m in range(2):
                    j = 2 * p + m
                    y = V.scalar_tensor_tensor(X[:, j, :], X[:, j, :], par[:, FIN + j:FIN + j + 1], RS[:, :], ALU.mult, ALU.mult)
                y.then_inc(fin_ready, 1)
                dve.wait_ge(fin_turned, p + 1)
                V.tensor_copy(YS[:, 256 * p:256 * p + 256], PS[0:NS, 2 * (p % 4) + 1, 0:256]).then_inc(fin_samples, 1)


def flat(ap, rows):
    n = len(ap.shape)
    if n == 1:
        ap = ap.rearrange("(r f) -> r f", f=P)
    elif n == 2:
        ap = ap.rearrange("a (r f) -> (a r) f", f=P)
    else:
        ap = ap.rearrange("a b (r f) -> (a b r) f", f=P)
    assert ap.shape[0] == rows
    return ap


INS = ["x_prompt", "x_sample", "state_rglru_conv", "state_rglru_h", "state_conf_conv", "state_mlstm_C",
       "state_mlstm_n", "state_mlstm_m", "ab_norm", "ab_w_in", "rglru_conv_w", "rglru_conv_b", "rglru_wa",
       "rglru_ba", "rglru_wx", "rglru_bx", "rglru_lambda", "conf_dw_w", "conf_dw_b", "conf_ln_g", "conf_ln_b",
       "ab_w_out", "ml_norm", "ml_w_in", "ml_b_if", "ml_hnorm_g", "ml_w_out", "mlp_norm", "mlp_w_up",
       "mlp_w_down", "final_norm"]
OUTPUTS = [("y_prompt", (1, TP, D)), ("y_sample", (NS, 1, D)),
           ("p_rconv", (1, 1, W4 - 1, DR)), ("p_rh", (1, 1, DR)), ("p_cconv", (1, 1, W31 - 1, DR)),
           ("p_C", (1, 1, NH, DK, DV)), ("p_n", (1, 1, NH, DK)), ("p_m", (1, 1, NH)),
           ("s_rconv", (1, NS, W4 - 1, DR)), ("s_rh", (1, NS, DR)), ("s_cconv", (1, NS, W31 - 1, DR)),
           ("s_C", (1, NS, NH, DK, DV)), ("s_n", (1, NS, NH, DK)), ("s_m", (1, NS, NH))]


def kernel(**inputs):
    import numpy as np
    import concourse.bacc as bacc
    from concourse.bass_utils import run_bass_kernel_spmd

    nc = bacc.Bacc("TRN2", target_bir_lowering=False, num_devices=1)
    arrays, ins, outs = {}, {}, {}
    for name in INS:
        a = np.ascontiguousarray(inputs[name])
        arrays[f"in_{name}"] = a
        ins[name] = nc.dram_tensor(f"in_{name}", a.shape, mybir.dt.from_np(a.dtype), kind="ExternalInput").ap()
    for name, shape in OUTPUTS:
        outs[name] = nc.dram_tensor(f"out_{name}", shape, F32, kind="ExternalOutput").ap()
    program(nc, ins, outs)
    r = run_bass_kernel_spmd(nc, [arrays], core_ids=[0])
    return tuple(r.results[0][f"out_{name}"] for name, _ in OUTPUTS)
```

```python
from contextlib import ExitStack

import concourse.bass as bass
from concourse import mybir

F32 = mybir.dt.float32
F32R = mybir.dt.float32r
ACT = mybir.ActivationFunctionType
ALU = mybir.AluOpType
AX = mybir.AxisListType

P = 128
D = 2048
KT = D // P
TP, NS = 256, 8
T = TP + NS
DR = D // 2
FF = 4 * D
NH, DK, DV = 8, 128, 256
W4, W31 = 4, 31
C = 128
ESW = T + C + 2 * NS
EPS = 1e-6
BLK = 1024
RAW, SPLIT = 8, 4
HI_AHEAD, LO_AHEAD = 3, 2

ABN, MLN, MPN, FIN, HNG, CB, BA, BX, LAM = 0, 16, 32, 64, 80, 96, 104, 112, 120
DWB, LNG, LNB, H0, CW = 128, 136, 144, 152, 216
NPAR = 248


class Phase:

    def __init__(self, before, iters, steps, groups, lo="D"):
        self.iters, self.steps, self.groups = iters, steps, groups
        self.lo = (lo * steps)[:steps]
        self.n0 = before.n0 + before.iters * before.steps if before else 0
        self.g0 = before.g0 + before.iters * before.groups if before else 0
        self.d0 = before.d0 + before.iters * before.lo.count("D") if before else 0
        self.p0 = before.p0 + before.iters * before.lo.count("P") if before else 0
        self.next = None
        if before:
            before.next = self
            assert before.iters == 1 or before.lo[:LO_AHEAD] == self.lo[:LO_AHEAD]
        assert iters == 1 or (steps % RAW == 0 and groups % 2 == 0)

    def splitter(self, c):
        if c < self.steps:
            return self.lo[c]
        after = self.next if self.iters == 1 else self
        return after.lo[c - self.steps] if after else "D"

    def n(self, it, c):
        return self.n0 + c + it * self.steps

    def g(self, it, j):
        return self.g0 + j + it * self.groups


DEPTH = 2


def phases():
    ph = {}
    def add(name, *a, **k):
        ph[name] = Phase(list(ph.values())[-1] if ph else None, *a, **k)
    add("in0", 4, 16, 4, lo="DDPPDPPPDPPPDPPP")
    add("out0a", 1, 16, 8, lo="DDPPPPDPPPPPPPDP")
    add("out0b", 1, 16, 8, lo="PPDDPDPDPDPDPDPD")
    for l in range(DEPTH):
        for h in (0, 1):
            add(f"up{l}{h}", 8, 8, 2)
            add(f"down{l}{h}", 4, 16, 2)
        if l == 0:
            add("gif", 1, 2, 1)
            add("in1", 4, 24, 6, lo="DDPDDDPDDDPDDDPDDDPDDDPD")
            add("out1a", 1, 24, 8, lo="DDPDDDPDDDPDDDPDDDPDDDPD")
            add("out1b", 1, 8, 8, lo="DDPDPDPD")
    return ph


PH = phases()
LAST = PH[f"down{DEPTH - 1}1"]
NB = LAST.n(LAST.iters, 0)


def program(nc, I, O):
    ctx = ExitStack()
    with ctx:
        def sem(name):
            return ctx.enter_context(nc.semaphore(name))

        def sb(stack, name, shape, dt=F32):
            return stack.enter_context(nc.sbuf_tensor(name, shape, dt))

        X = sb(ctx, "X", [P, KT, T])
        raw = sb(ctx, "raw", [P, RAW, BLK])
        w_hi = sb(ctx, "w_hi", [P, SPLIT, BLK], F32R)
        w_lo = sb(ctx, "w_lo", [P, SPLIT, BLK], F32R)
        ident = sb(ctx, "ident", [P, P])
        ones = sb(ctx, "ones", [P, P])
        par = sb(ctx, "par", [P, NPAR])
        SQ = sb(ctx, "SQ", [P, 2, T])
        ssq = sb(ctx, "ssq", [P, 2, T])
        RMS = sb(ctx, "RMS", [P, T])
        RS = sb(ctx, "RS", [P, T])
        eps = sb(ctx, "eps", [P, 1])
        tiny = sb(ctx, "tiny", [P, 1])
        PS = ctx.enter_context(nc.psum_tensor("PS", [P, 8, 512], F32))

        inputs = ExitStack()
        A_hi = sb(inputs, "A_hi", [P, KT, T], F32R)
        A_lo = sb(inputs, "A_lo", [P, KT, T], F32R)
        mixers = ExitStack()
        B_hi = sb(mixers, "B_hi0", [P, KT, T], F32R)
        B_lo = sb(mixers, "B_lo0", [P, KT, T], F32R)
        m0 = ExitStack()
        GLs = sb(m0, "GLs", [P, 8, NS, W31])
        XRs = sb(m0, "XRs", [P, 8, NS, W4])
        w31 = sb(m0, "w31", [P, 8, W31])
        YC = sb(m0, "YC", [P, 8, T])
        HS = sb(m0, "HS", [P, 72])
        GLp = sb(m0, "GLp", [P, 2, W31 - 1 + TP])
        XRp = sb(m0, "XRp", [P, 2, W4 - 1 + TP])
        hBA = sb(m0, "hBA", [P, 8])
        hBX = sb(m0, "hBX", [P, 8])
        hla = sb(m0, "hla", [P, 8])
        nhla = sb(m0, "nhla", [P, 8])
        hLNG = sb(m0, "hLNG", [P, 8])
        hLNB = sb(m0, "hLNB", [P, 8])
        spt = sb(m0, "spt", [P, 6, 8])
        GW = sb(m0, "GW", [P, 4, P])
        TS = sb(m0, "TS", [P, 2, 49])
        tmp0 = ExitStack()
        XC = sb(tmp0, "XC", [P, 2, T])
        XP = sb(tmp0, "XP", [P, 2, NS, W4])
        G = sb(tmp0, "G", [P, 2, T])
        G2 = sb(tmp0, "G2", [P, 2, T])
        G3 = sb(tmp0, "G3", [P, 2, T])
        RG = sb(tmp0, "RG", [P, 2, T])
        IG = sb(tmp0, "IG", [P, 2, T])
        AA = sb(tmp0, "AA", [P, 2, T])
        TL = sb(tmp0, "TL", [P, 2, T])
        TB = sb(tmp0, "TB", [P, 2, T])
        GP = sb(tmp0, "GP", [P, 2, NS, W31])
        OH = sb(tmp0, "OH", [72, P])
        OT = sb(tmp0, "OT", [49, 2, P])
        tmp0.close()
        turn = ExitStack()
        crow = sb(turn, "crow", [120, 2, DR])
        drow = sb(turn, "drow", [W31, DR])
        rrow = sb(turn, "rrow", [24, DR])
        turn.close()
        m0.close()
        m1 = ExitStack()
        E = sb(m1, "E", [P, NH, 2, C])
        ES = sb(m1, "ES", [P, NH, ESW])
        AT = sb(m1, "AT", [P, 32])
        WK3 = sb(m1, "WK3", [3 * NS, NH])
        M3 = sb(m1, "M3", [3 * NS, NS])
        R3 = sb(m1, "R3", [3 * NS, 5])
        NSt = sb(m1, "NSt", [P, 64])
        NO = sb(m1, "NO", [P, 72])
        HG = sb(m1, "HG", [P, KT])
        nq = sb(m1, "nq", [P, NS])
        QA = sb(m1, "QA", [P, 2, T])
        KA = sb(m1, "KA", [P, 2, T])
        Qb = sb(m1, "Qb", [P, T])
        Kb = sb(m1, "Kb", [P, T])
        heads = ExitStack()
        VV = sb(heads, "VV", [P, 2, T])
        OG = [sb(heads, f"OG{i}", [P, 2, T]) for i in range(2)]
        KTt = sb(heads, "KTt", [P, 2, C])
        VT = sb(heads, "VT", [P, 2, DV + 1])
        SP = sb(heads, "SP", [P, 2, C])
        C1 = sb(heads, "C1", [P, DV + 1])
        kM = sb(heads, "kM", [3 * NS, 2, DK], F32R)
        KV = sb(heads, "KV", [3 * NS, DK + DV])
        kv3 = sb(heads, "kv3", [3 * NS, DK + DV], F32R)
        Hh = sb(heads, "Hh", [P, 2, T])
        Cs = sb(heads, "Cs", [P, NS, DV])
        heads.close()
        gate = ExitStack()
        rows = sb(gate, "rows", [NH, 8, T])
        rows_hi = sb(gate, "rows_hi", [NH, 2 * T + 2 * C], F32R)
        rows_lo = sb(gate, "rows_lo", [NH, 2 * T + 2 * C], F32R)
        IF = sb(gate, "IF", [2 * NH, T])
        SEL = sb(gate, "SEL", [NH, NH, P], F32R)
        MASK = sb(gate, "MASK", [P, 2, C])
        maskr = sb(gate, "maskr", [P, 2 * C], F32R)
        identr = sb(gate, "identr", [P, P], F32R)
        MO = sb(gate, "MO", [NH, 9])
        mprev = sb(gate, "mprev", [NH, NS])
        bIF = sb(gate, "bIF", [2 * NH, 1])
        W3 = sb(gate, "W3", [NH, 2, 3 * NS])
        m1s = sb(gate, "m1s", [NH, 4])
        nrow = sb(gate, "nrow", [64, P])
        gate.close()
        tail1 = ExitStack()
        OH1 = sb(tail1, "OH1", [72, P])
        tail1.close()
        m1.close()
        mixers.close()
        start = ExitStack()
        xt = sb(start, "xt", [P, 2, D])
        xs = sb(start, "xs", [NS, D])
        prow = sb(start, "prow", [P, 2, P])
        start.close()
        mlp = ExitStack()
        H_hi = sb(mlp, "H_hi", [P, 32, T], F32R)
        H_lo = sb(mlp, "H_lo", [P, 32, T], F32R)
        UT = sb(mlp, "UT", [P, 2, T])
        U = sb(mlp, "U", [P, 2, T])
        mlp.close()
        inputs.close()
        final = ExitStack()
        YO = sb(final, "YO", [P, 2, D])
        YS = sb(final, "YS", [NS, D])
        rt = sb(final, "rt", [P, 3])
        final.close()

        raw_ready = [sem(f"raw_ready{i}") for i in range(RAW)]
        hi_done, lo_dve, lo_pool = sem("hi_done"), sem("lo_dve"), sem("lo_pool")
        pe_block, evac_done = sem("pe_block"), sem("evac_done")
        params_in, x_in, states_in = sem("params_in"), [sem(f"x_in{i}") for i in range(2)], sem("states_in")
        consts, zeroed = sem("consts"), sem("zeroed")
        CONSTS = 7
        OUTS = 17
        par_turned, gain_in, par_ready = sem("par_turned"), sem("gain_in"), sem("par_ready")
        x_turned, x_loaded = sem("x_turned"), sem("x_loaded")
        sq_ready, ssq_added, ssq_ready = sem("sq_ready"), sem("ssq_added"), sem("ssq_ready")
        ssq_zeroed = sem("ssq_zeroed")
        rms_ready, rs_ready = sem("rms_ready"), sem("rs_ready")
        ah_ready, a_ready = sem("ah_ready"), sem("a_ready")
        small = sem("small")
        absl, expl = sem("absl"), sem("expl")
        states_turned, states_ready = sem("states_turned"), sem("states_ready")
        u_ready, hh_ready, h_ready = sem("u_ready"), sem("hh_ready"), sem("h_ready")
        out_done = sem("out_done")

        def two(bank):
            return PS[:, bank:bank + 2, 0:T]

        def over2(ap, n=2):
            return ap[:, None, :].broadcast_to([P, n, ap.shape[1]])

        def load(sp, ph, it, c, w, row, col):
            n, slot = ph.n(it, c), (ph.n0 + c) % RAW
            if not isinstance(n, int) or n >= RAW:
                sp.wait_ge(pe_block, n - RAW + 1)
            src = w[row:row + 4 * P, :].rearrange("(k p) e -> p k e", p=P)[:, :, bass.ds(col, 256)]
            sp.dma_start(raw[:, slot, :].rearrange("p (k e) -> p k e", k=4), src)\
              .then_inc(raw_ready[slot], 16)

        def split_hi(act, ph, it, c):
            n, m = ph.n(it, c) + HI_AHEAD, ph.n0 + c + HI_AHEAD
            if isinstance(n, int) and n >= NB:
                return
            act.wait_ge(raw_ready[m % RAW], 16 * (m // RAW + 1) + it * (16 * (ph.steps // RAW)))
            if not isinstance(n, int) or n >= SPLIT:
                act.wait_ge(pe_block, n - SPLIT + 1)
            nc.scalar.activation(w_hi[:, m % SPLIT, :], raw[:, m % RAW, :], ACT.Copy)\
              .then_inc(hi_done, 1)

        def split_lo(eng, who, ph, it, c):
            t = c + LO_AHEAD
            if ph.splitter(t) != who:
                return
            n, m = ph.n(it, c) + LO_AHEAD, ph.n0 + t
            if isinstance(n, int) and n >= NB:
                return
            eng.wait_ge(hi_done, n + 1)
            if not isinstance(n, int) or n >= SPLIT:
                eng.wait_ge(pe_block, n - SPLIT + 1)
            eng.tensor_tensor(w_lo[:, m % SPLIT, :], raw[:, m % RAW, :],
                              w_hi[:, m % SPLIT, :].bitcast(F32), ALU.subtract)\
               .then_inc(lo_dve if who == "D" else lo_pool, 1)

        def wait_split(pe, ph, it, c):
            who = ph.lo[c]
            done = ph.lo[:c + 1].count(who) + (ph.d0 if who == "D" else ph.p0)
            pe.wait_ge(lo_dve if who == "D" else lo_pool, done + it * ph.lo.count(who))

        def multiply(pe, ph, it, c, group, hi, lo, k0, first, last):
            wait_split(pe, ph, it, c)
            slot, bank = (ph.n0 + c) % SPLIT, 2 * ((ph.g0 + group) % 2)
            if first and not (isinstance(ph.g(it, group), int) and ph.g(it, group) < 2):
                pe.wait_ge(evac_done, ph.g(it, group) - 1)
            for k in range(4):
                for m in range(2):
                    w = slice(256 * k + P * m, 256 * k + P * m + P)
                    out = PS[:, bank + m, 0:T]
                    nc.tensor.matmul(out, w_hi[:, slot, w], hi[:, k0 + k, :], start=first and k == 0, stop=False)
                    nc.tensor.matmul(out, w_hi[:, slot, w], lo[:, k0 + k, :], start=False, stop=False)
                    mm = nc.tensor.matmul(out, w_lo[:, slot, w], hi[:, k0 + k, :], start=False,
                                          stop=last and k == 3)
            mm.then_inc(pe_block, 1)

        def group_bank(ph, j):
            return 2 * ((ph.g0 + j) % 2)

        def square_and_gain(act, e, p, gain):
            idx = p + 8 * e
            if not (isinstance(idx, int) and idx == 0):
                act.wait_ge(ssq_added, idx)
            nc.scalar.activation(SQ[:, :, :], X[:, bass.ds(2 * p, 2), :], ACT.Square).then_inc(sq_ready, 1)
            if gain is not None:
                for m in range(2):
                    q = nc.scalar.activation(A_hi[:, bass.ds(2 * p + m, 1), :], X[:, bass.ds(2 * p + m, 1), :],
                                             ACT.Copy, scale=par[:, bass.ds(2 * p + (gain + m), 1)])
                q.then_inc(ah_ready, 1)

        def gain_lo(dve, e, p, gain):
            dve.wait_ge(ah_ready, p + (8 * e + 1))
            for m in range(2):
                k = bass.ds(2 * p + m, 1)
                q = nc.vector.scalar_tensor_tensor(A_lo[:, k, :], X[:, k, :], par[:, bass.ds(2 * p + (gain + m), 1)],
                                                   A_hi[:, k, :].bitcast(F32), ALU.mult, ALU.subtract)
            q.then_inc(a_ready, 1)

        def add_squares(pool, e, p):
            pool.wait_ge(sq_ready, p + (8 * e + 1))
            pool.wait_ge(ssq_zeroed, e + 1)
            if not isinstance(p, int) or 8 * e + p > 0:
                pool.wait_ge(ssq_added, p + 8 * e)
            nc.gpsimd.tensor_tensor(ssq[:, :, :], ssq[:, :, :], SQ[:, :, :], ALU.add).then_inc(ssq_added, 1)

        def zero_squares(pool, e):
            if e:
                pool.wait_ge(ssq_ready, e)
            nc.gpsimd.memset(ssq[:, :, :], 0.0).then_inc(ssq_zeroed, 1)

        def sum_squares(pe, e):
            pe.wait_ge(ssq_added, 8 * (e + 1))
            nc.tensor.matmul(PS[:, 7, 0:T], ones[:, :], ssq[:, 0, :], start=True, stop=False)
            nc.tensor.matmul(PS[:, 7, 0:T], ones[:, :], ssq[:, 1, :], start=False, stop=True).then_inc(ssq_ready, 1)

        def root(act, e):
            act.wait_ge(ssq_ready, e + 1)
            if e:
                act.wait_ge(rs_ready, e)
            nc.scalar.activation(RMS[:, :], PS[:, 7, 0:T], ACT.Sqrt, scale=1.0 / D, bias=eps[:, :])\
              .then_inc(rms_ready, 1)

        def invert(dve, e):
            dve.wait_ge(rms_ready, e + 1)
            nc.vector.reciprocal(RS[:, :], RMS[:, :]).then_inc(rs_ready, 1)
            dve.wait_ge(rs_ready, e + 1)

        def turns(eng, ph, body, peel=0, tail=0):
            for it in range(peel):
                body(it)
            if ph.iters > peel + tail:
                with eng.Fori(peel, ph.iters - tail) as it:
                    body(it)
            for it in range(ph.iters - tail, ph.iters):
                body(it)

        xc_tap, xs_step, xc_ready = sem("xc_tap"), sem("xs_step"), sem("xc_ready")
        gw_in, gates_ready, gates_read, al_ready = sem("gw_in"), sem("gates_ready"), sem("gates_read"), sem("al_ready")
        w_step, w_ready, t_ready, root_ready = sem("w_step"), sem("w_ready"), sem("t_ready"), sem("root_ready")
        u0_ready, h0_step, h0_ready = sem("u0_ready"), sem("h0_step"), sem("h0_ready")
        g2_ready, g3_step, g3_ready, gth_ready = sem("g2_ready"), sem("g3_step"), sem("g3_ready"), sem("gth_ready")
        gl_step, y_ready, bh_ready, b_ready = sem("gl_step"), sem("y_ready"), sem("bh_ready"), sem("b_ready")
        tb_ready, gl_ready, tap_done = sem("tb_ready"), sem("gl_ready"), sem("tap_done")
        cs_step, yc_ready = sem("cs_step"), sem("yc_ready")
        tsx_ready, tsg_ready, hs_ready = sem("tsx_ready"), sem("tsg_ready"), sem("hs_ready")
        ts_turned, ot_ready, ot_out = sem("ts_turned"), sem("ot_ready"), sem("ot_out")
        hs_turned, oh_ready = sem("hs_turned"), sem("oh_ready")
        ln_zeroed, ln_added, mu_ready, mu_copied = sem("ln_zeroed"), sem("ln_added"), sem("mu_ready"), sem("mu_copied")
        yd_ready, lsq_ready, var_ready, dev_ready = sem("yd_ready"), sem("lsq_ready"), sem("var_ready"), sem("dev_ready")
        rv_ready, yn_ready, lth_ready = sem("rv_ready"), sem("yn_ready"), sem("lth_ready")
        z_step, z_ready = sem("z_step"), sem("z_ready")
        fin_ready, fin_turned, fin_copied = sem("fin_ready"), sem("fin_turned"), sem("fin_copied")
        rt_ready, rt_inv, ya_scaled, yd_scaled = sem("rt_ready"), sem("rt_inv"), sem("ya_scaled"), sem("yd_scaled")
        lam_ready = sem("lam_ready")

        in0, out0a, out0b = PH["in0"], PH["out0a"], PH["out0b"]
        w31f = w31[:, :, :].rearrange("p j w -> p (j w)")
        H0v = par[:, H0:H0 + 64].rearrange("p (b j) -> p j b", j=8)
        CWv = par[:, CW:CW + 32].rearrange("p (w j) -> p j w", j=8)
        HSv = HS[:, 0:64].rearrange("p (b j) -> p j b", j=8)
        IN0_COLS = [0, DR, 3 * DR, 2 * DR]
        Zb, Tb = [XC, AA, TL, RG], [G2, G3, TB, IG]
        PARAM_ROWS = [("ml_norm", 0, MLN, 16), ("mlp_norm", 0, MPN, 32),
                      ("final_norm", 0, FIN, 16), ("ml_hnorm_g", 0, HNG, 16), ("rglru_conv_b", 0, CB, 8),
                      ("rglru_ba", 0, BA, 8), ("rglru_bx", 0, BX, 8), ("rglru_lambda", 0, LAM, 8),
                      ("conf_dw_b", 1, DWB, 8), ("conf_ln_g", 1, LNG, 8), ("conf_ln_b", 1, LNB, 8),
                      ("state_rglru_h", 1, H0, 64), ("rglru_conv_w", 1, CW, 32)]

        gate_in, gate_i, gate_s = sem("gate_in"), sem("gate_i"), sem("gate_s")
        gate_f, gate_e, gate_m, gate_x, gate_y = sem("gate_f"), sem("gate_e"), sem("gate_m"), sem("gate_x"), sem("gate_y")
        masks, at_turned, at_ready = sem("masks"), sem("at_turned"), sem("at_ready")
        bc_made, bc_copied, e_ready = sem("bc_made"), sem("bc_copied"), sem("e_ready")
        qb_copied, og_ready, hp_turned, kt_ready = sem("qb_copied"), sem("og_ready"), sem("hp_turned"), sem("kt_ready")
        sp_ready, c1_made, c1_copied, qsc_ready = sem("sp_ready"), sem("c1_made"), sem("c1_copied"), sem("qsc_ready")
        c2_made, c2_ready, nn_ready, pc_out = sem("c2_made"), sem("c2_ready"), sem("nn_ready"), sem("pc_out")
        ns_step, nq_ready = sem("ns_step"), sem("nq_ready")
        km_ready, outer_made, cs_upd = sem("km_ready"), sem("outer_made"), sem("cs_upd")
        cs_in, cs_out = [sem(f"cs_in{i}") for i in range(2)], [sem(f"cs_out{i}") for i in range(2)]
        nums_made, rd_step, hn_ready, sqh_ready = sem("nums_made"), sem("rd_step"), sem("hn_ready"), sem("sqh_ready")
        hss_made, rm_ready, rn_ready, ogs_ready = sem("hss_made"), sem("rm_ready"), sem("rn_ready"), sem("ogs_ready")
        yy_ready, bh1_ready, b1_ready = sem("yy_ready"), sem("bh1_ready"), sem("b1_ready")
        kvh_ready, kvs_ready, kv3_ready, r3_step = sem("kvh_ready"), sem("kvs_ready"), sem("kv3_ready"), sem("r3_step")
        s3_ready, w3_ready, rows_high, rows_split = sem("s3_ready"), sem("w3_ready"), sem("rows_high"), sem("rows_split")
        no_turned, oh1_ready = sem("no_turned"), sem("oh1_ready")

        gif, in1, out1a, out1b = (PH.get(n) for n in ("gif", "in1", "out1a", "out1b"))
        VQ, VK, VV0, VO, VG = 0, NH * DK, 2 * NH * DK, 2 * NH * DK + NH * DV, 2 * NH * DK + 2 * NH * DV
        IN1_COLS = [(VQ, 2 * DK), (VK, 2 * DK), (VV0, 2 * DV), (VV0 + DV, 2 * DV), (VO, 2 * DV), (VO + DV, 2 * DV)]
        GF, GE, GZ, GY, GL, GEM, GSC, GNM = range(8)
        GM, GB, GA, GW1, GT = GF, GE, GZ, GY, GL
        rows_x = rows[:, GEM:GNM + 1, :].rearrange("p r t -> p (r t)")
        ROW_PARTS = [slice(0, ESW), slice(2 * T, 2 * T + 2 * C)]
        ESf = ES[:, :, :].rearrange("p h f -> p (h f)")
        Ef = E[:, :, :, :].rearrange("p h c t -> p (h c t)")
        SPf = SP[:, :, :].rearrange("p c t -> p (c t)")
        NOv = NO[:, 0:64].rearrange("p (b h) -> p b h", b=NS)
        NStv = NSt[:, :].rearrange("p (b h) -> p b h", b=NS)
        id8 = ident[0:NS, 0:NS]

        S3 = SQ[:, 0, 0:72]
        def thrice(ap):
            return ap[:, None, :].broadcast_to([ap.shape[0], 3, NS])

        def as3(ap):
            return ap.rearrange("p (r s) -> p r s", r=3)

        def after(eng, s, value):
            if not (isinstance(value, int) and value <= 0):
                eng.wait_ge(s, value)

        def decays(k, first, n):
            return ESf[:, bass.ds(k * ESW + (T + first), n)]

        def head_steps(body, it, c):
            if c >= 12:
                body(c - 12, 2 * it, QA[:, 0, :], KA[:, 0, :], OG[0])
            elif not (isinstance(it, int) and it == 0):
                body(c, 2 * it - 1, Qb, Kb, OG[1])

        def load_mixer1(sp):
            w_in, w_out = I["ml_w_in"][0], I["ml_w_out"][0]
            for c in range(2):
                n, slot = gif.n(0, c), (gif.n0 + c) % RAW
                sp.wait_ge(pe_block, n - RAW + 1)
                src = w_in[1024 * c:1024 * c + 1024, VG:VG + 2 * NH].rearrange("(k p) e -> p k e", p=P)
                sp.dma_start(raw[:, slot, :].rearrange("p (k e) -> p k e", k=8)[:, :, 0:2 * NH], src)\
                  .then_inc(raw_ready[slot], 16)
            def load_in1(it):
                for c in range(24):
                    base, step = IN1_COLS[c // 4]
                    load(sp, in1, it, c, w_in, 512 * (c % 4), step * it + base)
            turns(sp, in1, load_in1)
            for c in range(24):
                load(sp, out1a, 0, c, w_out, 512 * (c % 3), 256 * (c // 3))
            for c in range(8):
                load(sp, out1b, 0, c, w_out, 1536, 256 * c)

        def pe_mixer1(pe):
            for c in range(2):
                pe.wait_ge(a_ready, 16 + 4 * (c + 1))
                wait_split(pe, gif, 0, c)
                slot, bank = (gif.n0 + c) % SPLIT, group_bank(gif, 0)
                if c == 0:
                    pe.wait_ge(evac_done, gif.g(0, 0) - 1)
                out = PS[0:2 * NH, bank, 0:T]
                for k in range(8):
                    w = slice(P * k, P * k + 2 * NH)
                    x = 8 * c + k
                    nc.tensor.matmul(out, w_hi[:, slot, w], A_hi[:, x, :], start=x == 0, stop=False)
                    nc.tensor.matmul(out, w_hi[:, slot, w], A_lo[:, x, :], start=False, stop=False)
                    mm = nc.tensor.matmul(out, w_lo[:, slot, w], A_hi[:, x, :], start=False, stop=x == 15)
                mm.then_inc(pe_block, 1)
            sum_squares(pe, 2)

            def gates(c):
                if c == 0:
                    pe.wait_ge(gate_i, 1)
                    nc.tensor.matmul(PS[0:NH, 5, 0:T], ident[0:2 * NH, NH:2 * NH], IF[:, :], start=True, stop=True).then_inc(gate_s, 1)
                if c == 6:
                    pe.wait_ge(w3_ready, 1)
                    for i in range(2):
                        nc.tensor.transpose(PS[:, 4, 8 * i:8 * i + 8], rows[:, GA, C * i:C * i + C], id8)
                        nc.tensor.transpose(PS[:, 4, 16 + 8 * i:24 + 8 * i], rows[:, GW1, C * i:C * i + C], id8)
                    nc.tensor.matmul(PS[0:3 * NS, 4, 32:40], W3[:, 0, :], id8, start=True, stop=True)
                    nc.tensor.matmul(PS[0:3 * NS, 4, 40:48], W3[:, 1, :], id8, start=True, stop=True)
                    nc.tensor.transpose(PS[:, 4, 64:128], nrow[:, :], ident[0:64, 0:64]).then_inc(at_turned, 1)
                if 7 <= c <= 10:
                    pe.wait_ge(masks, 5)
                    pe.wait_ge(rows_split, 1)
                    if c == 7:
                        pe.wait_ge(rms_ready, 3)
                        pe.wait_ge(at_ready, 1)
                    else:
                        pe.wait_ge(bc_copied, c - 7)
                        pe.wait_ge(e_ready, c - 7)
                    for x in range(2):
                        h = 2 * (c - 7) + x
                        for i, r in enumerate((rows_hi, rows_lo)):
                            nc.tensor.matmul(PS[:, 4 + x, 0:ESW], SEL[:, h, :], r[:, 0:ESW], start=i == 0, stop=i == 1)
                            nc.tensor.matmul(PS[:, 6 + x, 0:2 * C], SEL[:, h, :], r[:, 2 * T:2 * T + 2 * C], start=i == 0, stop=False)
                        mm = nc.tensor.matmul(PS[:, 6 + x, 0:2 * C], identr[:, :], maskr[:, :], start=False, stop=True)
                    mm.then_inc(bc_made, 1)

            def head(t, k, Q, K, og):
                if t == 0:
                    if isinstance(k, int) and k == 0:
                        pe.wait_ge(r3_step, 5)
                        pe.wait_ge(bc_copied, 4)
                        pe.wait_ge(e_ready, 4)
                        pe.wait_ge(evac_done, in1.g(0, 2) + 1)
                    else:
                        pe.wait_ge(cs_upd, k * 4)
                        pe.wait_ge(rm_ready, k)
                        pe.wait_ge(hn_ready, k)
                        pe.wait_ge(evac_done, in1.g0 + 3 + 3 * k)
                    pe.wait_ge(s3_ready, k + 1)
                    for i in range(2):
                        s = slice(C * i, C * i + C)
                        nc.tensor.transpose(PS[:, 4, s], K[:, s], ident[:, :])
                        for m in range(2):
                            nc.tensor.transpose(PS[:, 7, DV * i + P * m:DV * i + P * m + P], VV[:, m, s], ident[:, :])
                        nc.tensor.matmul(PS[:, 6, s], K[:, s], Q[:, s], start=True, stop=True)
                    for m in range(3):
                        tr = nc.tensor.transpose(PS[0:3 * NS, 5, P * m:P * m + P], S3[:, 24 * m:24 * m + 24], ident[:, :])
                    tr.then_inc(hp_turned, 1)
                if t == 1:
                    pe.wait_ge(kt_ready, k + 1)
                    nc.tensor.matmul(PS[:, 4, 0:DV + 1], KTt[:, 0, :], VT[:, 0, :], start=True, stop=True).then_inc(c1_made, 1)
                    pe.wait_ge(sp_ready, k + 1)
                    for m in range(2):
                        nc.tensor.matmul(PS[:, 6 + m, 0:C], VT[:, 0, P * m:P * m + P], SP[:, 0, :], start=True, stop=True)
                    nc.tensor.matmul(PS[:, 5, 0:C], ones[:, :], SP[:, 0, :], start=True, stop=True)
                if t == 2:
                    pe.wait_ge(qsc_ready, k + 1)
                    pe.wait_ge(c1_copied, k + 1)
                    for m in range(2):
                        v = slice(P * m, P * m + P)
                        nc.tensor.matmul(PS[:, 6 + m, C:2 * C], VT[:, 1, v], SP[:, 1, :], start=True, stop=False)
                        nc.tensor.matmul(PS[:, 6 + m, C:2 * C], C1[:, v], Q[:, C:2 * C], start=False, stop=True)
                    nc.tensor.matmul(PS[:, 5, C:2 * C], ones[:, :], SP[:, 1, :], start=True, stop=False)
                    nc.tensor.matmul(PS[:, 5, C:2 * C], C1[:, DV:DV + 1].broadcast_to([P, P]), Q[:, C:2 * C], start=False, stop=True)
                    nc.tensor.matmul(PS[:, 4, 0:DV + 1], KTt[:, 1, :], VT[:, 1, :], start=True, stop=True).then_inc(c2_made, 1)
                if 4 <= t <= 7:
                    r = t - 4
                    pe.wait_ge(cs_upd, k * 4 + (r + 1))
                    for b in (2 * r, 2 * r + 1):
                        for m in range(2):
                            mm = nc.tensor.matmul(PS[:, 6 + m, TP + b:TP + b + 1], Cs[:, b, P * m:P * m + P], Q[:, TP + b:TP + b + 1],
                                                  start=True, stop=True)
                    if t == 7:
                        pe.wait_ge(nq_ready, k + 1)
                        nc.tensor.matmul(PS[:, 5, TP:T], ones[:, :], nq[:, :], start=True, stop=True).then_inc(nums_made, 1)
                if 3 <= t <= 6:
                    r = t - 3
                    pe.wait_ge(km_ready, k * 4 + (r + 1))
                    if r == 0:
                        pe.wait_ge(c2_ready, k + 1)
                    for x in range(2):
                        mm = nc.tensor.matmul(PS[:, 4, DV * x:DV * x + DV], kM[:, x, :], kv3[:, DK:DK + DV], start=True, stop=True)
                    mm.then_inc(outer_made, 1)
                if t == 9:
                    pe.wait_ge(sqh_ready, k + 1)
                    nc.tensor.matmul(PS[:, 5, 0:T], ones[:, :], SQ[:, 0, :], start=True, stop=False)
                    nc.tensor.matmul(PS[:, 5, 0:T], ones[:, :], SQ[:, 1, :], start=False, stop=True).then_inc(hss_made, 1)

            def mul_in1(it):
                for c in range(24):
                    multiply(pe, in1, it, c, c // 4, A_hi, A_lo, 4 * (c % 4), c % 4 == 0, c % 4 == 3)
                    if isinstance(it, int) and it == 0:
                        gates(c)
                    head_steps(head, it, c)
            turns(pe, in1, mul_in1, peel=1)
            for c in range(24):
                pe.wait_ge(b1_ready, 2 * (c % 3) + 2)
                multiply(pe, out1a, 0, c, c // 3, B_hi, B_lo, 4 * (c % 3), c % 3 == 0, c % 3 == 2)
                if c < 12:
                    head(c, NH - 1, Qb, Kb, OG[1])
                if c == 14:
                    pe.wait_ge(cs_upd, 4 * NH)
                    pe.wait_ge(nn_ready, NH)
                    pe.wait_ge(nq_ready, NH)
                    nc.tensor.transpose(PS[0:72, 4, 0:P], NO[:, :], ident[:, :]).then_inc(no_turned, 1)
            pe.wait_ge(b1_ready, NH)
            for c in range(8):
                multiply(pe, out1b, 0, c, c, B_hi, B_lo, 12, True, True)

        def act_mixer1(act):
            for c in range(2):
                split_hi(act, gif, 0, c)
                if c == 0:
                    act.wait_ge(pe_block, gif.n(0, 0))
                    act.wait_ge(ot_out, 64 * 4)
                    act.wait_ge(out_done, 16 * 4)
                    act.dma_start(bIF[:, :], I["ml_b_if"][0].rearrange("(h o) -> h o", o=1)).then_inc(gate_in, 16)
                    act.dma_start(mprev[:, :], I["state_mlstm_m"][0].rearrange("b h -> h b"), allow_slow_non_contiguous=True).then_inc(gate_in, 16)
                    act.dma_start(nrow[:, :], I["state_mlstm_n"][0].rearrange("b h d -> (b h) d")).then_inc(gate_in, 16)
            root(act, 2)

            def gates(c):
                if c == 0:
                    act.wait_ge(gate_f, 1)
                    nc.scalar.activation(rows[:, GY, :], rows[:, GF, :], ACT.Abs).then_inc(gate_y, 1)
                    act.wait_ge(gate_y, 1)
                    nc.scalar.activation(rows[:, GE, :], rows[:, GY, :], ACT.Exp, scale=-1.0).then_inc(gate_e, 1)
                if c == 5:
                    act.wait_ge(gate_m, 1)
                    for i in range(2):
                        last = rows[:, GNM, C * i + C - 1:C * i + C]
                        nc.scalar.activation(rows[:, GW1, C * i:C * i + C], rows[:, GA, C * i:C * i + C], ACT.Exp, bias=last)\
                          .then_inc(gate_x if i else gate_e, 1)
                    nc.scalar.activation(rows[:, GSC, 0:C], rows[:, GNM, C:2 * C], ACT.Exp, bias=m1s[:, 0:1])
                    nc.scalar.activation(rows[:, GSC, C:C + 2 * NS], rows[:, GSC, C:C + 2 * NS], ACT.Exp).then_inc(gate_x, 1)
                    nc.scalar.activation(rows[:, GEM, :], rows[:, GT, :], ACT.Exp, scale=-1.0).then_inc(gate_x, 1)
                    act.wait_ge(gate_x, 3)
                    nc.scalar.copy(as3(W3[:, 0, :]), thrice(rows[:, GSC, 136:144]))
                    nc.scalar.copy(as3(W3[:, 1, :]), thrice(id8)).then_inc(w3_ready, 1)
                    for part in ROW_PARTS:
                        cp = nc.scalar.activation(rows_hi[:, part], rows_x[:, part], ACT.Copy)
                    cp.then_inc(rows_high, 1)
                    act.dma_start(O["p_m"][0, 0, :].rearrange("(h o) -> h o", o=1), MO[:, 0:1]).then_inc(out_done, 16)
                    act.dma_start(O["s_m"][0].rearrange("b h -> h b"), MO[:, 1:1 + NS], allow_slow_non_contiguous=True).then_inc(out_done, 16)
                if c == 7:
                    act.wait_ge(at_turned, 1)
                    nc.scalar.copy(AT[:, :], PS[:, 4, 0:32])
                    nc.scalar.copy(WK3[:, :], PS[0:3 * NS, 4, 32:40])
                    nc.scalar.copy(M3[:, :], PS[0:3 * NS, 4, 40:48])
                    nc.scalar.copy(NSt[:, :], PS[:, 4, 64:128]).then_inc(at_ready, 1)
                    act.wait_ge(at_ready, 1)
                if 8 <= c <= 11:
                    act.wait_ge(bc_made, c - 7)
                    for x in range(2):
                        h = 2 * (c - 8) + x
                        for i in range(2):
                            ex = nc.scalar.activation(E[:, h, i, :], PS[:, 6 + x, C * i:C * i + C], ACT.Exp,
                                                      bias=AT[:, NH * i + h:NH * i + h + 1])
                    ex.then_inc(e_ready, 1)
                if c == 11:
                    act.wait_ge(out_done, 16 * 6)
                    for half in range(2):
                        load_memory(0, half)

            def memory(ap, k, half):
                return ap.rearrange("b h d v -> h d b v")[bass.ds(k, 1), :, 4 * half:4 * half + 4, :].rearrange("h d b v -> (h d) b v")

            def load_memory(k, half):
                act.dma_start(Cs[:, 4 * half:4 * half + 4, :], memory(I["state_mlstm_C"][0], k, half)).then_inc(cs_in[half], 16)

            def sample_columns(t, k, Q, K, og):
                if t == 0:
                    if isinstance(k, int) and k == 0:
                        act.wait_ge(evac_done, in1.g(0, 2) + 1)
                        act.wait_ge(ssq_added, 24)
                    else:
                        act.wait_ge(evac_done, in1.g0 + 3 + 3 * k)
                    nc.scalar.copy(as3(S3[:, 0:24]), thrice(K[:, TP:T]))
                    for m in range(2):
                        cp = nc.scalar.copy(as3(S3[:, 24 * m + 24:24 * m + 48]), thrice(VV[:, m, TP:T]))
                    cp.then_inc(s3_ready, 1)

            def gate_of(it, i):
                act.wait_ge(evac_done, in1.g(it, 4 + i) + 1)
                nc.scalar.activation(OG[i][:, :, :], OG[i][:, :, :], ACT.Tanh, scale=0.5).then_inc(og_ready, 1)

            def head(t, k, Q, K, og):
                last = isinstance(k, int) and k == NH - 1
                if t == 0:
                    act.wait_ge(hp_turned, k + 1)
                    after(act, c2_made, k)
                    for i in range(2):
                        nc.scalar.activation(KTt[:, i, :], PS[:, 4, C * i:C * i + C], ACT.Copy,
                                             scale=AT[:, bass.ds(k + (16 + NH * i), 1)])
                    nc.scalar.copy(VT[:, :, 0:DV], PS[:, 7, :].rearrange("p (c v) -> p c v", c=2)).then_inc(kt_ready, 1)
                    act.wait_ge(sp_ready, k + 1)
                    after(act, outer_made, k * 4)
                    nc.scalar.activation(kv3[:, :], KV[:, :], ACT.Copy).then_inc(kvh_ready, 1)
                    act.wait_ge(kvh_ready, k + 1)
                    nc.scalar.activation(kv3[:, 0:DK], kv3[:, 0:DK].bitcast(F32), ACT.Copy, scale=R3[:, 2:3])
                    nc.scalar.activation(kv3[:, DK:DK + DV], kv3[:, DK:DK + DV].bitcast(F32), ACT.Copy, scale=R3[:, 3:4]).then_inc(kvs_ready, 1)
                if t == 1:
                    act.wait_ge(c1_made, k + 1)
                    after(act, pc_out, k * 16)
                    after(act, nn_ready, k)
                    nc.scalar.copy(C1[:, :], PS[:, 4, 0:DV + 1]).then_inc(c1_copied, 1)
                if t == 2:
                    act.wait_ge(c2_ready, k + 1)
                    act.dma_start(O["p_C"][0, 0, bass.ds(k, 1), :, :].rearrange("h d v -> (h d) v"), C1[:, 0:DV]).then_inc(pc_out, 16)
                if t in (5, 7):
                    half = (t - 5) // 2
                    act.wait_ge(cs_upd, k * 4 + (2 * half + 2))
                    act.dma_start(memory(O["s_C"][0], k, half), Cs[:, 4 * half:4 * half + 4, :]).then_inc(cs_out[half], 16)
                if t == 8:
                    act.wait_ge(hn_ready, k + 1)
                    if isinstance(k, int) and k == 0:
                        act.wait_ge(ssq_added, 24)
                    nc.scalar.activation(SQ[:, :, :], Hh[:, :, :], ACT.Square).then_inc(sqh_ready, 1)
                if t in (8, 10) and not last:
                    half = (t - 8) // 2
                    act.wait_ge(nums_made, k + 1)
                    act.wait_ge(cs_out[half], k * 16 + 16)
                    load_memory(k + 1, half)
                if t == 9:
                    act.wait_ge(hss_made, k + 1)
                    nc.scalar.activation(RMS[:, :], PS[:, 5, 0:T], ACT.Sqrt, scale=1.0 / DV, bias=eps[:, :]).then_inc(rm_ready, 1)
                if t == 10:
                    act.wait_ge(yy_ready, k + 1)
                    for m in range(2):
                        cp = nc.scalar.activation(B_hi[:, bass.ds(2 * k + m, 1), :], Hh[:, m:m + 1, :], ACT.Copy,
                                                  scale=HG[:, bass.ds(2 * k + m, 1)])
                    cp.then_inc(bh1_ready, 1)

            def act_in1(it):
                for c in range(24):
                    head_steps(sample_columns, it, c)
                    split_hi(act, in1, it, c)
                    if isinstance(it, int) and it == 0:
                        gates(c)
                    head_steps(head, it, c)
                    if c == 20:
                        gate_of(it, 0)
                    if c == 1 and not (isinstance(it, int) and it == 0):
                        gate_of(it - 1, 1)
            turns(act, in1, act_in1, peel=1)
            for c in range(24):
                if c == 0:
                    sample_columns(0, NH - 1, Qb, Kb, OG[1])
                split_hi(act, out1a, 0, c)
                if c < 12:
                    head(c, NH - 1, Qb, Kb, OG[1])
                if c == 1:
                    gate_of(3, 1)
                if c == 15:
                    act.wait_ge(no_turned, 1)
                    nc.scalar.copy(OH1[:, :], PS[0:72, 4, 0:P]).then_inc(oh1_ready, 1)
                    act.wait_ge(oh1_ready, 1)
                    act.dma_start(O["s_n"][0].rearrange("b h d -> (b h) d"), OH1[0:64, :]).then_inc(out_done, 16)
                    act.dma_start(O["p_n"][0, 0], OH1[64:72, :]).then_inc(out_done, 16)
            for c in range(8):
                split_hi(act, out1b, 0, c)
                act.wait_ge(evac_done, out1b.g(0, c) + 1)
                square_and_gain(act, 3, c, MPN + KT)
            wait_outputs1(act)

        def wait_outputs1(eng):
            eng.wait_ge(pc_out, 16 * NH)
            for half in range(2):
                eng.wait_ge(cs_out[half], 16 * NH)
            eng.wait_ge(out_done, 16 * 8)

        def pool_mixer1(pool):
            pool.wait_ge(pe_block, gif.n(0, 0))
            pool.wait_ge(ot_out, 64 * 4)
            pool.wait_ge(out_done, 16 * 4)
            nc.gpsimd.memset(MASK[:, :, :], 0.0).then_inc(masks, 1)
            nc.gpsimd.tensor_copy(SEL[:, :, :], ident[0:NH, 0:NH][:, :, None].broadcast_to([NH, NH, P])).then_inc(masks, 1)
            pool.wait_ge(masks, 2)
            nc.gpsimd.affine_select(out=MASK[:, :, :], in_=MASK[:, :, :], compare_op=ALU.is_ge, fill=-1e30, base=0,
                                    pattern=[[0, 2], [1, C]], channel_multiplier=-1).then_inc(masks, 1)
            nc.gpsimd.tensor_copy(identr[:, :], ident[:, :]).then_inc(masks, 1)
            pool.wait_ge(masks, 4)
            nc.gpsimd.tensor_copy(maskr[:, :], MASK[:, :, :].rearrange("p c t -> p (c t)")).then_inc(masks, 1)
            nc.gpsimd.memset(R3[:, :], 1.0).then_inc(r3_step, 1)
            pool.wait_ge(r3_step, 1)
            for col, first in ((0, 2 * NS), (4, NS)):
                nc.gpsimd.affine_select(out=R3[:, col:col + 1], in_=R3[:, col:col + 1], compare_op=ALU.is_ge, fill=0.0,
                                        base=-first, pattern=[[0, 1]], channel_multiplier=1).then_inc(r3_step, 1)
            pool.wait_ge(r3_step, 3)
            nc.gpsimd.tensor_tensor(R3[:, 1:2], R3[:, 4:5], R3[:, 0:1], ALU.subtract).then_inc(r3_step, 1)
            pool.wait_ge(r3_step, 4)
            nc.gpsimd.tensor_scalar(R3[:, 2:4], R3[:, 0:2], 2.0, -1.0, ALU.mult, ALU.add).then_inc(r3_step, 1)

            def pool_in1(it):
                for c in range(24):
                    if c == 12:
                        pool.wait_ge(evac_done, in1.g(it, 1) + 1)
                        if not (isinstance(it, int) and it == 0):
                            pool.wait_ge(nums_made, 2 * it)
                    split_lo(pool, "P", in1, it, c)
                    if c == 12:
                        nc.gpsimd.tensor_copy(Qb[:, :], QA[:, 1, :])
                        nc.gpsimd.tensor_copy(Kb[:, :], KA[:, 1, :]).then_inc(qb_copied, 1)
            turns(pool, in1, pool_in1, peel=1)
            for c in range(24):
                split_lo(pool, "P", out1a, 0, c)
            pool.wait_ge(b1_ready, NH)
            zero_squares(pool, 3)
            for c in range(8):
                split_lo(pool, "P", out1b, 0, c)
                add_squares(pool, 3, c)

        def dve_mixer1(dve, link, log1p_terms):
            V = nc.vector
            row = lambda r, a=0, b=T: rows[:, r, a:b]
            for c in range(2):
                split_lo(dve, "D", gif, 0, c)
            V.tensor_scalar(HG[:, :], par[:, HNG:HNG + KT], 0.5, None, ALU.mult)
            invert(dve, 2)
            dve.wait_ge(pe_block, gif.n(0, 2))
            dve.wait_ge(gate_in, 48)
            bank = group_bank(gif, 0)
            V.tensor_tensor(IF[:, :], PS[0:2 * NH, bank, 0:T], RS[0:2 * NH, :], ALU.mult).then_inc(evac_done, 1)
            dve.wait_ge(evac_done, gif.g(0, 1))
            V.tensor_scalar(IF[:, :], IF[:, :], bIF[:, :], None, ALU.add).then_inc(gate_i, 1)

            def gates(c):
                if c in (0, 1, 2):
                    if c == 0:
                        dve.wait_ge(gate_s, 1)
                        V.tensor_copy(row(GF), PS[0:NH, 5, 0:T]).then_inc(gate_f, 1)
                        dve.wait_ge(gate_e, 1)
                    log1p_terms(c, row(GE), row(GZ), row(GY), row(GL))
                if c == 2:
                    link(V.tensor_scalar(row(GY), row(GF), 0.0, None, ALU.min))
                    link(V.scalar_tensor_tensor(row(GL), row(GL), -2.0, row(GY), ALU.mult, ALU.add))
                if c == 3:
                    for i in range(2):
                        s = (C * i, C * i + C)
                        V.tensor_tensor_scan(row(GB, *s), ones[0:NH, :], row(GL, *s), 0.0, ALU.mult, ALU.add)
                    link(V.tensor_copy(row(GB, TP, T), row(GL, TP, T)))
                    link(V.tensor_tensor(row(GA), IF[0:NH, :], row(GB), ALU.subtract))
                if c == 4:
                    link(V.tensor_tensor_scan(row(GM, 0, C), ones[0:NH, :], row(GA, 0, C), 0.0, ALU.mult, ALU.max))
                    link(V.tensor_tensor(m1s[:, 0:1], row(GB, C - 1, C), row(GM, C - 1, C), ALU.add))
                    link(V.tensor_tensor_scan(row(GM, C, TP), ones[0:NH, :], row(GA, C, TP), m1s[:, 0:1], ALU.mult, ALU.max))
                    link(V.tensor_tensor(row(GM, TP, T), row(GA, TP, T), mprev[:, :], ALU.max))
                    V.tensor_tensor(row(GT), row(GB), row(GM), ALU.add)
                    V.tensor_scalar(row(GNM), row(GM), -1.0, None, ALU.mult)
                    V.tensor_tensor(row(GSC, C, C + NS), mprev[:, :], row(GM, TP, T), ALU.subtract)
                    link(V.tensor_tensor(row(GSC, C + NS, C + 2 * NS), row(GA, TP, T), row(GM, TP, T), ALU.subtract))
                    V.tensor_copy(MO[:, 0:1], row(GT, TP - 1, TP))
                    V.tensor_copy(MO[:, 1:1 + NS], row(GT, TP, T)).then_inc(gate_m, 1)
                if c == 6:
                    dve.wait_ge(rows_high, 1)
                    for part in ROW_PARTS:
                        lo = V.tensor_tensor(rows_lo[:, part], rows_x[:, part], rows_hi[:, part].bitcast(F32), ALU.subtract)
                    lo.then_inc(rows_split, 1)
                if 8 <= c <= 11:
                    dve.wait_ge(bc_made, c - 7)
                    g = 2 * (c - 8)
                    V.tensor_copy(ES[:, g:g + 2, :], PS[:, 4:6, 0:ESW]).then_inc(bc_copied, 1)

            def pair_keys(k, r):
                V.tensor_tensor(kM[:, :, :], kv3[:, 0:DK].bitcast(F32)[:, None, :].broadcast_to([3 * NS, 2, DK]),
                                M3[:, 2 * r:2 * r + 2][:, :, None].broadcast_to([3 * NS, 2, DK]), ALU.mult).then_inc(km_ready, 1)

            def head(t, k, Q, K, og):
                if t == 0:
                    dve.wait_ge(hp_turned, k + 1)
                    after(dve, c2_made, k)
                    after(dve, outer_made, k * 4)
                    V.tensor_tensor(SPf, PS[:, 6, 0:2 * C], Ef[:, bass.ds(k * (2 * C), 2 * C)], ALU.mult)
                    V.tensor_scalar(KV[:, 0:DK], PS[0:3 * NS, 5, 0:DK], WK3[:, bass.ds(k, 1)], None, ALU.mult)
                    V.tensor_copy(KV[:, DK:DK + DV], PS[0:3 * NS, 5, DK:DK + DV]).then_inc(sp_ready, 1)
                if t == 1:
                    V.tensor_tensor(Q[:, C:2 * C], Q[:, C:2 * C], decays(k, 0, C), ALU.mult).then_inc(qsc_ready, 1)
                    dve.wait_ge(kvs_ready, k + 1)
                    for i, s in enumerate((slice(0, DK), slice(DK, DK + DV))):
                        part = V.scalar_tensor_tensor(kv3[:, s], KV[:, s], R3[:, i:i + 1], kv3[:, s].bitcast(F32), ALU.mult, ALU.subtract)
                    part.then_inc(kv3_ready, 1)
                    dve.wait_ge(kv3_ready, k + 1)
                    pair_keys(k, 0)
                if t == 2:
                    dve.wait_ge(c2_made, k + 1)
                    V.scalar_tensor_tensor(C1[:, :], C1[:, :], decays(k, C - 1, 1), PS[:, 4, 0:DV + 1], ALU.mult, ALU.add).then_inc(c2_ready, 1)
                    dve.wait_ge(c2_ready, k + 1)
                    V.tensor_copy(NO[:, bass.ds(k + 64, 1)], C1[:, DV:DV + 1]).then_inc(nn_ready, 1)
                if t == 3:
                    after(dve, nums_made, k)
                    V.tensor_tensor(nq[:, :], K[:, TP:T], decays(k, C + NS, NS), ALU.mult)
                    new = NOv[:, :, bass.ds(k, 1)]
                    V.tensor_tensor(new, NStv[:, :, bass.ds(k, 1)], decays(k, C, NS)[:, :, None], ALU.mult).then_inc(ns_step, 1)
                    dve.wait_ge(ns_step, k * 2 + 1)
                    V.tensor_tensor(new, new, nq[:, :][:, :, None], ALU.add).then_inc(ns_step, 1)
                    dve.wait_ge(ns_step, k * 2 + 2)
                    V.tensor_tensor(nq[:, :][:, :, None], new, Q[:, TP:T][:, :, None], ALU.mult).then_inc(nq_ready, 1)
                if 3 <= t <= 6:
                    r = t - 3
                    dve.wait_ge(outer_made, k * 4 + (r + 1))
                    if r % 2 == 0:
                        dve.wait_ge(cs_in[r // 2], k * 16 + 16)
                    for x in range(2):
                        b = 2 * r + x
                        u = V.scalar_tensor_tensor(Cs[:, b, :], Cs[:, b, :], decays(k, C + b, 1), PS[:, 4, DV * x:DV * x + DV],
                                                   ALU.mult, ALU.add)
                    u.then_inc(cs_upd, 1)
                    if r < 3:
                        pair_keys(k, r + 1)
                if t == 7:
                    dve.wait_ge(nums_made, k + 1)
                    RD = ssq[:, 0, :]
                    V.scalar_tensor_tensor(RD, PS[:, 5, 0:T], -1.0, ESf[:, bass.ds(k * ESW, T)], ALU.mult, ALU.max).then_inc(rd_step, 1)
                    dve.wait_ge(rd_step, k * 3 + 1)
                    V.tensor_tensor(RD, PS[:, 5, 0:T], RD, ALU.max).then_inc(rd_step, 1)
                    dve.wait_ge(rd_step, k * 3 + 2)
                    V.reciprocal(RD, RD).then_inc(rd_step, 1)
                    dve.wait_ge(rd_step, k * 3 + 3)
                    after(dve, b1_ready, k)
                    V.tensor_tensor(Hh[:, :, :], two(6), over2(RD), ALU.mult).then_inc(hn_ready, 1)
                if t == 9:
                    dve.wait_ge(rm_ready, k + 1)
                    RN = ssq[:, 1, :]
                    V.reciprocal(RN, RMS[:, :]).then_inc(rn_ready, 1)
                    dve.wait_ge(rn_ready, k + 1)
                    dve.wait_ge(og_ready, k + 1)
                    V.scalar_tensor_tensor(og[:, :, :], og[:, :, :], 1.0, over2(RN), ALU.add, ALU.mult).then_inc(ogs_ready, 1)
                if t == 10:
                    dve.wait_ge(ogs_ready, k + 1)
                    dve.wait_ge(sqh_ready, k + 1)
                    V.tensor_tensor(Hh[:, :, :], og[:, :, :], Hh[:, :, :], ALU.mult).then_inc(yy_ready, 1)
                if t == 11:
                    dve.wait_ge(bh1_ready, k + 1)
                    for m in range(2):
                        j = bass.ds(2 * k + m, 1)
                        lo = V.scalar_tensor_tensor(B_lo[:, j, :], Hh[:, m:m + 1, :], HG[:, j], B_hi[:, j, :].bitcast(F32), ALU.mult, ALU.subtract)
                    lo.then_inc(b1_ready, 1)

            def dve_in1(it):
                zero = isinstance(it, int) and it == 0
                rs2 = over2(RS[:, :])
                for c in range(24):
                    split_lo(dve, "D", in1, it, c)
                    if zero:
                        gates(c)
                    head_steps(head, it, c)
                    if c % 4 == 3:
                        g = c // 4
                        dve.wait_ge(pe_block, in1.n(it, c + 1))
                        if c == 3 and not zero:
                            dve.wait_ge(qb_copied, it)
                            dve.wait_ge(nums_made, 2 * it - 1)
                        if c == 11 and zero:
                            dve.wait_ge(bc_made, 4)
                            dve.wait_ge(out_done, 16 * 6)
                            V.tensor_copy(VT[:, :, DV:DV + 1], ones[:, 0:2][:, :, None])
                        if c == 11 and not zero:
                            dve.wait_ge(hp_turned, 2 * it)
                        if c == 15:
                            dve.wait_ge(hp_turned, 2 * it + 1)
                        ps = two(group_bank(in1, g))
                        if g == 0:
                            V.scalar_tensor_tensor(QA[:, :, :], ps, DK ** -0.5, rs2, ALU.mult, ALU.mult).then_inc(evac_done, 1)
                        else:
                            out = (KA, VV, VV, OG[0], OG[1])[g - 1]
                            V.tensor_tensor(out[:, :, :], ps, rs2, ALU.mult).then_inc(evac_done, 1)
            turns(dve, in1, dve_in1, peel=1)
            for c in range(24):
                split_lo(dve, "D", out1a, 0, c)
                if c < 12:
                    head(c, NH - 1, Qb, Kb, OG[1])
                if c % 3 == 2:
                    dve.wait_ge(pe_block, out1a.n(0, c + 1))
                    add1(out1a, c // 3)
            for c in range(8):
                split_lo(dve, "D", out1b, 0, c)
                dve.wait_ge(pe_block, out1b.n(0, c + 1))
                add1(out1b, c)
                if c:
                    gain_lo(dve, 3, c - 1, MPN + KT)
            gain_lo(dve, 3, 7, MPN + KT)
            wait_outputs1(dve)

        def add1(ph, p):
            x = X[:, 2 * p:2 * p + 2, :]
            nc.vector.tensor_tensor(x, two(group_bank(ph, p)), x, ALU.add).then_inc(evac_done, 1)

        block = ctx.enter_context(nc.Block())

        @block.sync
        def _(sp):
            sp.dma_start(xs[:, :], I["x_sample"][:, 0, :]).then_inc(x_in[0], 16)
            for half in range(2):
                f = slice(DR * half, DR * half + DR)
                for c in range(2):
                    sp.dma_start(xt[:, c, f], I["x_prompt"][0, P * c:P * c + P, f]).then_inc(x_in[half], 16)
            w_in = I["ab_w_in"][0]
            def load_in0(it):
                for c in range(16):
                    load(sp, in0, it, c, w_in, 512 * (c % 4), 256 * it + IN0_COLS[c // 4])
                    if isinstance(it, int) and it == 0 and c == 3:
                        for name, half, col, rows in PARAM_ROWS:
                            sp.dma_start(prow[col - P * half:col - P * half + rows, half, :], flat(I[name], rows))\
                              .then_inc(params_in, 16)
                        sp.dma_start(drow[:, :], I["conf_dw_w"][0]).then_inc(states_in, 16)
                        sp.dma_start(rrow[:, :], I["state_rglru_conv"][0].rearrange("b t c -> (b t) c")).then_inc(states_in, 16)
                        for c2 in range(2):
                            sp.dma_start(crow[:, c2, :], I["state_conf_conv"][0].rearrange("b t c -> (b t) c")[120 * c2:120 * c2 + 120, :])\
                              .then_inc(states_in, 16)
            turns(sp, in0, load_in0, peel=1)
            sp.dma_start(O["s_cconv"][0, :, 0:W31 - 2, :], I["state_conf_conv"][0, :, 1:W31 - 1, :]).then_inc(out_done, 16)
            sp.dma_start(O["s_rconv"][0, :, 0:W4 - 2, :], I["state_rglru_conv"][0, :, 1:W4 - 1, :]).then_inc(out_done, 16)
            w_out = I["ab_w_out"][0]
            for ph, row in ((out0a, 0), (out0b, DR)):
                for c in range(16):
                    load(sp, ph, 0, c, w_out, row + 512 * (c % 2), 256 * (c // 2))
            def load_mlp(l):
                for h in (0, 1):
                    def load_up(it):
                        for c in range(8):
                            load(sp, PH[f"up{l}{h}"], it, c, I["mlp_w_up"][l], 512 * (c % 4),
                                 512 * it + (FF // 2 * h + 256 * (c // 4)))
                    def load_down(it):
                        for c in range(16):
                            load(sp, PH[f"down{l}{h}"], it, c, I["mlp_w_down"][l], FF // 2 * h + 512 * (c % 8),
                                 512 * it + 256 * (c // 8))
                    turns(sp, PH[f"up{l}{h}"], load_up)
                    turns(sp, PH[f"down{l}{h}"], load_down)
            load_mlp(0)
            load_mixer1(sp)
            load_mlp(1)
            for q in range(4):
                cols = slice(512 * q, 512 * q + 512)
                sp.wait_ge(ya_scaled, q + 1)
                sp.dma_start(O["y_prompt"][0, 0:P, cols], YO[:, 0, cols]).then_inc(out_done, 16)
                sp.wait_ge(yd_scaled, q + 1)
                sp.dma_start(O["y_prompt"][0, P:TP, cols], YO[:, 1, cols]).then_inc(out_done, 16)
            sp.wait_ge(yd_scaled, 5)
            sp.dma_start(O["y_sample"][:, 0, :], YS[:, :]).then_inc(out_done, 16)
            sp.wait_ge(out_done, 16 * OUTS)
            sp.wait_ge(ot_out, 64 * 4)
            wait_outputs1(sp)

        @block.tensor
        def _(pe):
            pe.wait_ge(consts, CONSTS)
            def turn_x(p):
                pe.wait_ge(x_in[p // 4], 48 if p < 4 else 32)
                if p >= 2:
                    pe.wait_ge(x_loaded, p - 1)
                for m in range(2):
                    bank, f = 4 + 2 * (p % 2) + m, slice(256 * p + P * m, 256 * p + P * m + P)
                    for c in range(2):
                        nc.tensor.transpose(PS[:, bank, P * c:P * c + P], xt[:, c, f], ident[:, :])
                    tr = nc.tensor.transpose(PS[:, bank, TP:T], xs[:, f], ident[0:NS, 0:NS])
                tr.then_inc(x_turned, 1)
            pe.wait_ge(gain_in, 16)
            nc.tensor.transpose(PS[:, 3, 0:KT], prow[0:KT, 0, :], ident[0:KT, 0:KT]).then_inc(par_turned, 1)
            for p in range(6):
                turn_x(p)
            def states_in_turn(part):
                pe.wait_ge(states_in, 64)
                if part == 0:
                    for j in range(8):
                        nc.tensor.transpose(PS[:, 4, 31 * j:31 * j + 31], drow[:, P * j:P * j + P], ident[0:W31, 0:W31])
                        tr = nc.tensor.transpose(PS[:, 5, 24 * j:24 * j + 24], rrow[:, P * j:P * j + P], ident[0:24, 0:24])
                else:
                    pe.wait_ge(states_ready, 2 * part)
                    for j in range(8):
                        tr = nc.tensor.transpose(PS[:, 4 + j // 4, 120 * (j % 4):120 * (j % 4) + 120],
                                                 crow[:, part - 1, P * j:P * j + P], ident[0:120, 0:120])
                tr.then_inc(states_turned, 1)

            def turn_states(q):
                for m in range(2):
                    tr = nc.tensor.transpose(PS[0:49, 4, P * m:P * m + P], TS[:, m, :], ident[:, :])
                tr.then_inc(ts_turned, 1)

            def wait_states(q):
                pe.wait_ge(tsg_ready, q + 1)
                pe.wait_ge(gates_read, q + 1)

            def mul_in0(it):
                zero = isinstance(it, int) and it == 0
                for c in range(16):
                    if c == 3 and not zero:
                        wait_states(it - 1)
                    if zero and c < 4:
                        pe.wait_ge(a_ready, 2 * (c + 1))
                    multiply(pe, in0, it, c, c // 4, A_hi, A_lo, 4 * (c % 4), c % 4 == 0, c % 4 == 3)
                    if zero and c == 0:
                        turn_x(6)
                        turn_x(7)
                    if zero and 2 <= c <= 4:
                        pe.wait_ge(x_loaded, 8)
                        states_in_turn(c - 2)
                    if zero and c == 1:
                        pe.wait_ge(params_in, 16 * 13)
                        pe.wait_ge(par_ready, 1)
                        nc.tensor.transpose(PS[:, 3, 0:P], prow[:, 0, :], ident[:, :])
                        nc.tensor.transpose(PS[:, 3, P:P + 120], prow[0:120, 1, :], ident[0:120, 0:120]).then_inc(par_turned, 1)
                    if zero and c == 2:
                        sum_squares(pe, 0)
                    if zero and c == 3:
                        pe.wait_ge(par_ready, 2)
                    if c == 3 and not zero:
                        turn_states(it - 1)
                    if c == 6:
                        pe.wait_ge(xc_ready, it + 1)
                        pe.wait_ge(gw_in, it * 64 + 64)
                        if zero:
                            pe.wait_ge(rms_ready, 1)
                            pe.wait_ge(states_ready, 6)
                        else:
                            pe.wait_ge(ot_ready, it)
                        for gate in range(2):
                            for m in range(2):
                                mm = nc.tensor.matmul(PS[:, 4 + 2 * gate + m, 0:T], GW[:, 2 * gate + m, :],
                                                      XC[:, m, :], start=True, stop=True)
                        mm.then_inc(gates_ready, 1)
            turns(pe, in0, mul_in0, peel=1)

            def column_sums(bank):
                nc.tensor.matmul(PS[:, bank, 0:T], ones[:, :], ssq[:, 0, :], start=True, stop=False)
                return nc.tensor.matmul(PS[:, bank, 0:T], ones[:, :], ssq[:, 1, :], start=False, stop=True)

            for c in range(16):
                pe.wait_ge(b_ready, 2 * (c % 2 + 1))
                multiply(pe, out0a, 0, c, c // 2, B_hi, B_lo, 4 * (c % 2), c % 2 == 0, c % 2 == 1)
                if c == 3:
                    wait_states(3)
                    turn_states(3)
                    pe.wait_ge(hs_ready, 4)
                    nc.tensor.transpose(PS[0:72, 5, 0:P], HS[:, :], ident[:, :]).then_inc(hs_turned, 1)
                if c == 11:
                    pe.wait_ge(ln_added, 4)
                    column_sums(6).then_inc(mu_ready, 1)
                if c == 13:
                    pe.wait_ge(ln_added, 8)
                    column_sums(7).then_inc(var_ready, 1)
            for c in range(16):
                pe.wait_ge(b_ready, 4 + 2 * (c % 2 + 1))
                multiply(pe, out0b, 0, c, c // 2, B_hi, B_lo, 8 + 4 * (c % 2), c % 2 == 0, c % 2 == 1)

            def turn_result(p):
                pe.wait_ge(fin_ready, p + 1)
                after(pe, fin_copied, p)
                for m in range(2):
                    for c in range(2):
                        nc.tensor.transpose(PS[:, 4, 256 * c + P * m:256 * c + P * m + P], U[:, m, P * c:P * c + P], ident[:, :])
                for m in range(2):
                    tr = nc.tensor.transpose(PS[0:NS, 5, P * m:P * m + P], U[:, m, TP:T], ident[:, :])
                tr.then_inc(fin_turned, 1)

            def mul_mlp(l):
                e = 1 + 2 * l
                for h in (0, 1):
                    up, down = PH[f"up{l}{h}"], PH[f"down{l}{h}"]
                    def mul_up(it):
                        for c in range(8):
                            if isinstance(it, int) and it == 0 and c < 4:
                                pe.wait_ge(a_ready, 8 * e + 2 * (c + 1))
                            multiply(pe, up, it, c, c // 4, A_hi, A_lo, 4 * (c % 4), c % 4 == 0, c % 4 == 3)
                            if isinstance(it, int) and it == 0 and c == 1 and h == 0:
                                sum_squares(pe, e)
                    def mul_down(it):
                        for c in range(16):
                            pe.wait_ge(h_ready, 16 * (2 * l + h) + 2 * (c % 8 + 1))
                            multiply(pe, down, it, c, c // 8, H_hi, H_lo, 4 * (c % 8), c % 8 == 0, c % 8 == 7)
                            if down is LAST and c == 9:
                                turn_result(2 * it)
                            if down is LAST and c == 1 and not (isinstance(it, int) and it == 0):
                                turn_result(2 * it - 1)
                    turns(pe, up, mul_up, peel=1 - h)
                    turns(pe, down, mul_down, peel=1 if down is LAST else 0)
            mul_mlp(0)
            pe_mixer1(pe)
            mul_mlp(1)
            turn_result(7)
            pe.wait_ge(ssq_added, 8 * (2 * DEPTH + 1))
            for c, tok in enumerate((slice(0, P), slice(P, TP), slice(TP, T))):
                out = PS[0:tok.stop - tok.start, 7, c:c + 1]
                nc.tensor.matmul(out, ssq[:, 0, tok], ones[:, 0:1], start=True, stop=False)
                mm = nc.tensor.matmul(out, ssq[:, 1, tok], ones[:, 0:1], start=False, stop=True)
            mm.then_inc(ssq_ready, 1)

        @block.scalar
        def _(act):
            act.dma_start(prow[0:KT, 0, :], flat(I["ab_norm"], KT)).then_inc(gain_in, 16)
            act.wait_ge(par_turned, 1)
            nc.scalar.copy(par[:, 0:KT], PS[:, 3, 0:KT]).then_inc(par_ready, 1)
            act.wait_ge(consts, CONSTS)
            act.wait_ge(par_ready, 1)
            for p in range(8):
                act.wait_ge(x_loaded, p + 1)
                square_and_gain(act, 0, p, ABN)
                if p % 2 == 1 and p < 7:
                    split_hi(act, in0, 0, p // 2 - HI_AHEAD)
            act.wait_ge(par_turned, 2)
            nc.scalar.copy(par[:, KT:NPAR], PS[:, 3, KT:NPAR]).then_inc(par_ready, 1)
            act.wait_ge(par_ready, 2)
            nc.scalar.mul(hBA[:, :], par[:, BA:BA + 8], 0.5).then_inc(absl, 1)
            nc.scalar.mul(hBX[:, :], par[:, BX:BX + 8], 0.5).then_inc(absl, 1)
            nc.scalar.mul(hLNG[:, :], par[:, LNG:LNG + 8], 0.5).then_inc(absl, 1)
            nc.scalar.mul(hLNB[:, :], par[:, LNB:LNB + 8], 0.5).then_inc(absl, 1)
            nc.scalar.activation(spt[:, 0, :], par[:, LAM:LAM + 8], ACT.Abs).then_inc(absl, 1)
            act.wait_ge(absl, 5)
            nc.scalar.activation(spt[:, 1, :], spt[:, 0, :], ACT.Exp, scale=-1.0).then_inc(expl, 1)

            def write_states(q):
                act.wait_ge(ts_turned, q + 1)
                if not isinstance(q, int) or q:
                    act.wait_ge(ot_out, q * 64)
                nc.scalar.copy(OT[:, :, :].rearrange("p m f -> p (m f)"), PS[0:49, 4, 0:256]).then_inc(ot_ready, 1)
                act.wait_ge(ot_ready, q + 1)
                cols = bass.ds(256 * q, 256)
                rows = OT[:, :, :].rearrange("p m f -> p (m f)")
                for dst, r in ((O["p_cconv"][0, 0, :, cols], slice(0, 30)),
                               (O["s_cconv"][0, :, W31 - 2, cols], slice(30, 38)),
                               (O["p_rconv"][0, 0, :, cols], slice(38, 41)),
                               (O["s_rconv"][0, :, W4 - 2, cols], slice(41, 49))):
                    act.dma_start(dst, rows[r, :]).then_inc(ot_out, 16)

            def act_in0(it):
                zero = isinstance(it, int) and it == 0
                for c in range(16):
                    split_hi(act, in0, it, c)
                    if c == 0:
                        if not zero:
                            act.wait_ge(gates_ready, it)
                        else:
                            act.wait_ge(consts, CONSTS)
                        for gate, name in enumerate(("rglru_wa", "rglru_wx")):
                            for sub in range(2):
                                src = I[name][0].rearrange("(q m s) a c -> q s a m c", m=2, s=2)[bass.ds(it, 1), sub]
                                act.dma_start(GW[64 * sub:64 * sub + 64, 2 * gate:2 * gate + 2, 64 * sub:64 * sub + 64],
                                              src.rearrange("q a m c -> (q a) m c")).then_inc(gw_in, 16)
                    if zero and c == 3:
                        root(act, 0)
                    if zero and c == 2:
                        act.wait_ge(states_turned, 1)
                        nc.scalar.copy(w31f, PS[:, 4, 0:248]).then_inc(states_ready, 1)
                        nc.scalar.copy(XRs[:, :, :, 0:3], PS[:, 5, 0:192].rearrange("p (j b w) -> p j b w", j=8, b=8))\
                          .then_inc(states_ready, 1)
                    if zero and 3 <= c <= 4:
                        half = c - 3
                        act.wait_ge(states_turned, half + 2)
                        for jh in range(2):
                            for jj in range(4):
                                cp = nc.scalar.copy(GLs[:, 4 * jh + jj, 4 * half:4 * half + 4, 0:30],
                                                    PS[:, 4 + jh, 120 * jj:120 * jj + 120].rearrange("p (b w) -> p b w", b=4))
                            cp.then_inc(states_ready, 1)
                    if c == 4 and not zero:
                        write_states(it - 1)
                    if c == 6:
                        act.wait_ge(gates_ready, it + 1)
                        if not zero:
                            act.wait_ge(hs_ready, it)
                        for m in range(2):
                            nc.scalar.activation(RG[:, m:m + 1, :], PS[:, 4 + m:5 + m, 0:T], ACT.Tanh, scale=0.5,
                                                 bias=hBA[:, bass.ds(2 * it + m, 1)])
                            q = nc.scalar.activation(IG[:, m:m + 1, :], PS[:, 6 + m:7 + m, 0:T], ACT.Tanh, scale=0.5,
                                                     bias=hBX[:, bass.ds(2 * it + m, 1)])
                        q.then_inc(gates_read, 1)
                    if c == 7:
                        act.wait_ge(gates_read, it + 1)
                        if zero:
                            act.wait_ge(lam_ready, 1)
                        for m in range(2):
                            j = bass.ds(2 * it + m, 1)
                            nc.scalar.activation(AA[:, m:m + 1, :], RG[:, m:m + 1, :], ACT.Exp, scale=hla[:, j], bias=hla[:, j])
                            q = nc.scalar.activation(TL[:, m:m + 1, :], RG[:, m:m + 1, :], ACT.Tanh, scale=nhla[:, j], bias=nhla[:, j])
                        q.then_inc(al_ready, 1)
                    if c == 8:
                        act.wait_ge(evac_done, in0.g(it, 1) + 1)
                        nc.scalar.activation(G2[:, :, :], G[:, :, :], ACT.Square).then_inc(g2_ready, 1)
                        act.wait_ge(w_ready, it + 1)
                        nc.scalar.activation(TL[:, :, :], TL[:, :, :], ACT.Sqrt, bias=tiny[:, :]).then_inc(root_ready, 1)
                    if c == 9:
                        act.wait_ge(g3_ready, it + 1)
                        nc.scalar.activation(G3[:, :, :], G3[:, :, :], ACT.Tanh, scale=0.7978845608028654).then_inc(gth_ready, 1)
                    if c == 11:
                        act.wait_ge(y_ready, it + 1)
                        nc.scalar.activation(B_hi[:, bass.ds(2 * it, 2), :], G2[:, :, :], ACT.Copy).then_inc(bh_ready, 1)
                    if c == 12:
                        act.wait_ge(evac_done, in0.g(it, 2) + 1)
                        nc.scalar.activation(TB[:, :, :], TB[:, :, :], ACT.Tanh, scale=0.5).then_inc(tb_ready, 1)
            turns(act, in0, act_in0, peel=1)

            for c in range(16):
                split_hi(act, out0a, 0, c)
                if c == 4:
                    write_states(3)
                    act.wait_ge(hs_turned, 1)
                    nc.scalar.copy(OH[:, :], PS[0:72, 5, 0:P]).then_inc(oh_ready, 1)
                    act.wait_ge(oh_ready, 1)
                    act.dma_start(flat(O["s_rh"], 64), OH[0:64, :]).then_inc(out_done, 16)
                    act.dma_start(flat(O["p_rh"], 8), OH[64:72, :]).then_inc(out_done, 16)
                if c == 11:
                    for q in range(4):
                        act.wait_ge(yd_ready, q + 1)
                        nc.scalar.activation(Tb[q][:, :, :], YC[:, 2 * q:2 * q + 2, :], ACT.Square).then_inc(lsq_ready, 1)
                if c == 14:
                    act.wait_ge(var_ready, 1)
                    nc.scalar.activation(G[:, 1, :], PS[:, 7, 0:T], ACT.Sqrt, scale=1.0 / DR, bias=eps[:, :]).then_inc(dev_ready, 1)
                if c == 15:
                    for q in range(4):
                        act.wait_ge(yn_ready, q + 1)
                        for m in range(2):
                            j = slice(2 * q + m, 2 * q + m + 1)
                            th = nc.scalar.activation(Tb[q][:, m, :], YC[:, 2 * q + m, :], ACT.Tanh, scale=hLNG[:, j], bias=hLNB[:, j])
                        th.then_inc(lth_ready, 1)
                if c == 15:
                    for q in range(4):
                        act.wait_ge(z_ready, q + 1)
                        nc.scalar.activation(B_hi[:, 8 + 2 * q:10 + 2 * q, :], Zb[q][:, :, :], ACT.Copy, scale=0.5).then_inc(bh_ready, 1)
            for c in range(16):
                split_hi(act, out0b, 0, c)
                if c % 2 == 1:
                    act.wait_ge(evac_done, out0b.g(0, c // 2) + 1)
                    square_and_gain(act, 1, c // 2, MPN)

            def result_gain(p):
                after(act, fin_turned, p)
                for m in range(2):
                    g = nc.scalar.activation(U[:, m:m + 1, :], X[:, bass.ds(2 * p + m, 1), :], ACT.Copy,
                                             scale=par[:, bass.ds(2 * p + (FIN + m), 1)])
                g.then_inc(fin_ready, 1)

            def result_rows(p):
                act.wait_ge(fin_turned, p + 1)
                nc.scalar.copy(YO[:, :, bass.ds(256 * p, 256)], PS[:, 4, :].rearrange("p (c f) -> p c f", c=2))
                nc.scalar.copy(YS[:, bass.ds(256 * p, 256)], PS[0:NS, 5, 0:256]).then_inc(fin_copied, 1)

            def act_mlp(l):
                for h in (0, 1):
                    up, down = PH[f"up{l}{h}"], PH[f"down{l}{h}"]
                    k = 2 * l + h
                    def act_up(it):
                        for c in range(8):
                            split_hi(act, up, it, c)
                            if isinstance(it, int) and it == 0 and c == 2 and h == 0:
                                root(act, 1 + 2 * l)
                            if c % 4 == 3:
                                p = 2 * it + c // 4
                                act.wait_ge(u_ready, p + (16 * k + 1))
                                nc.scalar.activation(H_hi[:, bass.ds(2 * p, 2), :], U[:, :, :], ACT.Copy).then_inc(hh_ready, 1)
                    def act_down(it):
                        for c in range(16):
                            split_hi(act, down, it, c)
                            if c % 8 == 7 and h == 1:
                                act.wait_ge(evac_done, down.g(it, c // 8) + 1)
                                p = 2 * it + c // 8
                                square_and_gain(act, 2 + 2 * l, p, None if l == DEPTH - 1 else MLN)
                                if down is LAST:
                                    result_gain(p)
                            if down is LAST and c == 10:
                                result_rows(2 * it)
                            if down is LAST and c == 2 and not (isinstance(it, int) and it == 0):
                                result_rows(2 * it - 1)
                    turns(act, up, act_up, peel=1 - h)
                    turns(act, down, act_down, peel=1 if down is LAST else 0, tail=1 if down is LAST else 0)
            act_mlp(0)
            act_mixer1(act)
            act_mlp(1)
            result_rows(7)
            act.wait_ge(ssq_ready, 2 * DEPTH + 1)
            nc.scalar.activation(rt[:, 0:2], PS[:, 7, 0:2], ACT.Sqrt, scale=1.0 / D, bias=eps[:, :])
            nc.scalar.activation(rt[0:NS, 2:3], PS[0:NS, 7, 2:3], ACT.Sqrt, scale=1.0 / D, bias=eps[0:NS, :]).then_inc(rt_ready, 1)
            act.wait_ge(rt_inv, 1)
            act.wait_ge(fin_copied, 8)
            for q in range(4):
                y = YO[:, 0, 512 * q:512 * q + 512]
                nc.scalar.activation(y, y, ACT.Copy, scale=rt[:, 0:1]).then_inc(ya_scaled, 1)

        @block.gpsimd
        def _(pool):
            nc.gpsimd.memset(ident[:, :], 0.0).then_inc(zeroed, 1)
            nc.gpsimd.memset(ones[:, :], 1.0).then_inc(consts, 1)
            pool.wait_ge(zeroed, 1)
            nc.gpsimd.affine_select(out=ident[:, :], in_=ident[:, :], compare_op=ALU.not_equal, fill=1.0, base=0,
                                    pattern=[[-1, P]], channel_multiplier=1).then_inc(consts, 1)
            nc.gpsimd.memset(eps[:, :], EPS).then_inc(consts, 1)
            nc.gpsimd.memset(tiny[:, :], 1e-30).then_inc(consts, 1)
            nc.gpsimd.memset(GW[:, :, :], 0.0).then_inc(consts, 1)
            nc.gpsimd.memset(GLp[:, :, 0:W31 - 1], 0.0).then_inc(consts, 1)
            nc.gpsimd.memset(XRp[:, :, 0:W4 - 1], 0.0).then_inc(consts, 1)
            zero_squares(pool, 0)
            for p in range(8):
                if p == 6:
                    split_lo(pool, "P", in0, 0, 0)
                add_squares(pool, 0, p)

            def glu_columns(q):
                nc.gpsimd.tensor_copy(TS[:, :, 0:30], GLp[:, :, TP:TP + 30])
                nc.gpsimd.tensor_copy(TS[:, :, 30:38], GLs[:, bass.ds(2 * q, 2), :, W31 - 1]).then_inc(tsg_ready, 1)

            def pool_in0(it):
                zero = isinstance(it, int) and it == 0
                pair = bass.ds(2 * it, 2)
                for c in range(16):
                    if c == 1 and not zero:
                        pool.wait_ge(gl_ready, it)
                    if c == 4:
                        pool.wait_ge(evac_done, in0.g(it, 0) + 1)
                        if not zero:
                            pool.wait_ge(ts_turned, it)
                    if c == 11:
                        pool.wait_ge(h0_ready, it + 1)
                    if not (zero and c == 0):
                        split_lo(pool, "P", in0, it, c)
                    if c == 1 and not zero:
                        glu_columns(it - 1)
                    if c == 4:
                        nc.gpsimd.tensor_copy(TS[:, :, 38:41], XRp[:, :, TP:TP + 3])
                        nc.gpsimd.tensor_copy(TS[:, :, 41:49], XRs[:, pair, :, 3]).then_inc(tsx_ready, 1)
                    if c == 11:
                        nc.gpsimd.tensor_copy(HSv[:, pair, :], RG[:, :, TP:T])
                        nc.gpsimd.tensor_copy(HS[:, bass.ds(2 * it + 64, 2)], RG[:, :, TP - 1]).then_inc(hs_ready, 1)
            turns(pool, in0, pool_in0, peel=1)

            for c in range(16):
                split_lo(pool, "P", out0a, 0, c)
                if c == 1:
                    pool.wait_ge(gl_ready, 4)
                    glu_columns(3)
                if c == 0:
                    pool.wait_ge(ssq_ready, 1)
                    nc.gpsimd.memset(ssq[:, :, :], 0.0).then_inc(ln_zeroed, 1)
                if c in (2, 4, 6, 10):
                    q = min(c // 2 - 1, 3)
                    pool.wait_ge(ln_zeroed, 1)
                    pool.wait_ge(yc_ready, q + 1)
                    if q:
                        pool.wait_ge(ln_added, q)
                    nc.gpsimd.tensor_tensor(ssq[:, :, :], ssq[:, :, :], YC[:, 2 * q:2 * q + 2, :], ALU.add).then_inc(ln_added, 1)
                if c == 11:
                    pool.wait_ge(mu_ready, 1)
                    nc.gpsimd.memset(ssq[:, :, :], 0.0).then_inc(ln_zeroed, 1)
                    pool.wait_ge(ln_zeroed, 2)
                    for q in range(4):
                        pool.wait_ge(lsq_ready, q + 1)
                        if q:
                            pool.wait_ge(ln_added, 4 + q)
                        nc.gpsimd.tensor_tensor(ssq[:, :, :], ssq[:, :, :], Tb[q][:, :, :], ALU.add).then_inc(ln_added, 1)
            pool.wait_ge(var_ready, 1)
            zero_squares(pool, 1)
            for c in range(16):
                split_lo(pool, "P", out0b, 0, c)
                if c % 2 == 1:
                    add_squares(pool, 1, c // 2)

            def pool_mlp(l):
                zero_squares(pool, 2 + 2 * l)
                down = PH[f"down{l}1"]
                def pool_down(it):
                    for c in (7, 15):
                        add_squares(pool, 2 + 2 * l, 2 * it + c // 8)
                turns(pool, down, pool_down)
            pool_mlp(0)
            pool_mixer1(pool)
            pool_mlp(1)

        @block.vector
        def _(dve):
            V = nc.vector
            steps = [0]

            def link(ins):
                steps[0] += 1
                ins.then_inc(small, 1)
                dve.wait_ge(small, steps[0])

            def log1p_terms(part, e, z, z2, p):
                if part == 0:
                    link(V.tensor_scalar(z2, e, 2.0, None, ALU.add))
                    link(V.reciprocal(z, z2))
                    link(V.tensor_tensor(z, z, e, ALU.mult))
                    link(V.tensor_tensor(z2, z, z, ALU.mult))
                    link(V.tensor_scalar(p, z2, 1.0 / 17, None, ALU.mult))
                for k in ((), (7, 6, 5, 4), (3, 2, 1))[part]:
                    link(V.scalar_tensor_tensor(p, p, 1.0 / (2 * k + 1), z2, ALU.add, ALU.mult))
                if part == 2:
                    link(V.scalar_tensor_tensor(p, p, 1.0, z, ALU.add, ALU.mult))

            for p in range(8):
                dve.wait_ge(x_turned, p + 1)
                V.tensor_copy(X[:, 2 * p:2 * p + 2, :], two(4 + 2 * (p % 2))).then_inc(x_loaded, 1)
                if p:
                    gain_lo(dve, 0, p - 1, ABN)
                if p in (2, 4):
                    split_lo(dve, "D", in0, 0, p // 2 - 1 - LO_AHEAD)
            gain_lo(dve, 0, 7, ABN)
            dve.wait_ge(expl, 1)
            for part in range(3):
                log1p_terms(part, spt[:, 1, :], spt[:, 2, :], spt[:, 3, :], spt[:, 4, :])
            link(V.tensor_scalar(spt[:, 5, :], par[:, LAM:LAM + 8], -1.0, 0.0, ALU.mult, ALU.max))
            link(V.scalar_tensor_tensor(spt[:, 5, :], spt[:, 4, :], 2.0, spt[:, 5, :], ALU.mult, ALU.add))
            link(V.tensor_scalar(hla[:, :], spt[:, 5, :], -4.0, None, ALU.mult))
            V.tensor_scalar(nhla[:, :], spt[:, 5, :], 4.0, None, ALU.mult).then_inc(lam_ready, 1)

            def tap(q, w):
                for m in range(2):
                    j = 2 * q + m
                    y = YC[:, bass.ds(j, 1), 0:TP]
                    x = GLp[:, m:m + 1, w:w + TP]
                    ww = w31f[:, bass.ds(31 * j + w, 1)]
                    if w == 0:
                        dve.wait_ge(gl_ready, q + 1)
                        V.tensor_scalar(y, x, ww, par[:, bass.ds(j + DWB, 1)], ALU.mult, ALU.add).then_inc(tap_done, 1)
                    else:
                        dve.wait_ge(tap_done, q * 62 + (2 * w + m - 1))
                        V.scalar_tensor_tensor(y, x, ww, y, ALU.mult, ALU.add).then_inc(tap_done, 1)

            def sample_conv(q):
                pair = bass.ds(2 * q, 2)
                w = w31[:, pair, :][:, :, None, :].broadcast_to([P, 2, NS, W31])
                V.tensor_tensor(GP[:, :, :, :], GLs[:, pair, :, :], w, ALU.mult).then_inc(cs_step, 1)
                dve.wait_ge(cs_step, q * 2 + 1)
                V.tensor_reduce(YC[:, pair, TP:T], GP[:, :, :, :], AX.X, ALU.add).then_inc(cs_step, 1)
                dve.wait_ge(cs_step, q * 2 + 2)
                bias = par[:, bass.ds(2 * q + DWB, 2)][:, :, None].broadcast_to([P, 2, NS])
                V.tensor_tensor(YC[:, pair, TP:T], YC[:, pair, TP:T], bias, ALU.add).then_inc(yc_ready, 1)

            def dve_in0(it):
                zero = isinstance(it, int) and it == 0
                pair = bass.ds(2 * it, 2)
                rs2, rsp, rss = over2(RS[:, :]), over2(RS[:, 0:TP]), over2(RS[:, TP:T])
                for c in range(16):
                    split_lo(dve, "D", in0, it, c)
                    def taps():
                        for w in (2 * c, 2 * c + 1):
                            if not zero and w < W31:
                                tap(it - 1, w)
                    if c not in (3, 4):
                        taps()
                    if c == 3:
                        if zero:
                            invert(dve, 0)
                        else:
                            dve.wait_ge(tsx_ready, it)
                        dve.wait_ge(pe_block, in0.n(it, 4))
                        b = group_bank(in0, 0)
                        V.tensor_tensor(XRp[:, :, 3:3 + TP], PS[:, b:b + 2, 0:TP], rsp, ALU.mult)
                        V.tensor_tensor(XRs[:, pair, :, 3], PS[:, b:b + 2, TP:T], rss, ALU.mult).then_inc(evac_done, 1)
                        dve.wait_ge(evac_done, in0.g(it, 0) + 1)
                        if zero:
                            dve.wait_ge(states_turned, 3)
                        for w in range(W4):
                            for m in range(2):
                                y, x = XC[:, m:m + 1, 0:TP], XRp[:, m:m + 1, w:w + TP]
                                ww = par[:, bass.ds(2 * it + (CW + 8 * w + m), 1)]
                                if w == 0:
                                    V.tensor_scalar(y, x, ww, par[:, bass.ds(2 * it + (CB + m), 1)], ALU.mult, ALU.add).then_inc(xc_tap, 1)
                                else:
                                    dve.wait_ge(xc_tap, it * 8 + (2 * w + m - 1))
                                    V.scalar_tensor_tensor(y, x, ww, y, ALU.mult, ALU.add).then_inc(xc_tap, 1)
                    if c == 4:
                        if zero:
                            dve.wait_ge(states_ready, 2)
                        w = CWv[:, pair, :][:, :, None, :].broadcast_to([P, 2, NS, W4])
                        V.tensor_tensor(XP[:, :, :, :], XRs[:, pair, :, :], w, ALU.mult).then_inc(xs_step, 1)
                        dve.wait_ge(xs_step, it * 2 + 1)
                        V.tensor_reduce(XC[:, :, TP:T], XP[:, :, :, :], AX.X, ALU.add).then_inc(xs_step, 1)
                        dve.wait_ge(xs_step, it * 2 + 2)
                        bias = par[:, bass.ds(2 * it + CB, 2)][:, :, None].broadcast_to([P, 2, NS])
                        V.tensor_tensor(XC[:, :, TP:T], XC[:, :, TP:T], bias, ALU.add).then_inc(xc_ready, 1)
                    if c in (3, 4):
                        taps()
                    if c == 7:
                        dve.wait_ge(pe_block, in0.n(it, 8))
                        V.tensor_tensor(G[:, :, :], two(group_bank(in0, 1)), rs2, ALU.mult).then_inc(evac_done, 1)
                        dve.wait_ge(al_ready, it + 1)
                        V.tensor_tensor(RG[:, :, :], AA[:, :, :], AA[:, :, :], ALU.mult).then_inc(w_step, 1)
                        V.scalar_tensor_tensor(IG[:, :, :], IG[:, :, :], 1.0, XC[:, :, :], ALU.add, ALU.mult).then_inc(t_ready, 1)
                        dve.wait_ge(w_step, it + 1)
                        V.scalar_tensor_tensor(TL[:, :, :], RG[:, :, :], 1.0, TL[:, :, :], ALU.add, ALU.mult).then_inc(w_ready, 1)
                    if c == 8:
                        dve.wait_ge(g2_ready, it + 1)
                        V.tensor_scalar(G3[:, :, :], G2[:, :, :], 0.044715, 1.0, ALU.mult, ALU.add).then_inc(g3_step, 1)
                        dve.wait_ge(g3_step, it + 1)
                        V.tensor_tensor(G3[:, :, :], G3[:, :, :], G[:, :, :], ALU.mult).then_inc(g3_ready, 1)
                    if c == 9:
                        dve.wait_ge(root_ready, it + 1)
                        dve.wait_ge(t_ready, it + 1)
                        V.scalar_tensor_tensor(IG[:, :, :], IG[:, :, :], 0.5, TL[:, :, :], ALU.mult, ALU.mult).then_inc(u0_ready, 1)
                        V.tensor_tensor(RG[:, :, TP:T], AA[:, :, TP:T], H0v[:, pair, :], ALU.mult).then_inc(h0_step, 1)
                        dve.wait_ge(u0_ready, it + 1)
                        for m in range(2):
                            V.tensor_tensor_scan(RG[:, m, 0:TP], AA[:, m, 0:TP], IG[:, m, 0:TP], 0.0, ALU.mult, ALU.add)
                        dve.wait_ge(h0_step, it + 1)
                        V.tensor_tensor(RG[:, :, TP:T], RG[:, :, TP:T], IG[:, :, TP:T], ALU.add).then_inc(h0_ready, 1)
                    if c == 10:
                        dve.wait_ge(gth_ready, it + 1)
                        V.scalar_tensor_tensor(G[:, :, :], G3[:, :, :], 1.0, G[:, :, :], ALU.add, ALU.mult).then_inc(gl_step, 1)
                        dve.wait_ge(gl_step, it + 1)
                        dve.wait_ge(h0_ready, it + 1)
                        V.scalar_tensor_tensor(G2[:, :, :], G[:, :, :], 0.5, RG[:, :, :], ALU.mult, ALU.mult).then_inc(y_ready, 1)
                    if c == 11:
                        dve.wait_ge(pe_block, in0.n(it, 12))
                        V.tensor_tensor(TB[:, :, :], two(group_bank(in0, 2)), rs2, ALU.mult).then_inc(evac_done, 1)
                    if c == 12:
                        dve.wait_ge(bh_ready, it + 1)
                        V.tensor_tensor(B_lo[:, pair, :], G2[:, :, :], B_hi[:, pair, :].bitcast(F32), ALU.subtract).then_inc(b_ready, 1)
                    if c == 15:
                        if not zero:
                            dve.wait_ge(states_ready, 6)
                            sample_conv(it - 1)
                            dve.wait_ge(tsg_ready, it)
                            dve.wait_ge(tap_done, it * 62)
                        dve.wait_ge(pe_block, in0.n(it, 16))
                        V.scalar_tensor_tensor(XC[:, :, :], two(group_bank(in0, 3)), 0.5, rs2, ALU.mult, ALU.mult).then_inc(evac_done, 1)
                        dve.wait_ge(evac_done, in0.g(it, 3) + 1)
                        dve.wait_ge(tb_ready, it + 1)
                        V.scalar_tensor_tensor(GLp[:, :, 30:30 + TP], TB[:, :, 0:TP], 1.0, XC[:, :, 0:TP], ALU.add, ALU.mult)
                        V.scalar_tensor_tensor(GLs[:, pair, :, 30], TB[:, :, TP:T], 1.0, XC[:, :, TP:T], ALU.add, ALU.mult).then_inc(gl_ready, 1)
            turns(dve, in0, dve_in0, peel=1)

            def add_to_x(ph, it, j, p):
                x = X[:, bass.ds(2 * p, 2), :]
                V.tensor_tensor(x, two(group_bank(ph, j)), x, ALU.add).then_inc(evac_done, 1)

            for c in range(16):
                split_lo(dve, "D", out0a, 0, c)
                if c <= 10:
                    for w in range(3 * c, min(3 * c + 3, W31)):
                        tap(3, w)
                if c == 10:
                    dve.wait_ge(tap_done, 4 * 62)
                    sample_conv(3)
                if c == 11:
                    dve.wait_ge(mu_ready, 1)
                    V.tensor_scalar(G[:, 0, :], PS[:, 6, 0:T], 1.0 / DR, None, ALU.mult).then_inc(mu_copied, 1)
                    dve.wait_ge(mu_copied, 1)
                    dve.wait_ge(yc_ready, 4)
                    dve.wait_ge(ln_added, 4)
                    for q in range(4):
                        y = YC[:, 2 * q:2 * q + 2, :]
                        V.tensor_tensor(y, y, over2(G[:, 0, :]), ALU.subtract).then_inc(yd_ready, 1)
                if c == 14:
                    dve.wait_ge(dev_ready, 1)
                    V.reciprocal(G[:, 1, :], G[:, 1, :]).then_inc(rv_ready, 1)
                    dve.wait_ge(rv_ready, 1)
                    dve.wait_ge(yd_ready, 4)
                    dve.wait_ge(lsq_ready, 4)
                    for q in range(4):
                        y = YC[:, 2 * q:2 * q + 2, :]
                        V.tensor_tensor(y, y, over2(G[:, 1, :]), ALU.mult).then_inc(yn_ready, 1)
                if c == 15:
                    for q in range(4):
                        dve.wait_ge(yn_ready, q + 1)
                        for m in range(2):
                            j = 2 * q + m
                            zz = V.tensor_scalar(Zb[q][:, m, :], YC[:, j, :], par[:, LNG + j:LNG + j + 1],
                                                 par[:, LNB + j:LNB + j + 1], ALU.mult, ALU.add)
                        zz.then_inc(z_step, 1)
                if c == 15:
                    for q in range(4):
                        dve.wait_ge(z_step, q + 1)
                        dve.wait_ge(lth_ready, q + 1)
                        V.scalar_tensor_tensor(Zb[q][:, :, :], Tb[q][:, :, :], 1.0, Zb[q][:, :, :], ALU.add, ALU.mult).then_inc(z_ready, 1)
                    for q in range(4):
                        k = slice(8 + 2 * q, 10 + 2 * q)
                        dve.wait_ge(bh_ready, 5 + q)
                        V.scalar_tensor_tensor(B_lo[:, k, :], Zb[q][:, :, :], 0.5, B_hi[:, k, :].bitcast(F32),
                                               ALU.mult, ALU.subtract).then_inc(b_ready, 1)
                if c % 2 == 1:
                    dve.wait_ge(pe_block, out0a.n(0, c + 1))
                    add_to_x(out0a, 0, c // 2, c // 2)
            for c in range(16):
                split_lo(dve, "D", out0b, 0, c)
                if c % 2 == 1:
                    p = c // 2
                    dve.wait_ge(pe_block, out0b.n(0, c + 1))
                    add_to_x(out0b, 0, p, p)
                    if p:
                        gain_lo(dve, 1, p - 1, MPN)
            gain_lo(dve, 1, 7, MPN)

            def dve_mlp(l):
                for h in (0, 1):
                    up, down = PH[f"up{l}{h}"], PH[f"down{l}{h}"]
                    k = 2 * l + h
                    def dve_up(it):
                        for c in range(8):
                            split_lo(dve, "D", up, it, c)
                            if c % 4 == 3:
                                p = 2 * it + c // 4
                                if isinstance(it, int) and it == 0 and c == 3 and h == 0:
                                    invert(dve, 1 + 2 * l)
                                dve.wait_ge(pe_block, up.n(it, c + 1))
                                V.tensor_tensor(UT[:, :, :], two(group_bank(up, c // 4)), over2(RS[:, :]), ALU.mult).then_inc(evac_done, 1)
                                dve.wait_ge(evac_done, up.g(it, c // 4) + 1)
                                V.scalar_tensor_tensor(U[:, :, :], UT[:, :, :], 0.0, UT[:, :, :], ALU.max, ALU.mult).then_inc(u_ready, 1)
                                dve.wait_ge(hh_ready, p + (16 * k + 1))
                                q = bass.ds(2 * p, 2)
                                V.tensor_tensor(H_lo[:, q, :], U[:, :, :], H_hi[:, q, :].bitcast(F32), ALU.subtract).then_inc(h_ready, 1)
                    def dve_down(it):
                        for c in range(16):
                            split_lo(dve, "D", down, it, c)
                            if c % 8 == 7:
                                p = 2 * it + c // 8
                                dve.wait_ge(pe_block, down.n(it, c + 1))
                                add_to_x(down, it, c // 8, p)
                                if h == 1 and l < DEPTH - 1:
                                    gain_lo(dve, 2 + 2 * l, p, MLN)
                    turns(dve, up, dve_up, peel=1 - h)
                    turns(dve, down, dve_down, tail=1 if down is LAST else 0)
            dve_mlp(0)
            dve_mixer1(dve, link, log1p_terms)
            dve_mlp(1)
            dve.wait_ge(rt_ready, 1)
            V.reciprocal(rt[:, 0:2], rt[:, 0:2])
            V.reciprocal(rt[0:NS, 2:3], rt[0:NS, 2:3]).then_inc(rt_inv, 1)
            dve.wait_ge(rt_inv, 1)
            dve.wait_ge(fin_copied, 8)
            for q in range(4):
                y = YO[:, 1, 512 * q:512 * q + 512]
                V.tensor_scalar(y, y, rt[:, 1:2], None, ALU.mult).then_inc(yd_scaled, 1)
            V.tensor_scalar(YS[:, :], YS[:, :], rt[0:NS, 2:3], None, ALU.mult).then_inc(yd_scaled, 1)


def flat(ap, rows):
    n = len(ap.shape)
    if n == 1:
        ap = ap.rearrange("(r f) -> r f", f=P)
    elif n == 2:
        ap = ap.rearrange("a (r f) -> (a r) f", f=P)
    else:
        ap = ap.rearrange("a b (r f) -> (a b r) f", f=P)
    assert ap.shape[0] == rows
    return ap


INS = ["x_prompt", "x_sample", "state_rglru_conv", "state_rglru_h", "state_conf_conv", "state_mlstm_C",
       "state_mlstm_n", "state_mlstm_m", "ab_norm", "ab_w_in", "rglru_conv_w", "rglru_conv_b", "rglru_wa",
       "rglru_ba", "rglru_wx", "rglru_bx", "rglru_lambda", "conf_dw_w", "conf_dw_b", "conf_ln_g", "conf_ln_b",
       "ab_w_out", "ml_norm", "ml_w_in", "ml_b_if", "ml_hnorm_g", "ml_w_out", "mlp_norm", "mlp_w_up",
       "mlp_w_down", "final_norm"]
OUTPUTS = [("y_prompt", (1, TP, D)), ("y_sample", (NS, 1, D)),
           ("p_rconv", (1, 1, W4 - 1, DR)), ("p_rh", (1, 1, DR)), ("p_cconv", (1, 1, W31 - 1, DR)),
           ("p_C", (1, 1, NH, DK, DV)), ("p_n", (1, 1, NH, DK)), ("p_m", (1, 1, NH)),
           ("s_rconv", (1, NS, W4 - 1, DR)), ("s_rh", (1, NS, DR)), ("s_cconv", (1, NS, W31 - 1, DR)),
           ("s_C", (1, NS, NH, DK, DV)), ("s_n", (1, NS, NH, DK)), ("s_m", (1, NS, NH))]


def kernel(**inputs):
    import numpy as np
    import concourse.bacc as bacc
    from concourse.bass_utils import run_bass_kernel_spmd

    nc = bacc.Bacc("TRN2", target_bir_lowering=False, num_devices=1)
    arrays, ins, outs = {}, {}, {}
    for name in INS:
        a = np.ascontiguousarray(inputs[name])
        arrays[f"in_{name}"] = a
        ins[name] = nc.dram_tensor(f"in_{name}", a.shape, mybir.dt.from_np(a.dtype), kind="ExternalInput").ap()
    for name, shape in OUTPUTS:
        outs[name] = nc.dram_tensor(f"out_{name}", shape, F32, kind="ExternalOutput").ap()
    program(nc, ins, outs)
    r = run_bass_kernel_spmd(nc, [arrays], core_ids=[0])
    return tuple(r.results[0][f"out_{name}"] for name, _ in OUTPUTS)
```
